# Optimizing a Trainium2 kernel written in Bass

```python
import math
import jax, jax.numpy as jnp
from jax import lax
import numpy as np

D_MODEL = 1024
BATCH = 1
SEQ = 1024
DEPTH = 1

HEAD_DIM = 64
POOL_WINDOWS = (2, 4, 8, 16)
POOL_GROUP = 64
POOL_WIDTH = POOL_GROUP * len(POOL_WINDOWS)
ATTN_CONFIGS = ((128, 1), (512, 4), (2048, 16))
HEADS_PER_GROUP = 4
N_ATTN_HEADS = HEADS_PER_GROUP * len(ATTN_CONFIGS)
ATTN_WIDTH = N_ATTN_HEADS * HEAD_DIM
MIX_WIDTH = POOL_WIDTH + ATTN_WIDTH
IN_PROJ_WIDTH = POOL_WIDTH + 3 * ATTN_WIDTH
ATTN_BLOCK = 64
PEER_HEADS = 8
PEER_N_KEYS = 128
PEER_N_EXPERTS = PEER_N_KEYS * PEER_N_KEYS
PEER_HALF = 128
PEER_QUERY_DIM = 2 * PEER_HALF
PEER_TOPK = 16
PEER_CHUNK = 128
RMS_EPS = 1e-6
NEG_INF = -1e30

kernel_name = "hybrid_pool_dilated_alibi_peer_block"

def rms_norm(x, g):
    xf = x.astype(jnp.float32)
    y = xf * lax.rsqrt(jnp.mean(xf * xf, axis=-1, keepdims=True) + RMS_EPS)
    return (y * g.astype(jnp.float32)).astype(x.dtype)

def alibi_slopes():
    return jnp.asarray(2.0 ** (-8.0 * np.arange(1, N_ATTN_HEADS + 1) / N_ATTN_HEADS), dtype=jnp.float32)

def multiscale_pool(p, w_pool, pool_scale):
    B, S, C = p.shape
    pf = p.astype(jnp.float32)
    csum = jnp.concatenate([jnp.zeros((B, 1, C), jnp.float32), jnp.cumsum(pf, axis=1)], axis=1)
    pos = jnp.arange(S)
    outs = []
    for gi, w in enumerate(POOL_WINDOWS):
        sl = slice(gi * POOL_GROUP, (gi + 1) * POOL_GROUP)
        lo = jnp.clip(pos - w // 2, 0, S)
        hi = jnp.clip(pos + w // 2, 0, S)
        cg = csum[..., sl]
        mean = (cg[:, hi] - cg[:, lo]) / (hi - lo).astype(jnp.float32)[None, :, None]
        outs.append(mean - pf[..., sl])
    pooled = jnp.stack(outs, axis=2)
    mixed = jnp.einsum('bsgc,gcd->bsgd', pooled, w_pool.astype(jnp.float32))
    return (mixed.reshape(B, S, C) * pool_scale.astype(jnp.float32)).astype(p.dtype)

def dilated_window_attention(q, k, v, window, dilation, slopes):
    B, S, H, Dh = q.shape
    L = S // dilation
    half = window // (2 * dilation)
    nb = -(-L // ATTN_BLOCK)
    Lp = nb * ATTN_BLOCK

    def to_sub(t):
        return t.reshape(B, L, dilation, H, Dh).transpose(0, 2, 1, 3, 4)

    qs = jnp.pad(to_sub(q), ((0, 0), (0, 0), (0, Lp - L), (0, 0), (0, 0)))
    qb = qs.reshape(B, dilation, nb, ATTN_BLOCK, H, Dh)

    def key_blocks(t):
        ts = jnp.pad(to_sub(t), ((0, 0), (0, 0), (ATTN_BLOCK, Lp - L + ATTN_BLOCK), (0, 0), (0, 0)))
        ts = ts.reshape(B, dilation, nb + 2, ATTN_BLOCK, H, Dh)
        return jnp.concatenate([ts[:, :, :-2], ts[:, :, 1:-1], ts[:, :, 2:]], axis=3)

    kb = key_blocks(k)
    vb = key_blocks(v)

    scale = 1.0 / math.sqrt(Dh)
    scores = jnp.einsum('brnqhc,brnkhc->brnhqk', qb.astype(jnp.float32), kb.astype(jnp.float32)) * scale
    qi = jnp.arange(nb)[:, None] * ATTN_BLOCK + jnp.arange(ATTN_BLOCK)[None, :]
    kj = jnp.arange(nb)[:, None] * ATTN_BLOCK - ATTN_BLOCK + jnp.arange(3 * ATTN_BLOCK)[None, :]
    rel = kj[:, None, :] - qi[:, :, None]
    valid = (jnp.abs(rel) <= half) & (kj[:, None, :] >= 0) & (kj[:, None, :] < L)
    dist = (dilation * jnp.abs(rel)).astype(jnp.float32)
    bias = -slopes[None, :, None, None] * dist[:, None]
    scores = jnp.where(valid[:, None], scores + bias, NEG_INF)
    m = jnp.max(scores, axis=-1, keepdims=True)
    pexp = jnp.exp(scores - m)
    den = jnp.sum(pexp, axis=-1, keepdims=True)
    lse = (m + jnp.log(den))[..., 0]
    o = jnp.einsum('brnhqk,brnkhc->brnqhc', (pexp / den).astype(v.dtype), vb)
    o = o.reshape(B, dilation, Lp, H, Dh)[:, :, :L].transpose(0, 2, 1, 3, 4).reshape(B, S, H, Dh)
    lse = lse.transpose(0, 1, 2, 4, 3).reshape(B, dilation, Lp, H)[:, :, :L]
    lse = lse.transpose(0, 2, 1, 3).reshape(B, S, H)
    return o, lse

def peer_ffn(h, w_q, subkeys, u, v):
    B, S, D = h.shape
    n_chunks = (B * S) // PEER_CHUNK
    hc = h.reshape(n_chunks, PEER_CHUNK, D)

    def chunk(ht):
        q = (ht @ w_q).reshape(PEER_CHUNK, PEER_HEADS, 2, PEER_HALF)
        s = jnp.einsum('thpc,hpnc->thpn', q.astype(jnp.float32), subkeys.astype(jnp.float32))
        sv, si = lax.top_k(s, PEER_TOPK)
        cand_s = sv[:, :, 0, :, None] + sv[:, :, 1, None, :]
        cand_i = si[:, :, 0, :, None] * PEER_N_KEYS + si[:, :, 1, None, :]
        cand_s = cand_s.reshape(PEER_CHUNK, PEER_HEADS, PEER_TOPK * PEER_TOPK)
        cand_i = cand_i.reshape(PEER_CHUNK, PEER_HEADS, PEER_TOPK * PEER_TOPK)
        top_s, top_pos = lax.top_k(cand_s, PEER_TOPK)
        expert = jnp.take_along_axis(cand_i, top_pos, axis=-1)
        gate = jax.nn.softmax(top_s, axis=-1)
        ue = u[expert]
        ve = v[expert]
        act = jax.nn.gelu(jnp.einsum('thkd,td->thk', ue, ht).astype(jnp.float32), approximate=False)
        return jnp.einsum('thk,thkd->td', (gate * act).astype(ht.dtype), ve)

    return lax.map(chunk, hc).reshape(B, S, D)

def setup_inputs(seed: int = 0) -> dict:
    key = jax.random.key(seed)
    ks = jax.random.split(key, 12)
    f32 = jnp.float32
    x = jax.random.normal(ks[0], (BATCH, SEQ, D_MODEL), f32)
    g_mix = 1.0 + 0.02 * jax.random.normal(ks[1], (DEPTH, D_MODEL), f32)
    w_in = jax.random.normal(ks[2], (DEPTH, D_MODEL, IN_PROJ_WIDTH), f32) * D_MODEL ** -0.5
    w_pool = jax.random.normal(ks[3], (DEPTH, len(POOL_WINDOWS), POOL_GROUP, POOL_GROUP), f32) * POOL_GROUP ** -0.5
    pool_scale = 1.0 + 0.02 * jax.random.normal(ks[4], (DEPTH, POOL_WIDTH), f32)
    w_out = jax.random.normal(ks[5], (DEPTH, MIX_WIDTH, D_MODEL), f32) * MIX_WIDTH ** -0.5
    g_ffn = 1.0 + 0.02 * jax.random.normal(ks[6], (DEPTH, D_MODEL), f32)
    w_peer_q = jax.random.normal(ks[7], (DEPTH, D_MODEL, PEER_HEADS * PEER_QUERY_DIM), f32) * D_MODEL ** -0.5
    peer_subkeys = jax.random.normal(ks[8], (DEPTH, PEER_HEADS, 2, PEER_N_KEYS, PEER_HALF), f32) * PEER_HALF ** -0.5
    peer_u = jax.random.normal(ks[9], (DEPTH, PEER_N_EXPERTS, D_MODEL), f32) * D_MODEL ** -0.5
    peer_v = jax.random.normal(ks[10], (DEPTH, PEER_N_EXPERTS, D_MODEL), f32) * PEER_HEADS ** -0.5
    g_final = 1.0 + 0.02 * jax.random.normal(ks[11], (D_MODEL,), f32)
    return {"x": x, "g_mix": g_mix, "w_in": w_in, "w_pool": w_pool, "pool_scale": pool_scale,
            "w_out": w_out, "g_ffn": g_ffn, "w_peer_q": w_peer_q, "peer_subkeys": peer_subkeys,
            "peer_u": peer_u, "peer_v": peer_v, "g_final": g_final}

def reference(x, g_mix, w_in, w_pool, pool_scale, w_out, g_ffn, w_peer_q, peer_subkeys,
              peer_u, peer_v, g_final):
    B, S, D = x.shape
    slopes = alibi_slopes()
    for layer in range(DEPTH):
        h = rms_norm(x, g_mix[layer])
        proj = h @ w_in[layer]
        p = proj[..., :POOL_WIDTH]
        q = proj[..., POOL_WIDTH:POOL_WIDTH + ATTN_WIDTH].reshape(B, S, N_ATTN_HEADS, HEAD_DIM)
        k = proj[..., POOL_WIDTH + ATTN_WIDTH:POOL_WIDTH + 2 * ATTN_WIDTH].reshape(B, S, N_ATTN_HEADS, HEAD_DIM)
        v = proj[..., POOL_WIDTH + 2 * ATTN_WIDTH:].reshape(B, S, N_ATTN_HEADS, HEAD_DIM)

        pool_out = multiscale_pool(p, w_pool[layer], pool_scale[layer])

        outs, lses = [], []
        for gi, (window, dilation) in enumerate(ATTN_CONFIGS):
            hs = slice(gi * HEADS_PER_GROUP, (gi + 1) * HEADS_PER_GROUP)
            o, lse = dilated_window_attention(q[:, :, hs], k[:, :, hs], v[:, :, hs],
                                              window, dilation, slopes[hs])
            outs.append(o)
            lses.append(lse)
        alpha = jax.nn.softmax(jnp.stack(lses, axis=2), axis=2)
        attn = (jnp.stack(outs, axis=2).astype(jnp.float32) * alpha[..., None]).astype(x.dtype)
        attn = attn.reshape(B, S, ATTN_WIDTH)

        mixed = jnp.concatenate([pool_out, attn], axis=-1) @ w_out[layer]
        x = x + mixed

        x = x + peer_ffn(rms_norm(x, g_ffn[layer]), w_peer_q[layer], peer_subkeys[layer],
                         peer_u[layer], peer_v[layer])
    return rms_norm(x, g_final)


_drawn_inputs = setup_inputs


def setup_inputs(seed=0):
    import zlib

    import numpy as np

    out = dict(_drawn_inputs(seed))
    spreads = {}
    factors = {'g_mix': 3.025, 'pool_scale': 9.841, 'g_final': 7.991, 'g_ffn': 8.0}
    for name, (base, spread) in spreads.items():
        noise = np.random.default_rng([zlib.crc32(name.encode()), seed]).standard_normal(out[name].shape)
        drawn = base * np.exp(spread * noise) if base else spread * noise
        out[name] = __import__('jax').numpy.asarray(drawn.astype(out[name].dtype))
    for name, factor in factors.items():
        out[name] = (out[name] * factor).astype(out[name].dtype)
    return out
```

```python
import concourse.bass as bass
from concourse import mybir
from contextlib import ExitStack

F32 = mybir.dt.float32
F32R = mybir.dt.float32r
U32 = mybir.dt.uint32
ALU = mybir.AluOpType
ACT = mybir.ActivationFunctionType
AX = mybir.AxisListType

P = 128
D = 1024
S = 1024
KC = D // P
NT = S // P
HALF = 512
DH = 64
GROUPS = 3
DIL = (1, 4, 16)
NRES = DIL
SPAN = 64
EPS = 1e-6
PH = 8
TOP = 16
NK = 128
FAR = 3.0e38

IN_PIECES = 2 + 6 * GROUPS
OUT_PIECES = KC
Q_PIECES = 2 * PH
W_OUT0 = IN_PIECES
W_Q0 = W_OUT0 + OUT_PIECES
W_U0 = W_Q0 + Q_PIECES

TW = 32
A_BODIES = 32
EXP_BODY = 20
B_BODIES = NK // 2 - A_BODIES
assert B_BODIES * TW == S
VJ = 4
UNITS = 16


def v_tiles(g):
    if g == 2:
        return [(r * SPAN, SPAN) for r in range(NRES[2])]
    length = S // NRES[g]
    out = []
    for r in range(NRES[g]):
        for x in range(length // P + 1):
            lo, hi = max(x * P - SPAN, 0), min(x * P + SPAN, length)
            out.append((r * length + lo, hi - lo))
    return out


def window(g, b):
    if g == 2:
        return b * P, 0, P, [(b, P)]
    per = S // NRES[g] // P
    r, x = b // per, b % per
    lo = SPAN if x == 0 else 0
    hi = 2 * P - SPAN if x == per - 1 else 2 * P
    return b * P - SPAN + lo, lo, hi - lo, [(r * (per + 1) + x, P - lo), (r * (per + 1) + x + 1, hi - P)]


def by_residue(ap, g, r0, nr, l0, nl):
    n = NRES[g]
    return ap.rearrange("p (l r) -> p r l", r=n)[:, r0:r0 + nr, l0:l0 + nl]


def build(nc, x, g_mix, w_in, w_pool, pool_scale, w_out, g_ffn, w_q, subkeys, u, v, g_final,
          ident_c, iota_c, bias01_c, bias2_c, sel_c, edge_c, inv_c, out):
    ctx = ExitStack()
    with ctx:
        base = (nc.sbuf_base + 63) // 64 * 64

        def at(name, kb, shape, dt=F32):
            return nc.alloc_sbuf_tensor_at(name, shape, dt, offset=base + int(kb * 1024))

        def sem(name):
            return ctx.enter_context(nc.semaphore(name))

        h_hi = at("h_hi", 0, [P, KC, S], F32R)
        h_lo = at("h_lo", 32, [P, KC, S], F32R)
        xs = at("xs", 64, [P, NT, D])
        ot = at("ot", 64, [P, 2 * GROUPS, S])
        pmix = at("pmix", 88, [P, 2, S])
        w_raw = at("w_raw", 96, [P, 2, 1024])
        w_hi = at("w_hi", 104, [P, 2, 1024], F32R)
        w_lo = at("w_lo", 112, [P, 2, 1024], F32R)
        gain = at("gain", 120, [P, D])
        ident = at("ident", 124, [P, P])
        iota = at("iota", 124.5, [P, P])
        stat_nm = at("stat_nm", 125, [P, GROUPS, NT, 4])
        stat_den = at("stat_den", 125.375, [P, GROUPS, NT, 4])
        ss = at("ss", 125.75, [P, 3, NT])
        std = at("std", 125.875, [P, 3, NT])
        rstd = at("rstd", 126, [P, 3, NT])
        sel = at("sel", 126.125, [4, 2, P])
        wpool = at("wpool", 127.125, [P, 2, DH])
        pscale = at("pscale", 127.625, [P, 2])
        edge = at("edge", 127.6875, [P, 2, 16])
        inv = at("inv", 127.8125, [P, 2])
        xn = at("xn", 128, [P, 2, D])
        bias01 = at("bias01", 128, [P, 8, 2 * P])
        bias2 = at("bias2", 136, [P, 4, P])
        qt = [at(f"qt{s}", 138 + 28 * s, [P, 2, S]) for s in range(2)]
        kt = [at(f"kt{s}", 146 + 28 * s, [P, 2, S]) for s in range(2)]
        vt = [at(f"vt{s}", 154 + 28 * s, [P, 12, 4 * DH]) for s in range(2)]
        sc = at("sc", 194, [P, 2, 2, 2 * P])
        pr = at("pr", 198, [P, 2, 2, 2 * P])
        pt = at("pt", 202, [P, 2, 4, P])
        PADW = S + 16
        pp = at("pp", 166, [P, 2, PADW])
        pa = at("pa", 174.125, [P, 2, PADW])
        pb_ = at("pb_", 182.25, [P, PADW])
        lt = at("lt", 138, [4, 2, GROUPS, S])
        mn = at("mn", 162, [4, S])
        den = at("den", 166, [4, S])
        wo_hi = at("wo_hi", 138, [P, KC, D], F32R)
        wo_lo = at("wo_lo", 170, [P, KC, D], F32R)
        sk = at("sk", 138, [P, 2 * PH, NK])
        q2 = at("q2", 146, [P, 2, S])
        top1 = at("top1", 154, [P, NT, PH, 2, TOP])
        ix1 = at("ix1", 162, [P, NT, PH, 2, TOP], U32)
        ix1f = at("ix1f", 170, [P, NT, PH, 2, TOP])
        cand = at("cand", 178, [P, PH, TOP * TOP])
        eq = at("eq", 186, [P, PH, TOP, TOP])
        rep = at("rep", 194, [P, 8, 2 * P])
        pos = at("pos", 202, [P, 2, PH, TOP], U32)
        posf = at("posf", 203, [P, 2, PH, TOP])
        top2 = at("top2", 204, [P, PH, TOP])
        gsum = at("gsum", 204.5, [P, 2, NT, PH])
        act_st = at("act_st", 64, [P, 2, S])
        route = at("route", 72, [P, 3, NT, P])
        oneh = at("oneh", 84, [P, 2, 2, 4, P])
        strip_r = at("strip_r", 92, [P, 2, 3, TW])
        g_st = at("g_st", 138, [P, 2, NK, TW])
        route_t = at("route_t", 170, [P, 3, S])
        v_raw = at("v_raw", 0, [P, 2, VJ, D])
        a_raw = at("a_raw", 32, [P, 2, VJ, HALF])
        g_raw = at("g_raw", 48, [P, 2, HALF // TW, VJ * TW])
        v_hi = at("v_hi", 64, [P, VJ, D], F32R)
        v_lo = at("v_lo", 80, [P, VJ, D], F32R)
        a_hi = at("a_hi", 96, [P, VJ, HALF], F32R)
        a_lo = at("a_lo", 104, [P, VJ, HALF], F32R)
        prod = at("prod", 112, [P, 2, HALF])
        zero = at("zero", 116, [P, HALF], F32R)
        y = at("y", 138, [P, NT, D])
        yo = at("yo", 170, [P, 2, D])

        bank = [ctx.enter_context(nc.psum_tensor(f"bank{k}", [P, HALF], F32)) for k in range(8)]

        act_d = nc.dram_tensor("act_d", [NK, P, S], F32).ap()
        g_d = nc.dram_tensor("g_d", [B_BODIES, P, NK, TW], F32).ap()
        x1_d = nc.dram_tensor("x1_d", [NT, P, D], F32).ap()

        cst_in = sem("cst_in")
        bias_in = sem("bias_in")
        gain_in = sem("gain_in")
        x_in = [sem(f"x_in{i}") for i in range(NT)]
        sk_in = sem("sk_in")
        raw_in = [sem("raw_in0"), sem("raw_in1")]
        hi_done = sem("hi_done")
        lo_done = sem("lo_done")
        ss_done = sem("ss_done")
        std_done = sem("std_done")
        rs_done = sem("rs_done")
        xn_done = sem("xn_done")
        xt_done = sem("xt_done")
        hh_done = sem("hh_done")
        hl_done = sem("hl_done")
        pj_done = sem("pj_done")
        pj_free = sem("pj_free")
        pool_pad = sem("pool_pad")
        pool_st = sem("pool_st")
        pool_mm = sem("pool_mm")
        pool_ev = sem("pool_ev")
        qk_done = sem("qk_done")
        s_done = sem("s_done")
        p_done = sem("p_done")
        pt_done = sem("pt_done")
        pt_ev = sem("pt_ev")
        pv_done = sem("pv_done")
        ot_ev = sem("ot_ev")
        st_done = sem("st_done")
        st_ev = sem("st_ev")
        al_st = sem("al_st")
        al_e = sem("al_e")
        bc_done = sem("bc_done")
        bc_mul = sem("bc_mul")
        mx_hi = sem("mx_hi")
        mx_lo = sem("mx_lo")
        op_done = sem("op_done")
        x1_done = sem("x1_done")
        x1_out = sem("x1_out")
        sc_done = sem("sc_done")
        sc_free = sem("sc_free")
        r_st = sem("r_st")
        g_e = sem("g_e")
        g_ask = sem("g_ask")
        route_done = sem("route_done")
        m1_done = sem("m1_done")
        act_done = sem("act_done")
        act_out = [sem("act_out0"), sem("act_out1")]
        rt_done = sem("rt_done")
        rt_ev = sem("rt_ev")
        oh_cp = sem("oh_cp")
        oh_done = sem("oh_done")
        gp_done = sem("gp_done")
        gs_done = sem("gs_done")
        g_out = [sem("g_out0"), sem("g_out1")]
        v_in = [sem("v_in0"), sem("v_in1")]
        a_in = [sem("a_in0"), sem("a_in1")]
        g_in = [sem("g_in0"), sem("g_in1")]
        y_in = sem("y_in")
        z_set = sem("z_set")
        vh_done = sem("vh_done")
        vl_done = sem("vl_done")
        pd_done = sem("pd_done")
        ah_done = sem("ah_done")
        al_done = sem("al_done")
        m2_done = sem("m2_done")
        y_done = sem("y_done")
        yo_done = sem("yo_done")
        y_out = [sem("y_out0"), sem("y_out1")]

        block = ctx.enter_context(nc.Block())
        win_d, wout_d, wq_d, u_d = w_in, w_out, w_q, u
        out_t = out.rearrange("a (t p) d -> (a t) p d", p=P)
        x_t = x.rearrange("a (t p) d -> (a t) p d", p=P)

        def bcast_row(row):
            return bass.AP(tensor=row.tensor, offset=row.offset, ap=[[0, P]] + [list(a) for a in row.ap[-1:]])

        PIECE_BANKS = [2, 4]
        for g in range(GROUPS):
            for _ in range(4):
                PIECE_BANKS.append(PIECE_BANKS[-1] + 2)
            PIECE_BANKS += [PIECE_BANKS[-1] + len(v_tiles(g))] * 2
        PJ_G = [PIECE_BANKS[2 + 6 * g + 5] for g in range(GROUPS)]
        PJ_IN = PIECE_BANKS[-1]
        for _ in range(Q_PIECES):
            PIECE_BANKS.append(PIECE_BANKS[-1] + 2)
        PJ_ALL = PIECE_BANKS[-1]
        LO_BANKS = 2 * NT

        @block.sync
        def _(sp):
            sp.dma_start(gain[:, :], bcast_row(g_mix)).then_inc(gain_in, 16)
            for i in range(NT):
                sp.dma_start(xs[:, i, :], x_t[i]).then_inc(x_in[i], 16)
                if i == 1:
                    consts = ((ident[:, :], ident_c), (iota[:, :], iota_c), (sel[:, :, :], sel_c),
                              (wpool[:, :, :], w_pool), (pscale[:, :], pool_scale), (edge[:, :, :], edge_c),
                              (inv[:, :], inv_c))
                    for dst, src in consts:
                        sp.dma_start(dst, src).then_inc(cst_in, 16)

            def load_piece(n, src):
                if n >= 2:
                    sp.wait_ge(lo_done, n - 1)
                sp.dma_start(w_raw[:, n % 2, :], src).then_inc(raw_in[n % 2], 16)

            for n in range(IN_PIECES):
                load_piece(n, win_d[n])
                if n == 2:
                    sp.wait_ge(xt_done, LO_BANKS)
                    sp.dma_start(bias01[:, :, :], bias01_c).then_inc(bias_in, 16)
                    sp.dma_start(bias2[:, :, :], bias2_c).then_inc(bias_in, 16)
                    sp.dma_start(gain[:, :], bcast_row(g_ffn)).then_inc(gain_in, 16)
            for n in range(OUT_PIECES):
                load_piece(W_OUT0 + n, wout_d[n])
            sp.wait_ge(mx_lo, 2 * GROUPS * 2 + 4)
            for i in range(NT):
                sp.dma_start(xs[:, i, :], x_t[i]).then_inc(x_in[i], 16)
                if i < 2:
                    load_piece(W_Q0 + i, wq_d[i])
            for i in range(NT):
                sp.wait_ge(x1_done, 2 * i + 2)
                sp.dma_start(x1_d[i], xs[:, i, :]).then_inc(x1_out, 16)
            sp.wait_ge(op_done, 2 * NT)
            sp.dma_start(sk[:, :, :], subkeys).then_inc(sk_in, 16)
            sp.wait_ge(xn_done, 2 * NT)
            sp.dma_start(gain[:, :], bcast_row(g_final)).then_inc(gain_in, 16)
            for n in range(2, Q_PIECES):
                load_piece(W_Q0 + n, wq_d[n])
            load_piece(W_U0, u_d[0])
            load_piece(W_U0 + 1, u_d[1])

            def first_half(it, strips, last):
                for s in range(2):
                    if not last:
                        sp.wait_ge(lo_done, it * 2 + (W_U0 + s + 1))
                        sp.dma_start(w_raw[:, s, :], u_d[it * 2 + (2 + s)]).then_inc(raw_in[s], 16)
                    sp.wait_ge(act_done, it * 4 + (2 * s + 2))
                    sp.dma_start(act_d[it * 2 + s], act_st[:, s, :]).then_inc(act_out[s], 16)

            with sp.Fori(0, A_BODIES) as it:
                first_half(it, False, False)

            def second_part(it, s2, last):
                first_half(it * 2 + (A_BODIES + s2), True, last)
                sp.wait_ge(gs_done, it * 16 + (8 * s2 + 8))
                sp.dma_start(g_d[it * 2 + s2], g_st[:, s2, :, :]).then_inc(g_out[s2], 16)

            with sp.Fori(0, B_BODIES // 2 - 1) as it:
                for s2 in range(2):
                    second_part(it, s2, False)
            second_part(B_BODIES // 2 - 1, 0, False)
            second_part(B_BODIES // 2 - 1, 1, True)

            for s in range(2):
                sp.wait_ge(act_out[s], 16 * NK // 2)
                sp.wait_ge(g_out[s], 16 * B_BODIES // 2)
            sp.wait_ge(m1_done, 2 * NK)
            sp.wait_ge(x1_out, 16 * NT)

            def loads(hf, it, s):
                sp.dma_start(v_raw[:, s, :, :], v[it * 2 + s]).then_inc(v_in[s], 16)
                sp.dma_start(a_raw[:, s, :, :],
                             act_d[bass.ds(it * (2 * VJ) + VJ * s, VJ), :, hf * HALF:(hf + 1) * HALF]
                             .rearrange("j p t -> p j t")).then_inc(a_in[s], 16)
                sp.dma_start(g_raw[:, s, :, :],
                             g_d[hf * (B_BODIES // 2):(hf + 1) * (B_BODIES // 2), :,
                                 bass.ds(it * (2 * VJ) + VJ * s, VJ), :]
                             .rearrange("b p j t -> p b (j t)")).then_inc(g_in[s], 16)

            def free_raw(hf, it, s):
                sp.wait_ge(vl_done, it * (2 * VJ) + (hf * NK + VJ * s - VJ))
                sp.wait_ge(pd_done, it * (2 * VJ) + (hf * NK + VJ * s - VJ))

            NG2 = NK // VJ // 2
            for hf in range(2):
                for s in range(2):
                    if hf:
                        free_raw(hf, 0, s)
                    loads(hf, 0, s)
                if hf == 0:
                    sp.dma_start(y[:, :, :], x1_d.rearrange("t p d -> p t d")).then_inc(y_in, 16)
                with sp.Fori(1, NG2) as it:
                    for s in range(2):
                        free_raw(hf, it, s)
                        loads(hf, it, s)
            for i in range(NT):
                sp.wait_ge(yo_done, i + 1)
                sp.dma_start(out_t[i], yo[:, i % 2, :]).then_inc(y_out[i % 2], 16)
            for s in range(2):
                sp.wait_ge(y_out[s], 16 * NT // 2)

        @block.gpsimd
        def _(pool):
            def lower(n, dst, hi):
                pool.wait_ge(hi_done, n + 1)
                nc.gpsimd.tensor_tensor(dst, w_raw[:, n % 2, :], hi, ALU.subtract).then_inc(lo_done, 1)

            for n in range(IN_PIECES):
                lower(n, w_lo[:, n % 2, :], w_hi[:, n % 2, :])
            for n in range(OUT_PIECES):
                lower(W_OUT0 + n, wo_lo[:, n, :], wo_hi[:, n, :])
            for n in range(Q_PIECES):
                lower(W_Q0 + n, w_lo[:, n % 2, :], w_hi[:, n % 2, :])

            with pool.Fori(0, NK // 2) as it:
                for s in range(2):
                    pool.wait_ge(hi_done, it * 2 + (W_U0 + s + 1))
                    nc.gpsimd.tensor_tensor(w_lo[:, s, :], w_raw[:, s, :], w_hi[:, s, :],
                                            ALU.subtract).then_inc(lo_done, 1)

            for hf in range(2):
                with pool.Fori(0, NK // VJ // 2) as it:
                    for s in range(2):
                        for j in range(VJ):
                            pool.wait_ge(vh_done, it * (2 * VJ) + (hf * NK + VJ * s + j + 1))
                            nc.gpsimd.tensor_tensor(v_lo[:, j, :], v_raw[:, s, j, :], v_hi[:, j, :],
                                                    ALU.subtract).then_inc(vl_done, 1)

        @block.scalar
        def _(act):
            def upper(n, dst):
                act.wait_ge(raw_in[n % 2], 16 * (n // 2 + 1))
                nc.scalar.activation(dst, w_raw[:, n % 2, :], ACT.Copy).then_inc(hi_done, 1)

            def upper_slot(n, m):
                if m >= 2:
                    act.wait_ge(pj_done, PIECE_BANKS[m - 2])
                upper(n, w_hi[:, n % 2, :])

            def norm_stats(k, i):
                n = k * NT + i
                if n >= 2:
                    act.wait_ge(xt_done, 2 * (n - 1))
                nc.scalar.activation(xn[:, i % 2, :], xs[:, i, :], ACT.Square,
                                     accum_out=ss[:, k, i:i + 1]).then_inc(ss_done, 1)
                act.wait_ge(rs_done, 2 * n + 1)
                nc.scalar.activation(std[:, k, i:i + 1], rstd[:, k, i:i + 1], ACT.Sqrt).then_inc(std_done, 1)

            def norm_upper(k, i):
                for c in range(2):
                    n = k * LO_BANKS + 2 * i + c
                    act.wait_ge(xt_done, n + 1)
                    nc.scalar.activation(h_hi[:, 4 * c:4 * c + 4, i * P:(i + 1) * P],
                                         bank[(4 if k else 0) + (2 * i + c) % 4][:, :]
                                         .rearrange("p (k t) -> p k t", k=4), ACT.Copy).then_inc(hh_done, 1)

            for i in range(NT):
                act.wait_ge(x_in[i], 16)
                norm_stats(0, i)
                if i:
                    norm_upper(0, i - 1)
            upper_slot(0, 0)
            norm_upper(0, NT - 1)
            upper_slot(1, 1)

            pj = [0]

            def take(dst, src_of, scale=1.0):
                n = pj[0]
                act.wait_ge(pj_done, n + 1)
                nc.scalar.activation(dst, src_of(bank[n % 4]), ACT.Copy, scale=scale).then_inc(pj_free, 1)
                pj[0] = n + 1

            act.wait_ge(pool_pad, 1)
            for c in range(2):
                for hf in range(2):
                    take(pp[:, c, 8 + hf * HALF:8 + (hf + 1) * HALF], lambda b: b[:, :])
                upper_slot(2 + c, 2 + c)

            def exps(g, k):
                n = g * UNITS + k
                c, b = k // NT, k % NT
                _, lo, w, _ = window(g, b)
                for e in range(2):
                    if e == 0:
                        act.wait_ge(s_done, 2 * n + 2)
                        if n >= 2:
                            act.wait_ge(pt_done, n - 1)
                    ins = nc.scalar.activation(pr[:, n % 2, e, lo:lo + w], sc[:, n % 2, e, lo:lo + w], ACT.Exp,
                                               bias=stat_nm[:, g, b, 2 * c + e:2 * c + e + 1], scale=-1.0,
                                               accum_out=stat_den[:, g, b, 2 * c + e:2 * c + e + 1])
                ins.then_inc(p_done, 1)

            def projections(g):
                length, n_res = S // NRES[g], NRES[g]
                if g == 1:
                    act.wait_ge(pool_mm, 4)
                if g == 2:
                    act.wait_ge(pv_done, UNITS)
                for q in range(4):
                    n = 2 + 6 * g + q
                    dst = (qt if q < 2 else kt)[g % 2][:, q % 2, :].rearrange("p (r l) -> p r l", r=n_res)
                    for hf in range(2):
                        take(dst[:, :, hf * length // 2:(hf + 1) * length // 2],
                             lambda b: b[:, :].rearrange("p (l r) -> p r l", r=n_res),
                             -DH ** -0.5 if q < 2 else 1.0)
                        yield
                    upper_slot(n + 2, n + 2)
                for j, (_, rows) in enumerate(v_tiles(g)):
                    dst = vt[0][SPAN * (j % 2):SPAN * (j % 2) + rows, j // 2, :] if g == 2 else vt[g][0:rows, j, :]
                    take(dst, lambda b: b[0:rows, 0:4 * DH])
                    yield
                for n in (8 + 6 * g, 9 + 6 * g):
                    if n < IN_PIECES:
                        upper_slot(n, n)
                yield

            for _ in projections(0):
                pass
            for g in range(1, GROUPS):
                work = projections(g)
                for k in range(UNITS):
                    exps(g - 1, k)
                    for _ in range(2):
                        next(work, None)
                for _ in work:
                    pass
            for k in range(UNITS):
                exps(GROUPS - 1, k)

            act.wait_ge(pv_done, GROUPS * UNITS)
            act.wait_ge(pj_done, PJ_IN)
            for c in range(2):
                for hf in range(2):
                    act.wait_ge(pool_ev, 4)
                    cols = slice(hf * HALF, (hf + 1) * HALF)
                    nc.scalar.activation(h_hi[:, c, cols], pmix[:, c, cols], ACT.Copy).then_inc(mx_hi, 1)
            act.wait_ge(al_st, 3)
            nc.scalar.activation(lt[:, 0, :, :], lt[:, 0, :, :], ACT.Exp).then_inc(al_e, 1)
            for n in range(4 * GROUPS):
                act.wait_ge(bc_mul, n + 1)
                cols = slice(n % 2 * HALF, (n % 2 + 1) * HALF)
                nc.scalar.activation(h_hi[:, 2 + n // 2, cols], ot[:, n // 2, cols], ACT.Copy).then_inc(mx_hi, 1)
            act.wait_ge(bc_done, 4 * GROUPS)
            for n in range(OUT_PIECES):
                upper(W_OUT0 + n, wo_hi[:, n, :])
            upper_slot(W_Q0, IN_PIECES)
            upper_slot(W_Q0 + 1, IN_PIECES + 1)
            for i in range(NT):
                act.wait_ge(x1_done, 2 * i + 2)
                norm_stats(1, i)
                if i:
                    norm_upper(1, i - 1)
            norm_upper(1, NT - 1)

            def take_query(hp):
                if hp >= 2:
                    act.wait_ge(sc_done, 2 * (hp - 1))
                if hp == 0:
                    act.wait_ge(op_done, 2 * NT)
                for hf in range(2):
                    take(q2[:, hp % 2, hf * HALF:(hf + 1) * HALF], lambda b: b[:, :])

            for hp in range(Q_PIECES):
                take_query(hp)
                m = IN_PIECES + hp + 2
                upper_slot(W_Q0 + hp + 2, m)

            def chunk(it, s, first, ahead):
                if not first:
                    act.wait_ge(act_out[s], it * 16)
                for hf in range(2):
                    act.wait_ge(m1_done, it * 4 + (2 * s + hf + 1))
                    nc.scalar.activation(act_st[:, s, hf * HALF:(hf + 1) * HALF], bank[2 * s + hf][:, :],
                                         ACT.Gelu).then_inc(act_done, 1)
                if ahead:
                    act.wait_ge(raw_in[s], it * 16 + 16 * (W_U0 // 2 + 2))
                    nc.scalar.activation(w_hi[:, s, :], w_raw[:, s, :], ACT.Copy).then_inc(hi_done, 1)

            for s in range(2):
                chunk(0, s, True, True)
            with act.Fori(1, EXP_BODY) as it:
                for s in range(2):
                    chunk(it, s, False, True)
            act.wait_ge(g_ask, NT)
            nc.scalar.activation(route[:, 2, :, :], route[:, 2, :, :], ACT.Exp).then_inc(g_e, 1)
            with act.Fori(EXP_BODY, A_BODIES) as it:
                for s in range(2):
                    chunk(it, s, False, True)

            def strip(it, s2, first, ahead):
                if not first:
                    act.wait_ge(g_out[s2], it * 16)
                for s in range(2):
                    for q in range(4):
                        n = 4 * s + q
                        act.wait_ge(gp_done, it * 16 + (8 * s2 + n + 1))
                        nc.scalar.activation(g_st[:, s2, :, 4 * n:4 * n + 4],
                                             bank[4 + n % 2][:, :].rearrange("p (t j) -> p j t", t=4),
                                             ACT.Copy).then_inc(gs_done, 1)
                    chunk(it * 2 + (A_BODIES + s2), s, False, ahead)

            strip(0, 0, True, True)
            strip(0, 1, True, True)
            with act.Fori(1, B_BODIES // 2 - 1) as it:
                for s2 in range(2):
                    strip(it, s2, False, True)
            strip(B_BODIES // 2 - 1, 0, False, True)
            strip(B_BODIES // 2 - 1, 1, False, False)

            def upper_v(hf, it, s, j, first):
                n = hf * NK + VJ * s + j
                if j == 0:
                    act.wait_ge(v_in[s], it * 16 + (hf * 8 * (NK // VJ) + 16))
                if not first:
                    act.wait_ge(m2_done, it * (2 * VJ) + (n - VJ + 1))
                nc.scalar.activation(v_hi[:, j, :], v_raw[:, s, j, :], ACT.Copy).then_inc(vh_done, 1)
                act.wait_ge(pd_done, it * (2 * VJ) + (n + 1))
                nc.scalar.activation(a_hi[:, j, :], prod[:, j % 2, :], ACT.Copy).then_inc(ah_done, 1)

            for hf in range(2):
                for s in range(2):
                    for j in range(VJ):
                        upper_v(hf, 0, s, j, hf == 0 and s == 0)
                with act.Fori(1, NK // VJ // 2) as it:
                    for s in range(2):
                        for j in range(VJ):
                            upper_v(hf, it, s, j, False)
            for i in range(NT):
                act.wait_ge(y_done, 2 * (i + 1))
                if i >= 2:
                    act.wait_ge(y_out[i % 2], 16 * (i // 2))
                nc.scalar.activation(yo[:, i % 2, :], y[:, i, :], ACT.Square,
                                     accum_out=ss[:, 2, i:i + 1]).then_inc(ss_done, 1)
                act.wait_ge(rs_done, 2 * (2 * NT + i) + 1)
                nc.scalar.activation(std[:, 2, i:i + 1], rstd[:, 2, i:i + 1], ACT.Sqrt).then_inc(std_done, 1)

        @block.vector
        def _(dve):
            V = nc.vector

            def norm_scale(k, i, src, dst, done):
                n = k * NT + i
                dve.wait_ge(ss_done, n + 1)
                V.tensor_scalar(rstd[:, k, i:i + 1], ss[:, k, i:i + 1], 1.0 / D, EPS, ALU.mult,
                                ALU.add).then_inc(rs_done, 1)
                dve.wait_ge(std_done, n + 1)
                V.reciprocal(rstd[:, k, i:i + 1], std[:, k, i:i + 1]).then_inc(rs_done, 1)
                dve.wait_ge(rs_done, 2 * n + 2)
                V.scalar_tensor_tensor(out=dst, in0=src, scalar=rstd[:, k, i:i + 1], in1=gain[:, :],
                                       op0=ALU.mult, op1=ALU.mult).then_inc(done, 1)

            def norm_lower(k, i):
                for c in range(2):
                    n = k * LO_BANKS + 2 * i + c
                    dve.wait_ge(hh_done, n + 1)
                    cols = slice(i * P, (i + 1) * P)
                    V.tensor_tensor(h_lo[:, 4 * c:4 * c + 4, cols],
                                    bank[(4 if k else 0) + (2 * i + c) % 4][:, :].rearrange("p (k t) -> p k t", k=4),
                                    h_hi[:, 4 * c:4 * c + 4, cols], ALU.subtract).then_inc(hl_done, 1)

            dve.wait_ge(gain_in, 16)
            for i in range(NT):
                norm_scale(0, i, xs[:, i, :], xn[:, i % 2, :], xn_done)
                if i:
                    norm_lower(0, i - 1)
            norm_lower(0, NT - 1)

            V.memset(pp[:, :, :], 0.0).then_inc(pool_pad, 1)
            st = [0]

            def step(ins, sem_=pool_st, count=st):
                ins.then_inc(sem_, 1)
                count[0] += 1
                dve.wait_ge(sem_, count[0])

            dve.wait_ge(cst_in, 16 * 7)
            for c in range(2):
                dve.wait_ge(pj_free, 2 * c + 2)
                w1, w2, w4, w8 = PADW - 1, PADW - 3, PADW - 7, PADW - 15
                step(V.tensor_tensor(pb_[:, 0:w1], pp[:, c, 0:w1], pp[:, c, 1:w1 + 1], ALU.add))
                if c == 0:
                    step(V.tensor_tensor(pa[64:128, 0, 0:w2], pb_[64:128, 0:w2], pb_[64:128, 2:w2 + 2], ALU.add))
                    parts = ((0, 64, pb_[0:64, 7:7 + S]), (64, 128, pa[64:128, 0, 6:6 + S]))
                else:
                    step(V.tensor_tensor(pa[:, 1, 0:w2], pb_[:, 0:w2], pb_[:, 2:w2 + 2], ALU.add))
                    step(V.tensor_tensor(pb_[:, 0:w4], pa[:, 1, 0:w4], pa[:, 1, 4:w4 + 4], ALU.add))
                    step(V.tensor_tensor(pa[64:128, 1, 0:w8], pb_[64:128, 0:w8], pb_[64:128, 8:w8 + 8], ALU.add))
                    parts = ((0, 64, pb_[0:64, 4:4 + S]), (64, 128, pa[64:128, 1, 0:S]))
                for a, b, sums in parts:
                    dst = pmix[a:b, c, :]
                    step(V.tensor_scalar(dst, sums, inv[a:b, c:c + 1], None, ALU.mult))
                    V.tensor_tensor(dst[:, 0:8], sums[:, 0:8], edge[a:b, c, 0:8], ALU.mult)
                    step(V.tensor_tensor(dst[:, S - 8:S], sums[:, S - 8:S], edge[a:b, c, 8:16], ALU.mult))
                    step(V.tensor_tensor(pa[a:b, c, 8:8 + S], dst, pp[a:b, c, 8:8 + S], ALU.subtract))
            for c in range(2):
                for hf in range(2):
                    n = 2 * c + hf
                    dve.wait_ge(pool_mm, n + 1)
                    V.tensor_scalar(pmix[:, c, hf * HALF:(hf + 1) * HALF], bank[6 + n % 2][:, :],
                                    pscale[:, c:c + 1], None, ALU.mult).then_inc(pool_ev, 1)

            def scores(g, k):
                n = g * UNITS + k
                c, b = k // NT, k % NT
                _, lo, w, _ = window(g, b)
                dve.wait_ge(qk_done, n + 1)
                if n >= 2:
                    dve.wait_ge(p_done, n - 1)
                for e in range(2):
                    table = bias2[:, 2 * c + e, :] if g == 2 else bias01[:, 4 * g + 2 * c + e, lo:lo + w]
                    V.tensor_tensor_reduce(sc[:, n % 2, e, lo:lo + w], bank[4 + e][:, 0:w],
                                           table, 1.0, FAR, ALU.add, ALU.min,
                                           stat_nm[:, g, b, 2 * c + e:2 * c + e + 1]).then_inc(s_done, 1)

            def probs_out(g, k):
                n = g * UNITS + k
                dve.wait_ge(pt_done, n + 1)
                if n >= 2:
                    dve.wait_ge(pv_done, n - 1)
                tiles = window(g, k % NT)[3]
                for j, (_, rows) in enumerate(tiles):
                    src = bank[6][0:rows, :].rearrange("p (e j q) -> p e j q", e=2, j=2)[:, :, j, :]
                    dst = pt[0:rows, n % 2, :, :].rearrange("p (e j) q -> p e j q", e=2)[:, :, j, :]
                    ins = V.tensor_copy(dst, src)
                ins.then_inc(pt_ev, 1)

            def attn_out(g, k):
                n = g * UNITS + k
                c, b = k // NT, k % NT
                dve.wait_ge(pv_done, n + 1)
                per = S // NRES[g]
                if per >= P:
                    dst = by_residue(ot[:, 2 * g + c, :], g, b * P // per, 1, b * P % per, P)
                else:
                    dst = by_residue(ot[:, 2 * g + c, :], g, b * P // per, P // per, 0, per)
                V.tensor_copy(dst, bank[7][:, 0:P].rearrange("p (r l) -> p r l", l=min(per, P))).then_inc(ot_ev, 1)

            def stats_out(g):
                for n in range(4):
                    m = 4 * g + n
                    hf = n % 2
                    dve.wait_ge(st_done, m + 1)
                    if m == 0:
                        dve.wait_ge(pv_done, GROUPS * UNITS)
                    row = lt[0:4, n // 2, g, :]
                    if g == 0:
                        dst, src = row[:, hf * HALF:(hf + 1) * HALF], bank[4 + n % 2][0:4, :]
                    else:
                        dst = by_residue(row, g, hf * NRES[g] // 2, NRES[g] // 2, 0, S // NRES[g])
                        src = bank[4 + n % 2][0:4, :].rearrange("p (r l) -> p r l", r=NRES[g] // 2)
                    V.tensor_copy(dst, src).then_inc(st_ev, 1)

            dve.wait_ge(bias_in, 32)
            for g in range(GROUPS):
                for k in range(UNITS + 2):
                    if k < UNITS:
                        scores(g, k)
                    if 1 <= k <= UNITS:
                        probs_out(g, k - 1)
                    if k >= 2:
                        attn_out(g, k - 2)
            for g in range(GROUPS):
                stats_out(g)

            al = [0]
            dve.wait_ge(st_ev, 4 * GROUPS)
            nm_t, den_t = lt[:, 0, :, :], lt[:, 1, :, :]
            step(V.tensor_tensor(mn[:, :], nm_t[:, 0, :], nm_t[:, 1, :], ALU.min), al_st, al)
            step(V.tensor_tensor(mn[:, :], mn[:, :], nm_t[:, 2, :], ALU.min), al_st, al)
            step(V.tensor_tensor(nm_t, mn[:, :].unsqueeze(1).broadcast_to([4, GROUPS, S]), nm_t, ALU.subtract), al_st, al)
            dve.wait_ge(al_e, 1)
            step(V.tensor_tensor(den_t, den_t, nm_t, ALU.mult), al_st, al)
            step(V.tensor_tensor(den[:, :], den_t[:, 0, :], den_t[:, 1, :], ALU.add), al_st, al)
            step(V.tensor_tensor(den[:, :], den[:, :], den_t[:, 2, :], ALU.add), al_st, al)
            step(V.reciprocal(mn[:, :], den[:, :]), al_st, al)
            step(V.tensor_tensor(nm_t, nm_t, mn[:, :].unsqueeze(1).broadcast_to([4, GROUPS, S]), ALU.mult), al_st, al)
            dve.wait_ge(ot_ev, GROUPS * UNITS)
            for n in range(4 * GROUPS):
                cols = slice(n % 2 * HALF, (n % 2 + 1) * HALF)
                dve.wait_ge(bc_done, n + 1)
                V.tensor_tensor(ot[:, n // 2, cols], ot[:, n // 2, cols], bank[n % 4][:, :],
                                ALU.mult).then_inc(bc_mul, 1)
            for c in range(2):
                for hf in range(2):
                    cols = slice(hf * HALF, (hf + 1) * HALF)
                    dve.wait_ge(mx_hi, 2 * c + hf + 1)
                    V.tensor_tensor(h_lo[:, c, cols], pmix[:, c, cols], h_hi[:, c, cols],
                                    ALU.subtract).then_inc(mx_lo, 1)
            for n in range(4 * GROUPS):
                cols = slice(n % 2 * HALF, (n % 2 + 1) * HALF)
                dve.wait_ge(mx_hi, 4 + n + 1)
                V.tensor_tensor(h_lo[:, 2 + n // 2, cols], ot[:, n // 2, cols], h_hi[:, 2 + n // 2, cols],
                                ALU.subtract).then_inc(mx_lo, 1)

            dve.wait_ge(gain_in, 32)
            for i in range(NT):
                dve.wait_ge(x_in[i], 32)
                for hf in range(2):
                    n = 2 * i + hf
                    dve.wait_ge(op_done, n + 1)
                    cols = slice(hf * HALF, (hf + 1) * HALF)
                    V.tensor_tensor(xs[:, i, cols], bank[n % 4][:, :], xs[:, i, cols], ALU.add).then_inc(x1_done, 1)
                norm_scale(1, i, xs[:, i, :], xn[:, i % 2, :], xn_done)
                if i:
                    norm_lower(1, i - 1)
            norm_lower(1, NT - 1)

            rs = [0]

            def group(instructions):
                for ins in instructions:
                    ins.then_inc(r_st, 1)
                    rs[0] += 1
                dve.wait_ge(r_st, rs[0])

            for hp in range(Q_PIECES):
                h, half = hp // 2, hp % 2
                for q in range(2):
                    n = 2 * hp + q
                    dve.wait_ge(sc_done, n + 1)
                    src = [bank[4 + n % 4][:, t * NK:(t + 1) * NK] for t in range(4)]
                    val = [top1[:, 4 * q + t, h, half, :] for t in range(4)]
                    idx = [ix1[:, 4 * q + t, h, half, :] for t in range(4)]
                    rest = [rep[:, t, 0:NK] for t in range(4)]
                    group([V.max(val[t][:, 0:8], src[t]) for t in range(4)])
                    group([V.match_replace(rest[t], val[t][:, 0:8], src[t], -FAR) for t in range(4)])
                    group([V.max(val[t][:, 8:16], rest[t]) for t in range(4)])
                    for t in range(4):
                        ins = V.max_index(idx[t][:, 0:8], val[t][:, 0:8], src[t])
                    ins.then_inc(sc_free, 1)
                    for t in range(4):
                        last = V.max_index(idx[t][:, 8:16], val[t][:, 8:16], rest[t])
                    group([last])

            for t in range(NT):
                one, two = top1[:, t, :, 0, :], top1[:, t, :, 1, :]
                shape = [P, PH, TOP, TOP]
                sums = cand[:, :, :].rearrange("p h (a b) -> p h a b", a=TOP)
                group([V.tensor_tensor(sums, one.unsqueeze(3).broadcast_to(shape),
                                       two.unsqueeze(2).broadcast_to(shape), ALU.add),
                       V.tensor_copy(ix1f[:, t, :, :, :], ix1[:, t, :, :, :])])
                group([V.max(top2[:, h, 0:8], cand[:, h, :]) for h in range(PH)])
                group([V.match_replace(rep[:, h, :], top2[:, h, 0:8], cand[:, h, :], -FAR) for h in range(PH)])
                group([V.max(top2[:, h, 8:16], rep[:, h, :]) for h in range(PH)])
                V.tensor_tensor(route[:, 2, t, :].rearrange("p (h k) -> p h k", h=PH), top2[:, :, :],
                                top2[:, :, 0:1].broadcast_to([P, PH, TOP]), ALU.subtract).then_inc(g_ask, 1)
                group([V.max_index(pos[:, 0, h, 0:8], top2[:, h, 0:8], cand[:, h, :]) for h in range(PH)]
                      + [V.max_index(pos[:, 0, h, 8:16], top2[:, h, 8:16], rep[:, h, :]) for h in range(PH)])
                group([V.tensor_scalar(pos[:, 1, :, :], pos[:, 0, :, :], TOP - 1, None, ALU.bitwise_and)])
                group([V.tensor_scalar(pos[:, 0, :, :], pos[:, 0, :, :], 4, None, ALU.logical_shift_right)])
                group([V.tensor_copy(posf[:, :, :, :], pos[:, :, :, :])])
                for half in range(2):
                    ranks = iota[:, 0:TOP].unsqueeze(1).unsqueeze(1).broadcast_to(shape)
                    group([V.tensor_tensor(eq[:, :, :, :], posf[:, half, :, :].unsqueeze(3).broadcast_to(shape),
                                           ranks, ALU.is_equal)])
                    group([V.tensor_tensor(eq[:, :, :, :], eq[:, :, :, :],
                                           ix1f[:, t, :, half, :].unsqueeze(2).broadcast_to(shape), ALU.mult)])
                    group([V.tensor_reduce(route[:, half, t, :].rearrange("p (h k) -> p h k", h=PH),
                                           eq[:, :, :, :], AX.X, ALU.add)])
            dve.wait_ge(g_e, 1)
            gate = route[:, 2, :, :].rearrange("p t (h k) -> p t h k", h=PH)
            group([V.tensor_reduce(gsum[:, 0, :, :], gate, AX.X, ALU.add)])
            group([V.reciprocal(gsum[:, 1, :, :], gsum[:, 0, :, :])])
            V.tensor_tensor(gate, gate, gsum[:, 1, :, :].unsqueeze(3).broadcast_to([P, NT, PH, TOP]),
                            ALU.mult).then_inc(route_done, 1)
            for n in range(6):
                dve.wait_ge(rt_done, n + 1)
                V.tensor_copy(route_t[:, n // 2, n % 2 * HALF:(n % 2 + 1) * HALF], bank[4 + n % 4][:, :]).then_inc(rt_ev, 1)
            dve.wait_ge(rt_ev, 6)

            def one_hots(it, s2, first):
                if not (isinstance(it, int) and it == 0):
                    dve.wait_ge(oh_done, it * 16 + (8 * s2 - 8))
                V.tensor_copy(strip_r[:, s2, :, :],
                              route_t[:, :, bass.ds(it * (2 * TW) + s2 * TW, TW)]).then_inc(oh_cp, 1)
                dve.wait_ge(oh_cp, it * 2 + (s2 + 1))
                for n in range(8):
                    if not (first and n < 2):
                        dve.wait_ge(gp_done, it * 16 + (8 * s2 + n - 1))
                    for k in range(4):
                        t = 4 * n + k
                        V.tensor_scalar(oneh[:, n % 2, 0, k, :], iota[:, :], strip_r[:, s2, 0, t:t + 1], None, ALU.is_equal)
                        ins = V.tensor_scalar(oneh[:, n % 2, 1, k, :], iota[:, :], strip_r[:, s2, 1, t:t + 1],
                                              strip_r[:, s2, 2, t:t + 1], ALU.is_equal, ALU.mult)
                    ins.then_inc(oh_done, 1)

            one_hots(0, 0, True)
            one_hots(0, 1, False)
            with dve.Fori(1, B_BODIES // 2) as it:
                for s2 in range(2):
                    one_hots(it, s2, False)

            dve.wait_ge(m1_done, 2 * NK)
            V.memset(zero[:, :].bitcast(F32), 0.0).then_inc(z_set, 1)

            def gated(hf, it, s, j, first):
                n = hf * NK + VJ * s + j
                if j == 0:
                    dve.wait_ge(a_in[s], it * 16 + (hf * 8 * (NK // VJ) + 16))
                    dve.wait_ge(g_in[s], it * 16 + (hf * 8 * (NK // VJ) + 16))
                if not (first and j < 2):
                    dve.wait_ge(ah_done, it * (2 * VJ) + (n - 1))
                V.tensor_tensor(prod[:, j % 2, :].rearrange("p (b t) -> p b t", t=TW),
                                a_raw[:, s, j, :].rearrange("p (b t) -> p b t", t=TW),
                                g_raw[:, s, :, j * TW:(j + 1) * TW], ALU.mult).then_inc(pd_done, 1)

            def lower_a(it, n, j):
                dve.wait_ge(ah_done, it * (2 * VJ) + (n + 1))
                V.tensor_tensor(a_lo[:, j, :], prod[:, j % 2, :], a_hi[:, j, :], ALU.subtract).then_inc(al_done, 1)

            def gated_group(hf, it, first):
                for s in range(2):
                    for j in range(VJ):
                        gated(hf, it, s, j, first and s == 0)
                        lower_a(it, hf * NK + VJ * s + j, j)

            def add_residual(hf):
                for n in range(8):
                    i, c = 4 * hf + n // 2, n % 2
                    cols = slice(c * HALF, (c + 1) * HALF)
                    V.tensor_tensor(y[:, i, cols], y[:, i, cols], bank[n][:, :], ALU.add).then_inc(y_done, 1)

            gated_group(0, 0, True)
            with dve.Fori(1, NK // VJ // 2) as it:
                gated_group(0, it, False)
            dve.wait_ge(y_in, 16)
            dve.wait_ge(m2_done, NK)
            add_residual(0)
            with dve.Fori(0, NK // VJ // 2) as it:
                gated_group(1, it, False)
            dve.wait_ge(gain_in, 48)
            for i in range(NT):
                if i == 4:
                    dve.wait_ge(m2_done, 2 * NK)
                    add_residual(1)
                norm_scale(2, i, y[:, i, :], yo[:, i % 2, :], yo_done)

        @block.tensor
        def _(pe):
            def both_halves(lhs_hi, lhs_lo, banks, done, between=None):
                for k in range(KC):
                    part = slice(k * P, (k + 1) * P)
                    for lhs, rhs in ((lhs_hi, h_hi), (lhs_hi, h_lo), (lhs_lo, h_hi)):
                        for h in range(2):
                            ins = pe.matmul(banks[h][:, :], lhs[:, part], rhs[:, k, h * HALF:(h + 1) * HALF],
                                            start=(k == 0 and lhs is lhs_hi and rhs is h_hi),
                                            stop=(k == KC - 1 and lhs is lhs_lo))
                            if k == KC - 1 and lhs is lhs_lo:
                                ins.then_inc(done, 1)
                    if between is not None:
                        between(k)

            def norm_turn(k, i):
                n0 = k * NT + i
                pe.wait_ge(xn_done, n0 + 1)
                for c in range(2):
                    n = k * LO_BANKS + 2 * i + c
                    if 2 * i + c >= 4:
                        pe.wait_ge(hl_done, n - 3)
                    for q in range(4):
                        kc = 4 * c + q
                        ins = pe.transpose(bank[(4 if k else 0) + (2 * i + c) % 4][:, q * P:(q + 1) * P],
                                           xn[:, i % 2, kc * P:(kc + 1) * P], ident[:, :])
                    ins.then_inc(xt_done, 1)

            pe.wait_ge(cst_in, 16 * 7)
            for i in range(NT):
                norm_turn(0, i)
            pe.wait_ge(hl_done, LO_BANKS)

            pj = [0]

            def project(n):
                pe.wait_ge(lo_done, n + 1)
                b = pj[0]
                if b >= 4:
                    pe.wait_ge(pj_free, b - 2)
                both_halves(w_hi[:, n % 2, :], w_lo[:, n % 2, :], [bank[b % 4], bank[(b + 1) % 4]], pj_done)
                pj[0] = b + 2

            def project_v(g, j):
                n = 6 + 6 * g
                first, rows = v_tiles(g)[j]
                per = S // NRES[g]
                b = pj[0]
                pe.wait_ge(lo_done, n + 2)
                pe.wait_ge(pj_free, b - 3)
                for k in range(KC):
                    rhs = [w[:, k // 4, :].rearrange("p (k n) -> p k n", k=4)[:, k % 4, :] for w in (w_hi, w_lo)]
                    lhs = []
                    for h in (h_hi, h_lo):
                        lhs.append(by_residue(h[:, k, :], g, first // per, 1, first % per, rows)[:, 0, :])
                    dst = bank[b % 4][0:rows, 0:4 * DH]
                    pe.matmul(dst, lhs[0], rhs[0], start=(k == 0), stop=False)
                    pe.matmul(dst, lhs[0], rhs[1], start=False, stop=False)
                    ins = pe.matmul(dst, lhs[1], rhs[0], start=False, stop=(k == KC - 1))
                ins.then_inc(pj_done, 1)
                pj[0] = b + 1

            def projection_step(g, k):
                if k < 4:
                    project(2 + 6 * g + k)
                else:
                    for j in range(2 * (k - 4), min(2 * (k - 4) + 2, len(v_tiles(g)))):
                        project_v(g, j)

            def qk(g, k):
                n = g * UNITS + k
                c, b = k // NT, k % NT
                k0, _, w, _ = window(g, b)
                if n:
                    pe.wait_ge(s_done, 2 * n)
                for e in range(2):
                    rows = slice(DH * e, DH * e + DH)
                    ins = pe.matmul(bank[4 + e][:, 0:w], qt[g % 2][rows, c, b * P:(b + 1) * P],
                                    kt[g % 2][rows, c, k0:k0 + w], start=True, stop=True)
                ins.then_inc(qk_done, 1)

            def turn(g, k):
                n = g * UNITS + k
                pe.wait_ge(p_done, n + 1)
                if n:
                    pe.wait_ge(pt_ev, n)
                _, lo, _, tiles = window(g, k % NT)
                for e in range(2):
                    for j, (_, rows) in enumerate(tiles):
                        c0 = lo if j == 0 else P
                        ins = pe.transpose(bank[6][0:rows, (2 * e + j) * P:(2 * e + j + 1) * P],
                                           pr[:, n % 2, e, c0:c0 + rows], ident[:, :])
                ins.then_inc(pt_done, 1)

            def pv(g, k):
                n = g * UNITS + k
                c = k // NT
                pe.wait_ge(pt_ev, n + 1)
                if n:
                    pe.wait_ge(ot_ev, n)
                tiles = window(g, k % NT)[3]
                for e in range(2):
                    for j, (tile, rows) in enumerate(tiles):
                        ins = pe.matmul(bank[7][DH * e:DH * e + DH, 0:P],
                                        vt[g % 2][0:rows, tile, (2 * c + e) * DH:(2 * c + e + 1) * DH],
                                        pt[0:rows, n % 2, 2 * e + j, :], start=(j == 0), stop=(j == len(tiles) - 1))
                ins.then_inc(pv_done, 1)

            project(0)
            project(1)
            for k in range(4 + (len(v_tiles(0)) + 1) // 2):
                projection_step(0, k)
            pool_steps = (8, 18)
            for c in range(2):
                pe.wait_ge(pool_st, pool_steps[c])
                for hf in range(2):
                    if c:
                        pe.wait_ge(pool_ev, hf + 1)
                    for a in (0, DH):
                        ins = pe.matmul(bank[6 + hf][a:a + DH, :], wpool[a:a + DH, c, :],
                                        pa[a:a + DH, c, 8 + hf * HALF:8 + (hf + 1) * HALF], start=True, stop=True)
                    ins.then_inc(pool_mm, 1)
            pe.wait_ge(pool_ev, 4)
            for g in range(GROUPS):
                pe.wait_ge(pj_free, PJ_G[g])
                qk(g, 0)
                for k in range(UNITS):
                    turn(g, k)
                    if k + 1 < UNITS:
                        qk(g, k + 1)
                    if k:
                        pv(g, k - 1)
                    if g + 1 < GROUPS and k < 4 + (len(v_tiles(g + 1)) + 1) // 2:
                        projection_step(g + 1, k)
                pv(g, UNITS - 1)

            for m in range(4 * GROUPS):
                g, n = m // 4, m % 4
                if m == 0:
                    pe.wait_ge(s_done, 2 * GROUPS * UNITS)
                if m >= 2:
                    pe.wait_ge(st_ev, m - 1)
                stat = (stat_nm, stat_den)[n // 2]
                for q in range(4):
                    ins = pe.transpose(bank[4 + n % 2][0:4, q * P:(q + 1) * P], stat[:, g, 4 * (n % 2) + q, :],
                                       ident[:, :])
                ins.then_inc(st_done, 1)
            pe.wait_ge(al_st, 8)
            for n in range(4 * GROUPS):
                if n >= 4:
                    pe.wait_ge(bc_mul, n - 3)
                g, c = n // 4, n // 2 % 2
                pe.matmul(bank[n % 4][:, :], sel[0:4, c, :], lt[0:4, 0, g, n % 2 * HALF:(n % 2 + 1) * HALF],
                          start=True, stop=True).then_inc(bc_done, 1)

            for i in range(NT):
                if i == 0:
                    pe.wait_ge(bc_mul, 4 * GROUPS)
                if i >= 2:
                    pe.wait_ge(x1_done, 2 * i - 2)
                toks = slice(i * P, (i + 1) * P)
                for k in range(KC):
                    if i == 0:
                        pe.wait_ge(mx_lo, 2 * k + 2)
                        pe.wait_ge(lo_done, W_OUT0 + k + 1)
                    for lhs, rhs in ((h_hi, wo_hi), (h_hi, wo_lo), (h_lo, wo_hi)):
                        for h in range(2):
                            ins = pe.matmul(bank[(2 * i + h) % 4][:, :], lhs[:, k, toks],
                                            rhs[:, k, h * HALF:(h + 1) * HALF], start=(k == 0 and rhs is wo_hi
                                                                                      and lhs is h_hi),
                                            stop=(k == KC - 1 and lhs is h_lo))
                            if k == KC - 1 and lhs is h_lo:
                                ins.then_inc(op_done, 1)
                if i:
                    norm_turn(1, i - 1)
            norm_turn(1, NT - 1)

            def key_scores(hp):
                pe.wait_ge(pj_free, PJ_IN + 2 * hp + 2)
                for q in range(2):
                    n = 2 * hp + q
                    if n >= 4:
                        pe.wait_ge(sc_free, n - 3)
                    for t in range(4):
                        ins = pe.matmul(bank[4 + n % 4][:, t * NK:(t + 1) * NK],
                                        q2[:, hp % 2, (4 * q + t) * P:(4 * q + t + 1) * P], sk[:, hp, :],
                                        start=True, stop=True)
                    ins.then_inc(sc_done, 1)

            pe.wait_ge(hl_done, 2 * LO_BANKS)
            pe.wait_ge(x1_done, 2 * NT)
            for hp in range(Q_PIECES):
                project(W_Q0 + hp)
                if hp == 0:
                    pe.wait_ge(sk_in, 16)
                else:
                    key_scores(hp - 1)
            key_scores(Q_PIECES - 1)

            def chunk(it, s, first, between=None):
                pe.wait_ge(lo_done, it * 2 + (W_U0 + s + 1))
                if first:
                    pe.wait_ge(pj_free, PJ_ALL)
                else:
                    pe.wait_ge(act_done, it * 4 + (2 * s - 2))
                both_halves(w_hi[:, s, :], w_lo[:, s, :], [bank[2 * s], bank[2 * s + 1]], m1_done, between)

            for s in range(2):
                chunk(0, s, True)
            with pe.Fori(1, A_BODIES) as it:
                for s in range(2):
                    chunk(it, s, False)
            pe.wait_ge(route_done, 1)
            for n in range(6):
                if n >= 4:
                    pe.wait_ge(rt_ev, n - 3)
                for q in range(4):
                    ins = pe.transpose(bank[4 + n % 4][:, q * P:(q + 1) * P], route[:, n // 2, 4 * (n % 2) + q, :],
                                       ident[:, :])
                ins.then_inc(rt_done, 1)

            def gates(it, s2, n, first):
                pe.wait_ge(oh_done, it * 16 + (8 * s2 + n + 1))
                if not (first and n < 2):
                    pe.wait_ge(gs_done, it * 16 + (8 * s2 + n - 1))
                for k in range(4):
                    ins = pe.matmul(bank[4 + n % 2][:, k * NK:(k + 1) * NK], oneh[:, n % 2, 0, k, :],
                                    oneh[:, n % 2, 1, k, :], start=True, stop=True)
                ins.then_inc(gp_done, 1)

            def strip(it, s2, first):
                for s in range(2):
                    def between(k):
                        if k % 2 == 0:
                            gates(it, s2, 4 * s + k // 2, first)
                    chunk(it * 2 + (A_BODIES + s2), s, False, between)

            pe.wait_ge(rt_ev, 6)
            strip(0, 0, True)
            strip(0, 1, False)
            with pe.Fori(1, B_BODIES // 2) as it:
                for s2 in range(2):
                    strip(it, s2, False)

            def products(hf, it, s, j):
                n = hf * NK + VJ * s + j
                pe.wait_ge(vl_done, it * (2 * VJ) + (n + 1))
                pe.wait_ge(al_done, it * (2 * VJ) + (n + 1))
                for q in range(4):
                    toks = slice(q * P, (q + 1) * P)
                    for lhs, rhs in ((a_hi, v_hi), (a_hi, v_lo), (a_lo, v_hi)):
                        for c in range(2):
                            ins = pe.matmul(bank[2 * q + c][:, :], lhs[:, j, toks],
                                            rhs[:, j, c * HALF:(c + 1) * HALF], start=False, stop=True,
                                            skip_group_check=True)
                ins.then_inc(m2_done, 1)

            pe.wait_ge(z_set, 1)
            pe.wait_ge(act_done, 2 * NK)
            pe.wait_ge(gs_done, 8 * B_BODIES)
            for hf in range(2):
                for n in range(8):
                    if hf:
                        pe.wait_ge(y_done, n + 1)
                    pe.matmul(bank[n][:, :], zero[:, 0:P], zero[:, :], start=True, stop=True)
                with pe.Fori(0, NK // VJ // 2) as it:
                    for s in range(2):
                        for j in range(VJ):
                            products(hf, it, s, j)


def kernel(x, g_mix, w_in, w_pool, pool_scale, w_out, g_ffn, w_peer_q, peer_subkeys, peer_u, peer_v, g_final):
    import numpy as np
    import concourse.bacc as bacc
    from concourse.bass_utils import run_bass_kernel_spmd

    def arr(a):
        return np.ascontiguousarray(a)

    w_in = np.asarray(w_in)[0]
    def cols(c0):
        return w_in[:, c0:c0 + P].reshape(KC, P, P).transpose(1, 0, 2).reshape(P, 1024)

    pool_w, attn_w = 256, 768
    pieces = [cols(0), cols(P)]
    for g in range(GROUPS):
        for part in range(2):
            for c in range(2):
                pieces.append(cols(pool_w + part * attn_w + (2 * g + c) * P))
        wv = w_in[:, pool_w + 2 * attn_w + g * 256:pool_w + 2 * attn_w + (g + 1) * 256]
        for k in range(2):
            pieces.append(wv.reshape(2, 4, P, 256)[k].transpose(1, 0, 2).reshape(P, 1024))
    ins = {
        "x": arr(x),
        "g_mix": arr(g_mix),
        "w_in": np.stack(pieces),
        "w_pool": arr(np.asarray(w_pool)[0].reshape(2, 2 * DH, DH).transpose(1, 0, 2)),
        "pool_scale": arr(np.asarray(pool_scale)[0].reshape(2, P).T),
        "w_out": arr(np.asarray(w_out)[0].reshape(KC, P, D)),
        "g_ffn": arr(g_ffn),
        "w_q": arr(np.asarray(w_peer_q)[0].reshape(KC, P, Q_PIECES, P).transpose(2, 1, 0, 3)).reshape(Q_PIECES, P, 1024),
        "subkeys": arr(np.asarray(peer_subkeys)[0].reshape(Q_PIECES, NK, P).transpose(2, 0, 1)),
        "u": arr(np.asarray(peer_u)[0].reshape(NK, NK, KC, P).transpose(1, 3, 2, 0)).reshape(NK, P, 1024),
        "v": arr(np.asarray(peer_v)[0].reshape(NK, NK // VJ, VJ, D).transpose(1, 0, 2, 3)),
        "g_final": arr(np.asarray(g_final).reshape(1, D)),
    }
    slopes = (2.0 ** (-8.0 * np.arange(1, 13) / 12)).astype(np.float32)
    q = np.arange(P)[:, None]
    rel = np.abs(np.arange(2 * P)[None, :] - SPAN - q)
    bias01 = np.stack([np.where(rel <= SPAN, slopes[h] * (DIL[h // 4] * rel).astype(np.float32), np.float32(1e30))
                       for h in range(8)], axis=1).astype(np.float32)
    k = np.arange(P)[None, :]
    bias2 = np.stack([np.where(q // 64 == k // 64, slopes[8 + h] * (DIL[2] * np.abs(q - k)).astype(np.float32),
                               np.float32(1e30)) for h in range(4)], axis=1).astype(np.float32)
    sel = np.zeros((4, 2, P), np.float32)
    for h in range(4):
        sel[h, h // 2, DH * (h % 2):DH * (h % 2) + DH] = 1.0
    edge = np.zeros((P, 2, 16), np.float32)
    inv = np.zeros((P, 2), np.float32)
    t = np.concatenate([np.arange(8), np.arange(S - 8, S)])
    for g, w in enumerate((2, 4, 8, 16)):
        rows = slice(DH * (g % 2), DH * (g % 2) + DH)
        n = np.clip(t + w // 2, 0, S) - np.clip(t - w // 2, 0, S)
        edge[rows, g // 2, :] = (1.0 / n).astype(np.float32)
        inv[rows, g // 2] = 1.0 / w
    ins |= {"ident_c": np.eye(P, dtype=np.float32),
            "iota_c": np.ascontiguousarray(np.broadcast_to(np.arange(P, dtype=np.float32), (P, P))),
            "bias01_c": arr(bias01), "bias2_c": arr(bias2), "sel_c": sel, "edge_c": edge, "inv_c": inv}

    nc = bacc.Bacc("TRN2", target_bir_lowering=False, num_devices=1)
    aps = {n: nc.dram_tensor(f"in_{n}", a.shape, mybir.dt.from_np(a.dtype), kind="ExternalInput").ap()
           for n, a in ins.items()}
    out = nc.dram_tensor("out", (1, S, D), F32, kind="ExternalOutput").ap()
    build(nc, out=out, **aps)
    r = run_bass_kernel_spmd(nc, [{f"in_{n}": a for n, a in ins.items()}], core_ids=[0])
    return r.results[0]["out"]
```

```python
import concourse.bass as bass
from concourse import mybir
from contextlib import ExitStack

F32 = mybir.dt.float32
F32R = mybir.dt.float32r
U32 = mybir.dt.uint32
ALU = mybir.AluOpType
ACT = mybir.ActivationFunctionType
AX = mybir.AxisListType

P = 128
D = 1024
S = 1024
KC = D // P
NT = S // P
HALF = 512
DH = 64
GROUPS = 3
DIL = (1, 4, 16)
NRES = DIL
SPAN = 64
EPS = 1e-6
PH = 8
TOP = 16
NK = 128
FAR = 3.0e38

IN_PIECES = 2 + 6 * GROUPS
OUT_PIECES = KC
Q_PIECES = 2 * PH
W_OUT0 = IN_PIECES
W_Q0 = W_OUT0 + OUT_PIECES
W_U0 = W_Q0 + Q_PIECES

DT = NT - 1
DS = DT * P
MH = DS // 2
HT = (4, DT - 4)
TW = 32
STRIPS = DS // TW
BODIES = NK // 2
GR = 4
U_STEPS = P // GR
A_BODIES = 16
EXP_BODY = 14
A2_BODIES = U_STEPS - STRIPS
B0 = A_BODIES + A2_BODIES
C0 = B0 + STRIPS
V_STEPS1 = BODIES - C0
NG2 = NK // 8
assert U_STEPS - V_STEPS1 == NG2
VJ = 4
UNITS = 16


def v_tiles(g):
    if g == 2:
        return [(r * SPAN, SPAN) for r in range(NRES[2])]
    length = S // NRES[g]
    out = []
    for r in range(NRES[g]):
        for x in range(length // P + 1):
            lo, hi = max(x * P - SPAN, 0), min(x * P + SPAN, length)
            out.append((r * length + lo, hi - lo))
    return out


def window(g, b):
    if g == 2:
        return b * P, 0, P, [(b, P)]
    per = S // NRES[g] // P
    r, x = b // per, b % per
    lo = SPAN if x == 0 else 0
    hi = 2 * P - SPAN if x == per - 1 else 2 * P
    return b * P - SPAN + lo, lo, hi - lo, [(r * (per + 1) + x, P - lo), (r * (per + 1) + x + 1, hi - P)]


def by_residue(ap, g, r0, nr, l0, nl):
    n = NRES[g]
    return ap.rearrange("p (l r) -> p r l", r=n)[:, r0:r0 + nr, l0:l0 + nl]


def build(nc, x, g_mix, w_in, w_pool, pool_scale, w_out, g_ffn, w_q, subkeys, u, u_rows, v, g_final,
          ident_c, iota_c, bias01_c, bias2_c, sel_c, edge_c, inv_c, out):
    ctx = ExitStack()
    with ctx:
        base = (nc.sbuf_base + 63) // 64 * 64

        def at(name, kb, shape, dt=F32):
            return nc.alloc_sbuf_tensor_at(name, shape, dt, offset=base + int(kb * 1024))

        def sem(name):
            return ctx.enter_context(nc.semaphore(name))

        h_hi = at("h_hi", 0, [P, KC, S], F32R)
        h_lo = at("h_lo", 32, [P, KC, S], F32R)
        xs = at("xs", 64, [P, NT, D])
        ot = at("ot", 64, [P, 2 * GROUPS, S])
        pmix = at("pmix", 88, [P, 2, S])
        w_raw = at("w_raw", 96, [P, 2, 1024])
        w_hi = at("w_hi", 104, [P, 2, 1024], F32R)
        w_lo = at("w_lo", 112, [P, 2, 1024], F32R)
        gain = at("gain", 120, [P, D])
        ident = at("ident", 124, [P, P])
        iota = at("iota", 124.5, [P, P])
        stat_nm = at("stat_nm", 125, [P, GROUPS, NT, 4])
        stat_den = at("stat_den", 125.375, [P, GROUPS, NT, 4])
        ss = at("ss", 125.75, [P, 3, NT])
        std = at("std", 125.875, [P, 3, NT])
        rstd = at("rstd", 126, [P, 3, NT])
        sel = at("sel", 126.125, [4, 2, P])
        wpool = at("wpool", 127.125, [P, 2, DH])
        pscale = at("pscale", 127.625, [P, 2])
        edge = at("edge", 127.6875, [P, 2, 16])
        inv = at("inv", 127.8125, [P, 2])
        xn = at("xn", 128, [P, 2, D])
        bias01 = at("bias01", 128, [P, 8, 2 * P])
        bias2 = at("bias2", 136, [P, 4, P])
        qt = [at(f"qt{s}", 138 + 28 * s, [P, 2, S]) for s in range(2)]
        kt = [at(f"kt{s}", 146 + 28 * s, [P, 2, S]) for s in range(2)]
        vt = [at(f"vt{s}", 154 + 28 * s, [P, 12, 4 * DH]) for s in range(2)]
        sc = at("sc", 194, [P, 2, 2, 2 * P])
        pr = at("pr", 198, [P, 2, 2, 2 * P])
        pt = at("pt", 202, [P, 2, 4, P])
        PADW = S + 16
        pp = at("pp", 166, [P, 2, PADW])
        pa = at("pa", 174.125, [P, 2, PADW])
        pb_ = at("pb_", 182.25, [P, PADW])
        lt = at("lt", 138, [4, 2, GROUPS, S])
        mn = at("mn", 162, [4, S])
        den = at("den", 166, [4, S])
        wo_hi = at("wo_hi", 138, [P, KC, D], F32R)
        wo_lo = at("wo_lo", 170, [P, KC, D], F32R)
        sk = at("sk", 138, [P, 2 * PH, NK])
        q2 = at("q2", 146, [P, 2, S])
        top1 = at("top1", 154, [P, NT, PH, 2, TOP])
        ix1 = at("ix1", 162, [P, NT, PH, 2, TOP], U32)
        ix1f = at("ix1f", 170, [P, NT, PH, 2, TOP])
        cand = at("cand", 178, [P, PH, TOP * TOP])
        eq = at("eq", 186, [P, PH, TOP, TOP])
        rep = at("rep", 194, [P, 8, 2 * P])
        pos = at("pos", 202, [P, 2, PH, TOP], U32)
        posf = at("posf", 203, [P, 2, PH, TOP])
        top2 = at("top2", 204, [P, PH, TOP])
        gsum = at("gsum", 204.5, [P, 2, NT, PH])
        act_st = at("act_st", 64, [P, 2, DS])
        route = at("route", 72, [P, 3, NT, P])
        oneh = at("oneh", 84, [P, 2, 2, 4, P])
        strip_r = at("strip_r", 92, [P, 2, 3, TW])
        g_st = at("g_st", 138, [P, 2, NK, TW])
        route_t = at("route_t", 170, [P, 3, DS])
        rows = at("rows", 182, [P, GR, D])
        ya = at("ya", 198, [P, D])
        ids = at("ids", 205, [P, P], U32)
        uh = at("uh", 205.5, [P, P])
        ids4 = at("ids4", 206, [P, GR], U32)
        uh4 = at("uh4", 206.125, [P, GR])
        w4 = at("w4", 206.25, [P, GR])
        v_raw = at("v_raw", 0, [P, 2, VJ, D])
        a_raw = at("a_raw", 32, [P, 2, VJ, HALF])
        g_raw = at("g_raw", 48, [P, 2, HALF // TW, VJ * TW])
        v_hi = at("v_hi", 64, [P, VJ, D], F32R)
        v_lo = at("v_lo", 80, [P, VJ, D], F32R)
        a_hi = at("a_hi", 96, [P, VJ, HALF], F32R)
        a_lo = at("a_lo", 104, [P, VJ, HALF], F32R)
        prod = at("prod", 112, [P, 2, HALF])
        zero = at("zero", 116, [P, HALF], F32R)
        y = at("y", 138, [P, NT, D])
        yo = at("yo", 170, [P, 2, D])

        bank = [ctx.enter_context(nc.psum_tensor(f"bank{k}", [P, HALF], F32)) for k in range(8)]

        act_d = nc.dram_tensor("act_d", [NK, P, DS], F32).ap()
        g_d = nc.dram_tensor("g_d", [STRIPS, P, NK, TW], F32).ap()
        x1_d = nc.dram_tensor("x1_d", [NT, P, D], F32).ap()

        cst_in = sem("cst_in")
        bias_in = sem("bias_in")
        gain_in = sem("gain_in")
        x_in = [sem(f"x_in{i}") for i in range(NT)]
        sk_in = sem("sk_in")
        raw_in = [sem("raw_in0"), sem("raw_in1")]
        hi_done = sem("hi_done")
        lo_done = sem("lo_done")
        ss_done = sem("ss_done")
        std_done = sem("std_done")
        rs_done = sem("rs_done")
        xn_done = sem("xn_done")
        xt_done = sem("xt_done")
        hh_done = sem("hh_done")
        hl_done = sem("hl_done")
        pj_done = sem("pj_done")
        pj_free = sem("pj_free")
        pool_pad = sem("pool_pad")
        pool_st = sem("pool_st")
        pool_mm = sem("pool_mm")
        pool_ev = sem("pool_ev")
        qk_done = sem("qk_done")
        s_done = sem("s_done")
        p_done = sem("p_done")
        pt_done = sem("pt_done")
        pt_ev = sem("pt_ev")
        pv_done = sem("pv_done")
        ot_ev = sem("ot_ev")
        st_done = sem("st_done")
        st_ev = sem("st_ev")
        al_st = sem("al_st")
        al_e = sem("al_e")
        bc_done = sem("bc_done")
        bc_mul = sem("bc_mul")
        mx_hi = sem("mx_hi")
        mx_lo = sem("mx_lo")
        op_done = sem("op_done")
        x1_done = sem("x1_done")
        x1_out = sem("x1_out")
        sc_done = sem("sc_done")
        sc_free = sem("sc_free")
        r_st = sem("r_st")
        g_e = sem("g_e")
        g_ask = sem("g_ask")
        route_done = sem("route_done")
        m1_done = sem("m1_done")
        act_done = sem("act_done")
        act_out = [sem("act_out0"), sem("act_out1")]
        rt_done = sem("rt_done")
        rt_ev = sem("rt_ev")
        oh_cp = sem("oh_cp")
        oh_done = sem("oh_done")
        gp_done = sem("gp_done")
        gs_done = sem("gs_done")
        g_out = [sem("g_out0"), sem("g_out1")]
        ids_done = sem("ids_done")
        ids_cp = sem("ids_cp")
        row_in = [sem(f"row_in{r}") for r in range(GR)]
        row_used = sem("row_used")
        uh_cp = sem("uh_cp")
        uh_act = sem("uh_act")
        uh_gate = sem("uh_gate")
        w4_cp = sem("w4_cp")
        ya_in = sem("ya_in")
        v_in = [sem("v_in0"), sem("v_in1")]
        a_in = [sem("a_in0"), sem("a_in1")]
        g_in = [sem("g_in0"), sem("g_in1")]
        y_in = sem("y_in")
        z_set = sem("z_set")
        vh_done = sem("vh_done")
        vl_done = sem("vl_done")
        pd_done = sem("pd_done")
        ah_done = sem("ah_done")
        al_done = sem("al_done")
        m2_done = sem("m2_done")
        y_done = sem("y_done")
        yo_done = sem("yo_done")
        y_out = [sem("y_out0"), sem("y_out1")]

        block = ctx.enter_context(nc.Block())
        win_d, wout_d, wq_d, u_d = w_in, w_out, w_q, u
        v_rows = v.rearrange("j i d -> (j i) d")
        out_t = out.rearrange("a (t p) d -> (a t) p d", p=P)
        x_t = x.rearrange("a (t p) d -> (a t) p d", p=P)

        def bcast_row(row):
            return bass.AP(tensor=row.tensor, offset=row.offset, ap=[[0, P]] + [list(a) for a in row.ap[-1:]])

        PIECE_BANKS = [2, 4]
        for g in range(GROUPS):
            for _ in range(4):
                PIECE_BANKS.append(PIECE_BANKS[-1] + 2)
            PIECE_BANKS += [PIECE_BANKS[-1] + len(v_tiles(g))] * 2
        PJ_G = [PIECE_BANKS[2 + 6 * g + 5] for g in range(GROUPS)]
        PJ_IN = PIECE_BANKS[-1]
        for _ in range(Q_PIECES):
            PIECE_BANKS.append(PIECE_BANKS[-1] + 2)
        PJ_ALL = PIECE_BANKS[-1]
        LO_BANKS = 2 * NT

        @block.sync
        def _(sp):
            sp.dma_start(gain[:, :], bcast_row(g_mix)).then_inc(gain_in, 16)
            for i in range(NT):
                sp.dma_start(xs[:, i, :], x_t[i]).then_inc(x_in[i], 16)
                if i == 1:
                    consts = ((ident[:, :], ident_c), (iota[:, :], iota_c), (sel[:, :, :], sel_c),
                              (wpool[:, :, :], w_pool), (pscale[:, :], pool_scale), (edge[:, :, :], edge_c),
                              (inv[:, :], inv_c))
                    for dst, src in consts:
                        sp.dma_start(dst, src).then_inc(cst_in, 16)

            def load_piece(n, src):
                if n >= 2:
                    sp.wait_ge(lo_done, n - 1)
                sp.dma_start(w_raw[:, n % 2, :], src).then_inc(raw_in[n % 2], 16)

            for n in range(IN_PIECES):
                load_piece(n, win_d[n])
                if n == 2:
                    sp.wait_ge(xt_done, LO_BANKS)
                    sp.dma_start(bias01[:, :, :], bias01_c).then_inc(bias_in, 16)
                    sp.dma_start(bias2[:, :, :], bias2_c).then_inc(bias_in, 16)
                    sp.dma_start(gain[:, :], bcast_row(g_ffn)).then_inc(gain_in, 16)
            for n in range(OUT_PIECES):
                load_piece(W_OUT0 + n, wout_d[n])
            sp.wait_ge(mx_lo, 2 * GROUPS * 2 + 4)
            for i in range(NT):
                sp.dma_start(xs[:, i, :], x_t[i]).then_inc(x_in[i], 16)
                if i < 2:
                    load_piece(W_Q0 + i, wq_d[i])
            for i in range(NT):
                sp.wait_ge(x1_done, 2 * i + 2)
                sp.dma_start(x1_d[i], xs[:, i, :]).then_inc(x1_out, 16)
            sp.wait_ge(op_done, 2 * NT)
            sp.dma_start(sk[:, :, :], subkeys).then_inc(sk_in, 16)
            sp.wait_ge(xn_done, 2 * NT)
            sp.dma_start(gain[:, :], bcast_row(g_final)).then_inc(gain_in, 16)
            for n in range(2, Q_PIECES):
                load_piece(W_Q0 + n, wq_d[n])
            load_piece(W_U0, u_d[0])
            load_piece(W_U0 + 1, u_d[1])

            def first_half(it, last=False):
                for s in range(2):
                    if not last:
                        sp.wait_ge(lo_done, it * 2 + (W_U0 + s + 1))
                        sp.dma_start(w_raw[:, s, :], u_d[it * 2 + (2 + s)]).then_inc(raw_in[s], 16)
                    sp.wait_ge(act_done, it * 4 + (2 * s + 2))
                    sp.dma_start(act_d[it * 2 + s], act_st[:, s, :]).then_inc(act_out[s], 16)

            with sp.Fori(0, B0) as it:
                first_half(it)
            with sp.Fori(0, STRIPS // 2) as it:
                for s2 in range(2):
                    first_half(it * 2 + (B0 + s2))
                    sp.wait_ge(gs_done, it * 16 + (8 * s2 + 8))
                    sp.dma_start(g_d[it * 2 + s2], g_st[:, s2, :, :]).then_inc(g_out[s2], 16)
            sp.wait_ge(x1_out, 16 * NT)
            sp.dma_start(ya[:, :], x1_d[DT]).then_inc(ya_in, 16)
            with sp.Fori(C0, BODIES - 1) as it:
                first_half(it)
            first_half(BODIES - 1, last=True)

            for s in range(2):
                sp.wait_ge(act_out[s], 16 * NK // 2)
                sp.wait_ge(g_out[s], 16 * STRIPS // 2)
            sp.wait_ge(m1_done, 2 * NK)

            def loads(hf, it, s):
                sp.dma_start(v_raw[:, s, :, :], v[bass.ds(it * (2 * VJ) + VJ * s, VJ), :, :]
                             .rearrange("j p d -> p j d")).then_inc(v_in[s], 16)
                t0, n = hf * HALF, HT[hf] * P
                sp.dma_start(a_raw[:, s, :, 0:n],
                             act_d[bass.ds(it * (2 * VJ) + VJ * s, VJ), :, t0:t0 + n]
                             .rearrange("j p t -> p j t")).then_inc(a_in[s], 16)
                sp.dma_start(g_raw[:, s, 0:n // TW, :],
                             g_d[t0 // TW:(t0 + n) // TW, :, bass.ds(it * (2 * VJ) + VJ * s, VJ), :]
                             .rearrange("b p j t -> p b (j t)")).then_inc(g_in[s], 16)

            def free_raw(hf, it, s):
                sp.wait_ge(vl_done, it * (2 * VJ) + (hf * NK + VJ * s - VJ))
                sp.wait_ge(pd_done, it * (2 * VJ) + (hf * NK + VJ * s - VJ))

            for hf in range(2):
                for s in range(2):
                    if hf:
                        free_raw(hf, 0, s)
                    loads(hf, 0, s)
                if hf == 0:
                    sp.dma_start(y[:, 0:DT, :], x1_d[0:DT].rearrange("t p d -> p t d")).then_inc(y_in, 16)
                with sp.Fori(1, NG2) as it:
                    for s in range(2):
                        free_raw(hf, it, s)
                        loads(hf, it, s)
            for i in range(NT):
                sp.wait_ge(yo_done, i + 1)
                sp.dma_start(out_t[i], yo[:, i % 2, :]).then_inc(y_out[i % 2], 16)
            for s in range(2):
                sp.wait_ge(y_out[s], 16 * NT // 2)

        @block.gpsimd
        def _(pool):
            def lower(n, dst, hi):
                pool.wait_ge(hi_done, n + 1)
                nc.gpsimd.tensor_tensor(dst, w_raw[:, n % 2, :], hi, ALU.subtract).then_inc(lo_done, 1)

            for n in range(IN_PIECES):
                lower(n, w_lo[:, n % 2, :], w_hi[:, n % 2, :])
            for n in range(OUT_PIECES):
                lower(W_OUT0 + n, wo_lo[:, n, :], wo_hi[:, n, :])
            for n in range(Q_PIECES):
                lower(W_Q0 + n, w_lo[:, n % 2, :], w_hi[:, n % 2, :])

            def lower_u(it, s):
                pool.wait_ge(hi_done, it * 2 + (W_U0 + s + 1))
                nc.gpsimd.tensor_tensor(w_lo[:, s, :], w_raw[:, s, :], w_hi[:, s, :],
                                        ALU.subtract).then_inc(lo_done, 1)

            def next_ids(it, step0, first=False):
                if first:
                    pool.wait_ge(ids_done, 1)
                else:
                    pool.wait_ge(row_used, it * GR + GR * step0)
                nc.gpsimd.tensor_copy(ids4[:, :], ids[:, bass.ds(it * GR, GR)]).then_inc(ids_cp, 1)
                pool.wait_ge(ids_cp, it + (step0 + 1))

            def gather(table):
                for r in range(GR):
                    nc.gpsimd.indirect_dma_start(rows[:, r, :], None, table,
                                                 bass.IndirectOffsetOnAxis(ids4[:, r:r + 1], 0)).then_inc(row_in[r], 16)

            with pool.Fori(0, A_BODIES) as it:
                for s in range(2):
                    lower_u(it, s)
            next_ids(0, 0, first=True)
            lower_u(A_BODIES, 0)
            gather(u_rows)
            lower_u(A_BODIES, 1)
            with pool.Fori(1, U_STEPS) as it:
                next_ids(it, 0)
                lower_u(it + A_BODIES, 0)
                gather(u_rows)
                lower_u(it + A_BODIES, 1)
            with pool.Fori(0, V_STEPS1) as it:
                next_ids(it, U_STEPS)
                lower_u(it + C0, 0)
                gather(v_rows)
                lower_u(it + C0, 1)

            for hf in range(2):
                with pool.Fori(0, NG2) as it:
                    for s in range(2):
                        for j in range(VJ):
                            fetch = hf == 0 and s == 0 and j == 1
                            if fetch:
                                next_ids(it + V_STEPS1, U_STEPS)
                            pool.wait_ge(vh_done, it * (2 * VJ) + (hf * NK + VJ * s + j + 1))
                            nc.gpsimd.tensor_tensor(v_lo[:, j, :], v_raw[:, s, j, :], v_hi[:, j, :],
                                                    ALU.subtract).then_inc(vl_done, 1)
                            if fetch:
                                gather(v_rows)

        @block.scalar
        def _(act):
            def upper(n, dst):
                act.wait_ge(raw_in[n % 2], 16 * (n // 2 + 1))
                nc.scalar.activation(dst, w_raw[:, n % 2, :], ACT.Copy).then_inc(hi_done, 1)

            def upper_slot(n, m):
                if m >= 2:
                    act.wait_ge(pj_done, PIECE_BANKS[m - 2])
                upper(n, w_hi[:, n % 2, :])

            def norm_stats(k, i):
                n = k * NT + i
                if n >= 2:
                    act.wait_ge(xt_done, 2 * (n - 1))
                nc.scalar.activation(xn[:, i % 2, :], xs[:, i, :], ACT.Square,
                                     accum_out=ss[:, k, i:i + 1]).then_inc(ss_done, 1)
                act.wait_ge(rs_done, 2 * n + 1)
                nc.scalar.activation(std[:, k, i:i + 1], rstd[:, k, i:i + 1], ACT.Sqrt).then_inc(std_done, 1)

            def norm_upper(k, i):
                for c in range(2):
                    n = k * LO_BANKS + 2 * i + c
                    act.wait_ge(xt_done, n + 1)
                    nc.scalar.activation(h_hi[:, 4 * c:4 * c + 4, i * P:(i + 1) * P],
                                         bank[(4 if k else 0) + (2 * i + c) % 4][:, :]
                                         .rearrange("p (k t) -> p k t", k=4), ACT.Copy).then_inc(hh_done, 1)

            for i in range(NT):
                act.wait_ge(x_in[i], 16)
                norm_stats(0, i)
                if i:
                    norm_upper(0, i - 1)
            upper_slot(0, 0)
            norm_upper(0, NT - 1)
            upper_slot(1, 1)

            pj = [0]

            def take(dst, src_of, scale=1.0):
                n = pj[0]
                act.wait_ge(pj_done, n + 1)
                nc.scalar.activation(dst, src_of(bank[n % 4]), ACT.Copy, scale=scale).then_inc(pj_free, 1)
                pj[0] = n + 1

            act.wait_ge(pool_pad, 1)
            for c in range(2):
                for hf in range(2):
                    take(pp[:, c, 8 + hf * HALF:8 + (hf + 1) * HALF], lambda b: b[:, :])
                upper_slot(2 + c, 2 + c)

            def exps(g, k):
                n = g * UNITS + k
                c, b = k // NT, k % NT
                _, lo, w, _ = window(g, b)
                for e in range(2):
                    if e == 0:
                        act.wait_ge(s_done, 2 * n + 2)
                        if n >= 2:
                            act.wait_ge(pt_done, n - 1)
                    ins = nc.scalar.activation(pr[:, n % 2, e, lo:lo + w], sc[:, n % 2, e, lo:lo + w], ACT.Exp,
                                               bias=stat_nm[:, g, b, 2 * c + e:2 * c + e + 1], scale=-1.0,
                                               accum_out=stat_den[:, g, b, 2 * c + e:2 * c + e + 1])
                ins.then_inc(p_done, 1)

            def projections(g):
                length, n_res = S // NRES[g], NRES[g]
                if g == 1:
                    act.wait_ge(pool_mm, 4)
                if g == 2:
                    act.wait_ge(pv_done, UNITS)
                for q in range(4):
                    n = 2 + 6 * g + q
                    dst = (qt if q < 2 else kt)[g % 2][:, q % 2, :].rearrange("p (r l) -> p r l", r=n_res)
                    for hf in range(2):
                        take(dst[:, :, hf * length // 2:(hf + 1) * length // 2],
                             lambda b: b[:, :].rearrange("p (l r) -> p r l", r=n_res),
                             -DH ** -0.5 if q < 2 else 1.0)
                        yield
                    upper_slot(n + 2, n + 2)
                for j, (_, rows) in enumerate(v_tiles(g)):
                    dst = vt[0][SPAN * (j % 2):SPAN * (j % 2) + rows, j // 2, :] if g == 2 else vt[g][0:rows, j, :]
                    take(dst, lambda b: b[0:rows, 0:4 * DH])
                    yield
                for n in (8 + 6 * g, 9 + 6 * g):
                    if n < IN_PIECES:
                        upper_slot(n, n)
                yield

            for _ in projections(0):
                pass
            for g in range(1, GROUPS):
                work = projections(g)
                for k in range(UNITS):
                    exps(g - 1, k)
                    for _ in range(2):
                        next(work, None)
                for _ in work:
                    pass
            for k in range(UNITS):
                exps(GROUPS - 1, k)

            act.wait_ge(pv_done, GROUPS * UNITS)
            act.wait_ge(pj_done, PJ_IN)
            for c in range(2):
                for hf in range(2):
                    act.wait_ge(pool_ev, 4)
                    cols = slice(hf * HALF, (hf + 1) * HALF)
                    nc.scalar.activation(h_hi[:, c, cols], pmix[:, c, cols], ACT.Copy).then_inc(mx_hi, 1)
            act.wait_ge(al_st, 3)
            nc.scalar.activation(lt[:, 0, :, :], lt[:, 0, :, :], ACT.Exp).then_inc(al_e, 1)
            for n in range(4 * GROUPS):
                act.wait_ge(bc_mul, n + 1)
                cols = slice(n % 2 * HALF, (n % 2 + 1) * HALF)
                nc.scalar.activation(h_hi[:, 2 + n // 2, cols], ot[:, n // 2, cols], ACT.Copy).then_inc(mx_hi, 1)
            act.wait_ge(bc_done, 4 * GROUPS)
            for n in range(OUT_PIECES):
                upper(W_OUT0 + n, wo_hi[:, n, :])
            upper_slot(W_Q0, IN_PIECES)
            upper_slot(W_Q0 + 1, IN_PIECES + 1)
            for i in range(NT):
                act.wait_ge(x1_done, 2 * i + 2)
                norm_stats(1, i)
                if i:
                    norm_upper(1, i - 1)
            norm_upper(1, NT - 1)

            def take_query(hp):
                if hp >= 2:
                    act.wait_ge(sc_done, 2 * (hp - 1))
                if hp == 0:
                    act.wait_ge(op_done, 2 * NT)
                for hf in range(2):
                    take(q2[:, hp % 2, hf * HALF:(hf + 1) * HALF], lambda b: b[:, :])

            for hp in range(Q_PIECES):
                take_query(hp)
                m = IN_PIECES + hp + 2
                upper_slot(W_Q0 + hp + 2, m)

            def chunk(it, s, first, ahead):
                if not first:
                    act.wait_ge(act_out[s], it * 16)
                for hf in range(2):
                    act.wait_ge(m1_done, it * 4 + (2 * s + hf + 1))
                    nc.scalar.activation(act_st[:, s, hf * MH:(hf + 1) * MH], bank[2 * s + hf][:, 0:MH],
                                         ACT.Gelu).then_inc(act_done, 1)
                if ahead:
                    act.wait_ge(raw_in[s], it * 16 + 16 * (W_U0 // 2 + 2))
                    nc.scalar.activation(w_hi[:, s, :], w_raw[:, s, :], ACT.Copy).then_inc(hi_done, 1)

            for s in range(2):
                chunk(0, s, True, True)
            with act.Fori(1, EXP_BODY) as it:
                for s in range(2):
                    chunk(it, s, False, True)
            act.wait_ge(g_ask, NT)
            nc.scalar.activation(route[:, 2, :, :], route[:, 2, :, :], ACT.Exp).then_inc(g_e, 1)
            with act.Fori(EXP_BODY, B0) as it:
                for s in range(2):
                    chunk(it, s, False, True)

            def strip(it, s2, first):
                if not first:
                    act.wait_ge(g_out[s2], it * 16)
                for s in range(2):
                    for q in range(4):
                        n = 4 * s + q
                        act.wait_ge(gp_done, it * 16 + (8 * s2 + n + 1))
                        nc.scalar.activation(g_st[:, s2, :, 4 * n:4 * n + 4],
                                             bank[4 + n % 2][:, :].rearrange("p (t j) -> p j t", t=4),
                                             ACT.Copy).then_inc(gs_done, 1)
                    chunk(it * 2 + (B0 + s2), s, False, True)

            strip(0, 0, True)
            strip(0, 1, True)
            with act.Fori(1, STRIPS // 2) as it:
                for s2 in range(2):
                    strip(it, s2, False)
            for s in range(2):
                chunk(C0, s, False, True)
            act.wait_ge(uh_cp, U_STEPS)
            nc.scalar.activation(uh[:, :], uh[:, :], ACT.Gelu).then_inc(uh_act, 1)
            with act.Fori(C0 + 1, BODIES - 1) as it:
                for s in range(2):
                    chunk(it, s, False, True)
            for s in range(2):
                chunk(BODIES - 1, s, False, False)

            def upper_v(hf, it, s, j, first):
                n = hf * NK + VJ * s + j
                if j == 0:
                    act.wait_ge(v_in[s], it * 16 + (hf * 8 * (NK // VJ) + 16))
                if not first:
                    act.wait_ge(m2_done, it * (2 * VJ) + (n - VJ + 1))
                nc.scalar.activation(v_hi[:, j, :], v_raw[:, s, j, :], ACT.Copy).then_inc(vh_done, 1)
                act.wait_ge(pd_done, it * (2 * VJ) + (n + 1))
                n = HT[hf] * P
                nc.scalar.activation(a_hi[:, j, 0:n], prod[:, j % 2, 0:n], ACT.Copy).then_inc(ah_done, 1)

            for hf in range(2):
                for s in range(2):
                    for j in range(VJ):
                        upper_v(hf, 0, s, j, hf == 0 and s == 0)
                with act.Fori(1, NG2) as it:
                    for s in range(2):
                        for j in range(VJ):
                            upper_v(hf, it, s, j, False)
            for i in range(NT):
                if i < DT:
                    act.wait_ge(y_done, 2 * (i + 1))
                else:
                    act.wait_ge(row_used, 2 * P)
                if i >= 2:
                    act.wait_ge(y_out[i % 2], 16 * (i // 2))
                nc.scalar.activation(yo[:, i % 2, :], y[:, i, :] if i < DT else ya[:, :], ACT.Square,
                                     accum_out=ss[:, 2, i:i + 1]).then_inc(ss_done, 1)
                act.wait_ge(rs_done, 2 * (2 * NT + i) + 1)
                nc.scalar.activation(std[:, 2, i:i + 1], rstd[:, 2, i:i + 1], ACT.Sqrt).then_inc(std_done, 1)

        @block.vector
        def _(dve):
            V = nc.vector

            def norm_scale(k, i, src, dst, done):
                n = k * NT + i
                dve.wait_ge(ss_done, n + 1)
                V.tensor_scalar(rstd[:, k, i:i + 1], ss[:, k, i:i + 1], 1.0 / D, EPS, ALU.mult,
                                ALU.add).then_inc(rs_done, 1)
                dve.wait_ge(std_done, n + 1)
                V.reciprocal(rstd[:, k, i:i + 1], std[:, k, i:i + 1]).then_inc(rs_done, 1)
                dve.wait_ge(rs_done, 2 * n + 2)
                V.scalar_tensor_tensor(out=dst, in0=src, scalar=rstd[:, k, i:i + 1], in1=gain[:, :],
                                       op0=ALU.mult, op1=ALU.mult).then_inc(done, 1)

            def norm_lower(k, i):
                for c in range(2):
                    n = k * LO_BANKS + 2 * i + c
                    dve.wait_ge(hh_done, n + 1)
                    cols = slice(i * P, (i + 1) * P)
                    V.tensor_tensor(h_lo[:, 4 * c:4 * c + 4, cols],
                                    bank[(4 if k else 0) + (2 * i + c) % 4][:, :].rearrange("p (k t) -> p k t", k=4),
                                    h_hi[:, 4 * c:4 * c + 4, cols], ALU.subtract).then_inc(hl_done, 1)

            dve.wait_ge(gain_in, 16)
            for i in range(NT):
                norm_scale(0, i, xs[:, i, :], xn[:, i % 2, :], xn_done)
                if i:
                    norm_lower(0, i - 1)
            norm_lower(0, NT - 1)

            V.memset(pp[:, :, :], 0.0).then_inc(pool_pad, 1)
            st = [0]

            def step(ins, sem_=pool_st, count=st):
                ins.then_inc(sem_, 1)
                count[0] += 1
                dve.wait_ge(sem_, count[0])

            dve.wait_ge(cst_in, 16 * 7)
            for c in range(2):
                dve.wait_ge(pj_free, 2 * c + 2)
                n1, n2, n4, n8 = PADW - 1, PADW - 3, PADW - 7, PADW - 15
                step(V.tensor_tensor(pb_[:, 0:n1], pp[:, c, 0:n1], pp[:, c, 1:n1 + 1], ALU.add))
                if c == 0:
                    step(V.tensor_tensor(pa[64:128, 0, 0:n2], pb_[64:128, 0:n2], pb_[64:128, 2:n2 + 2], ALU.add))
                    parts = ((0, 64, pb_[0:64, 7:7 + S]), (64, 128, pa[64:128, 0, 6:6 + S]))
                else:
                    step(V.tensor_tensor(pa[:, 1, 0:n2], pb_[:, 0:n2], pb_[:, 2:n2 + 2], ALU.add))
                    step(V.tensor_tensor(pb_[:, 0:n4], pa[:, 1, 0:n4], pa[:, 1, 4:n4 + 4], ALU.add))
                    step(V.tensor_tensor(pa[64:128, 1, 0:n8], pb_[64:128, 0:n8], pb_[64:128, 8:n8 + 8], ALU.add))
                    parts = ((0, 64, pb_[0:64, 4:4 + S]), (64, 128, pa[64:128, 1, 0:S]))
                for a, b, sums in parts:
                    dst = pmix[a:b, c, :]
                    step(V.tensor_scalar(dst, sums, inv[a:b, c:c + 1], None, ALU.mult))
                    V.tensor_tensor(dst[:, 0:8], sums[:, 0:8], edge[a:b, c, 0:8], ALU.mult)
                    step(V.tensor_tensor(dst[:, S - 8:S], sums[:, S - 8:S], edge[a:b, c, 8:16], ALU.mult))
                    step(V.tensor_tensor(pa[a:b, c, 8:8 + S], dst, pp[a:b, c, 8:8 + S], ALU.subtract))
            for c in range(2):
                for hf in range(2):
                    n = 2 * c + hf
                    dve.wait_ge(pool_mm, n + 1)
                    V.tensor_scalar(pmix[:, c, hf * HALF:(hf + 1) * HALF], bank[6 + n % 2][:, :],
                                    pscale[:, c:c + 1], None, ALU.mult).then_inc(pool_ev, 1)

            def scores(g, k):
                n = g * UNITS + k
                c, b = k // NT, k % NT
                _, lo, w, _ = window(g, b)
                dve.wait_ge(qk_done, n + 1)
                if n >= 2:
                    dve.wait_ge(p_done, n - 1)
                for e in range(2):
                    table = bias2[:, 2 * c + e, :] if g == 2 else bias01[:, 4 * g + 2 * c + e, lo:lo + w]
                    V.tensor_tensor_reduce(sc[:, n % 2, e, lo:lo + w], bank[4 + e][:, 0:w],
                                           table, 1.0, FAR, ALU.add, ALU.min,
                                           stat_nm[:, g, b, 2 * c + e:2 * c + e + 1]).then_inc(s_done, 1)

            def probs_out(g, k):
                n = g * UNITS + k
                dve.wait_ge(pt_done, n + 1)
                if n >= 2:
                    dve.wait_ge(pv_done, n - 1)
                tiles = window(g, k % NT)[3]
                for j, (_, rows) in enumerate(tiles):
                    src = bank[6][0:rows, :].rearrange("p (e j q) -> p e j q", e=2, j=2)[:, :, j, :]
                    dst = pt[0:rows, n % 2, :, :].rearrange("p (e j) q -> p e j q", e=2)[:, :, j, :]
                    ins = V.tensor_copy(dst, src)
                ins.then_inc(pt_ev, 1)

            def attn_out(g, k):
                n = g * UNITS + k
                c, b = k // NT, k % NT
                dve.wait_ge(pv_done, n + 1)
                per = S // NRES[g]
                if per >= P:
                    dst = by_residue(ot[:, 2 * g + c, :], g, b * P // per, 1, b * P % per, P)
                else:
                    dst = by_residue(ot[:, 2 * g + c, :], g, b * P // per, P // per, 0, per)
                V.tensor_copy(dst, bank[7][:, 0:P].rearrange("p (r l) -> p r l", l=min(per, P))).then_inc(ot_ev, 1)

            def stats_out(g):
                for n in range(4):
                    m = 4 * g + n
                    hf = n % 2
                    dve.wait_ge(st_done, m + 1)
                    if m == 0:
                        dve.wait_ge(pv_done, GROUPS * UNITS)
                    row = lt[0:4, n // 2, g, :]
                    if g == 0:
                        dst, src = row[:, hf * HALF:(hf + 1) * HALF], bank[4 + n % 2][0:4, :]
                    else:
                        dst = by_residue(row, g, hf * NRES[g] // 2, NRES[g] // 2, 0, S // NRES[g])
                        src = bank[4 + n % 2][0:4, :].rearrange("p (r l) -> p r l", r=NRES[g] // 2)
                    V.tensor_copy(dst, src).then_inc(st_ev, 1)

            dve.wait_ge(bias_in, 32)
            for g in range(GROUPS):
                for k in range(UNITS + 2):
                    if k < UNITS:
                        scores(g, k)
                    if 1 <= k <= UNITS:
                        probs_out(g, k - 1)
                    if k >= 2:
                        attn_out(g, k - 2)
            for g in range(GROUPS):
                stats_out(g)

            al = [0]
            dve.wait_ge(st_ev, 4 * GROUPS)
            nm_t, den_t = lt[:, 0, :, :], lt[:, 1, :, :]
            step(V.tensor_tensor(mn[:, :], nm_t[:, 0, :], nm_t[:, 1, :], ALU.min), al_st, al)
            step(V.tensor_tensor(mn[:, :], mn[:, :], nm_t[:, 2, :], ALU.min), al_st, al)
            step(V.tensor_tensor(nm_t, mn[:, :].unsqueeze(1).broadcast_to([4, GROUPS, S]), nm_t, ALU.subtract), al_st, al)
            dve.wait_ge(al_e, 1)
            step(V.tensor_tensor(den_t, den_t, nm_t, ALU.mult), al_st, al)
            step(V.tensor_tensor(den[:, :], den_t[:, 0, :], den_t[:, 1, :], ALU.add), al_st, al)
            step(V.tensor_tensor(den[:, :], den[:, :], den_t[:, 2, :], ALU.add), al_st, al)
            step(V.reciprocal(mn[:, :], den[:, :]), al_st, al)
            step(V.tensor_tensor(nm_t, nm_t, mn[:, :].unsqueeze(1).broadcast_to([4, GROUPS, S]), ALU.mult), al_st, al)
            dve.wait_ge(ot_ev, GROUPS * UNITS)
            for n in range(4 * GROUPS):
                cols = slice(n % 2 * HALF, (n % 2 + 1) * HALF)
                dve.wait_ge(bc_done, n + 1)
                V.tensor_tensor(ot[:, n // 2, cols], ot[:, n // 2, cols], bank[n % 4][:, :],
                                ALU.mult).then_inc(bc_mul, 1)
            for c in range(2):
                for hf in range(2):
                    cols = slice(hf * HALF, (hf + 1) * HALF)
                    dve.wait_ge(mx_hi, 2 * c + hf + 1)
                    V.tensor_tensor(h_lo[:, c, cols], pmix[:, c, cols], h_hi[:, c, cols],
                                    ALU.subtract).then_inc(mx_lo, 1)
            for n in range(4 * GROUPS):
                cols = slice(n % 2 * HALF, (n % 2 + 1) * HALF)
                dve.wait_ge(mx_hi, 4 + n + 1)
                V.tensor_tensor(h_lo[:, 2 + n // 2, cols], ot[:, n // 2, cols], h_hi[:, 2 + n // 2, cols],
                                ALU.subtract).then_inc(mx_lo, 1)

            dve.wait_ge(gain_in, 32)
            for i in range(NT):
                dve.wait_ge(x_in[i], 32)
                for hf in range(2):
                    n = 2 * i + hf
                    dve.wait_ge(op_done, n + 1)
                    cols = slice(hf * HALF, (hf + 1) * HALF)
                    V.tensor_tensor(xs[:, i, cols], bank[n % 4][:, :], xs[:, i, cols], ALU.add).then_inc(x1_done, 1)
                norm_scale(1, i, xs[:, i, :], xn[:, i % 2, :], xn_done)
                if i:
                    norm_lower(1, i - 1)
            norm_lower(1, NT - 1)

            rs = [0]

            def group(instructions):
                for ins in instructions:
                    ins.then_inc(r_st, 1)
                    rs[0] += 1
                dve.wait_ge(r_st, rs[0])

            for hp in range(Q_PIECES):
                h, half = hp // 2, hp % 2
                for q in range(2):
                    n = 2 * hp + q
                    dve.wait_ge(sc_done, n + 1)
                    src = [bank[4 + n % 4][:, t * NK:(t + 1) * NK] for t in range(4)]
                    val = [top1[:, 4 * q + t, h, half, :] for t in range(4)]
                    idx = [ix1[:, 4 * q + t, h, half, :] for t in range(4)]
                    rest = [rep[:, t, 0:NK] for t in range(4)]
                    group([V.max(val[t][:, 0:8], src[t]) for t in range(4)])
                    group([V.match_replace(rest[t], val[t][:, 0:8], src[t], -FAR) for t in range(4)])
                    group([V.max(val[t][:, 8:16], rest[t]) for t in range(4)])
                    for t in range(4):
                        ins = V.max_index(idx[t][:, 0:8], val[t][:, 0:8], src[t])
                    ins.then_inc(sc_free, 1)
                    for t in range(4):
                        last = V.max_index(idx[t][:, 8:16], val[t][:, 8:16], rest[t])
                    group([last])

            for t in range(NT):
                one, two = top1[:, t, :, 0, :], top1[:, t, :, 1, :]
                shape = [P, PH, TOP, TOP]
                sums = cand[:, :, :].rearrange("p h (a b) -> p h a b", a=TOP)
                group([V.tensor_tensor(sums, one.unsqueeze(3).broadcast_to(shape),
                                       two.unsqueeze(2).broadcast_to(shape), ALU.add),
                       V.tensor_copy(ix1f[:, t, :, :, :], ix1[:, t, :, :, :])])
                group([V.max(top2[:, h, 0:8], cand[:, h, :]) for h in range(PH)])
                group([V.match_replace(rep[:, h, :], top2[:, h, 0:8], cand[:, h, :], -FAR) for h in range(PH)])
                group([V.max(top2[:, h, 8:16], rep[:, h, :]) for h in range(PH)])
                V.tensor_tensor(route[:, 2, t, :].rearrange("p (h k) -> p h k", h=PH), top2[:, :, :],
                                top2[:, :, 0:1].broadcast_to([P, PH, TOP]), ALU.subtract).then_inc(g_ask, 1)
                group([V.max_index(pos[:, 0, h, 0:8], top2[:, h, 0:8], cand[:, h, :]) for h in range(PH)]
                      + [V.max_index(pos[:, 0, h, 8:16], top2[:, h, 8:16], rep[:, h, :]) for h in range(PH)])
                group([V.tensor_scalar(pos[:, 1, :, :], pos[:, 0, :, :], TOP - 1, None, ALU.bitwise_and)])
                group([V.tensor_scalar(pos[:, 0, :, :], pos[:, 0, :, :], 4, None, ALU.logical_shift_right)])
                group([V.tensor_copy(posf[:, :, :, :], pos[:, :, :, :])])
                for half in range(2):
                    ranks = iota[:, 0:TOP].unsqueeze(1).unsqueeze(1).broadcast_to(shape)
                    group([V.tensor_tensor(eq[:, :, :, :], posf[:, half, :, :].unsqueeze(3).broadcast_to(shape),
                                           ranks, ALU.is_equal)])
                    group([V.tensor_tensor(eq[:, :, :, :], eq[:, :, :, :],
                                           ix1f[:, t, :, half, :].unsqueeze(2).broadcast_to(shape), ALU.mult)])
                    group([V.tensor_reduce(route[:, half, t, :].rearrange("p (h k) -> p h k", h=PH),
                                           eq[:, :, :, :], AX.X, ALU.add)])
            group([V.scalar_tensor_tensor(out=uh[:, :], in0=route[:, 1, DT, :], scalar=float(NK),
                                          in1=route[:, 0, DT, :], op0=ALU.mult, op1=ALU.add)])
            V.tensor_copy(ids[:, :], uh[:, :]).then_inc(ids_done, 1)
            dve.wait_ge(g_e, 1)
            gate = route[:, 2, :, :].rearrange("p t (h k) -> p t h k", h=PH)
            group([V.tensor_reduce(gsum[:, 0, :, :], gate, AX.X, ALU.add)])
            group([V.reciprocal(gsum[:, 1, :, :], gsum[:, 0, :, :])])
            V.tensor_tensor(gate, gate, gsum[:, 1, :, :].unsqueeze(3).broadcast_to([P, NT, PH, TOP]),
                            ALU.mult).then_inc(route_done, 1)

            def dots(it):
                for r in range(GR):
                    dve.wait_ge(row_in[r], it * 16 + 16)
                    V.tensor_tensor_reduce(rows[:, r, :], rows[:, r, :], xn[:, DT % 2, :], 1.0, 0.0, ALU.mult,
                                           ALU.add, uh4[:, r:r + 1]).then_inc(row_used, 1)
                dve.wait_ge(row_used, it * GR + GR)
                V.tensor_copy(uh[:, bass.ds(it * GR, GR)], uh4[:, :]).then_inc(uh_cp, 1)
                dve.wait_ge(uh_cp, it + 1)

            def add_rows(it):
                V.tensor_copy(w4[:, :], uh[:, bass.ds(it * GR, GR)]).then_inc(w4_cp, 1)
                dve.wait_ge(w4_cp, it + 1)
                for r in range(GR):
                    dve.wait_ge(row_in[r], it * 16 + 16 * (U_STEPS + 1))
                    V.scalar_tensor_tensor(out=ya[:, :], in0=rows[:, r, :], scalar=w4[:, r:r + 1], in1=ya[:, :],
                                           op0=ALU.mult, op1=ALU.add).then_inc(row_used, 1)
                    dve.wait_ge(row_used, it * GR + (GR * U_STEPS + r + 1))

            with dve.Fori(0, A2_BODIES) as it:
                dots(it)
            for n in range(6):
                w = HT[n % 2] * P
                dve.wait_ge(rt_done, n + 1)
                V.tensor_copy(route_t[:, n // 2, n % 2 * HALF:n % 2 * HALF + w], bank[4 + n % 4][:, 0:w]).then_inc(rt_ev, 1)
            dve.wait_ge(rt_ev, 6)

            def one_hots(it, s2, first):
                if not (isinstance(it, int) and it == 0):
                    dve.wait_ge(oh_done, it * 16 + (8 * s2 - 8))
                V.tensor_copy(strip_r[:, s2, :, :],
                              route_t[:, :, bass.ds(it * (2 * TW) + s2 * TW, TW)]).then_inc(oh_cp, 1)
                dve.wait_ge(oh_cp, it * 2 + (s2 + 1))
                for n in range(8):
                    if not (first and n < 2):
                        dve.wait_ge(gp_done, it * 16 + (8 * s2 + n - 1))
                    for k in range(4):
                        t = 4 * n + k
                        V.tensor_scalar(oneh[:, n % 2, 0, k, :], iota[:, :], strip_r[:, s2, 0, t:t + 1], None, ALU.is_equal)
                        ins = V.tensor_scalar(oneh[:, n % 2, 1, k, :], iota[:, :], strip_r[:, s2, 1, t:t + 1],
                                              strip_r[:, s2, 2, t:t + 1], ALU.is_equal, ALU.mult)
                    ins.then_inc(oh_done, 1)
                    if n == 3:
                        dots(it * 2 + (A2_BODIES + s2))

            one_hots(0, 0, True)
            one_hots(0, 1, False)
            with dve.Fori(1, STRIPS // 2) as it:
                for s2 in range(2):
                    one_hots(it, s2, False)
            dve.wait_ge(uh_act, 1)
            V.tensor_tensor(uh[:, :], uh[:, :], route[:, 2, DT, :], ALU.mult).then_inc(uh_gate, 1)
            dve.wait_ge(uh_gate, 1)
            dve.wait_ge(ya_in, 16)
            with dve.Fori(0, V_STEPS1) as it:
                add_rows(it)

            dve.wait_ge(m1_done, 2 * NK)
            V.memset(zero[:, :].bitcast(F32), 0.0).then_inc(z_set, 1)

            def gated(hf, it, s, j, first):
                n = hf * NK + VJ * s + j
                if j == 0:
                    dve.wait_ge(a_in[s], it * 16 + (hf * 8 * (NK // VJ) + 16))
                    dve.wait_ge(g_in[s], it * 16 + (hf * 8 * (NK // VJ) + 16))
                if not (first and j < 2):
                    dve.wait_ge(ah_done, it * (2 * VJ) + (n - 1))
                w = HT[hf] * P
                V.tensor_tensor(prod[:, j % 2, 0:w].rearrange("p (b t) -> p b t", t=TW),
                                a_raw[:, s, j, 0:w].rearrange("p (b t) -> p b t", t=TW),
                                g_raw[:, s, 0:w // TW, j * TW:(j + 1) * TW], ALU.mult).then_inc(pd_done, 1)

            def lower_a(hf, it, n, j):
                w = HT[hf] * P
                dve.wait_ge(ah_done, it * (2 * VJ) + (n + 1))
                V.tensor_tensor(a_lo[:, j, 0:w], prod[:, j % 2, 0:w], a_hi[:, j, 0:w],
                                ALU.subtract).then_inc(al_done, 1)

            def gated_group(hf, it, first):
                for s in range(2):
                    for j in range(VJ):
                        gated(hf, it, s, j, first and s == 0)
                        lower_a(hf, it, hf * NK + VJ * s + j, j)
                if hf == 0:
                    add_rows(it + V_STEPS1)

            def add_residual(hf):
                for n in range(2 * HT[hf]):
                    i, c = 4 * hf + n // 2, n % 2
                    cols = slice(c * HALF, (c + 1) * HALF)
                    V.tensor_tensor(y[:, i, cols], y[:, i, cols], bank[n][:, :], ALU.add).then_inc(y_done, 1)

            gated_group(0, 0, True)
            with dve.Fori(1, NG2) as it:
                gated_group(0, it, False)
            dve.wait_ge(y_in, 16)
            dve.wait_ge(m2_done, NK)
            add_residual(0)
            with dve.Fori(0, NG2) as it:
                gated_group(1, it, False)
            dve.wait_ge(gain_in, 48)
            for i in range(NT):
                if i == 4:
                    dve.wait_ge(m2_done, 2 * NK)
                    add_residual(1)
                norm_scale(2, i, y[:, i, :] if i < DT else ya[:, :], yo[:, i % 2, :], yo_done)

        @block.tensor
        def _(pe):
            def both_halves(lhs_hi, lhs_lo, banks, done, n=HALF, between=None):
                for k in range(KC):
                    part = slice(k * P, (k + 1) * P)
                    for lhs, rhs in ((lhs_hi, h_hi), (lhs_hi, h_lo), (lhs_lo, h_hi)):
                        for h in range(2):
                            ins = pe.matmul(banks[h][:, 0:n], lhs[:, part], rhs[:, k, h * n:(h + 1) * n],
                                            start=(k == 0 and lhs is lhs_hi and rhs is h_hi),
                                            stop=(k == KC - 1 and lhs is lhs_lo))
                            if k == KC - 1 and lhs is lhs_lo:
                                ins.then_inc(done, 1)
                    if between is not None:
                        between(k)

            def norm_turn(k, i):
                n0 = k * NT + i
                pe.wait_ge(xn_done, n0 + 1)
                for c in range(2):
                    n = k * LO_BANKS + 2 * i + c
                    if 2 * i + c >= 4:
                        pe.wait_ge(hl_done, n - 3)
                    for q in range(4):
                        kc = 4 * c + q
                        ins = pe.transpose(bank[(4 if k else 0) + (2 * i + c) % 4][:, q * P:(q + 1) * P],
                                           xn[:, i % 2, kc * P:(kc + 1) * P], ident[:, :])
                    ins.then_inc(xt_done, 1)

            pe.wait_ge(cst_in, 16 * 7)
            for i in range(NT):
                norm_turn(0, i)
            pe.wait_ge(hl_done, LO_BANKS)

            pj = [0]

            def project(n):
                pe.wait_ge(lo_done, n + 1)
                b = pj[0]
                if b >= 4:
                    pe.wait_ge(pj_free, b - 2)
                both_halves(w_hi[:, n % 2, :], w_lo[:, n % 2, :], [bank[b % 4], bank[(b + 1) % 4]], pj_done)
                pj[0] = b + 2

            def project_v(g, j):
                n = 6 + 6 * g
                first, rows = v_tiles(g)[j]
                per = S // NRES[g]
                b = pj[0]
                pe.wait_ge(lo_done, n + 2)
                pe.wait_ge(pj_free, b - 3)
                for k in range(KC):
                    rhs = [w[:, k // 4, :].rearrange("p (k n) -> p k n", k=4)[:, k % 4, :] for w in (w_hi, w_lo)]
                    lhs = []
                    for h in (h_hi, h_lo):
                        lhs.append(by_residue(h[:, k, :], g, first // per, 1, first % per, rows)[:, 0, :])
                    dst = bank[b % 4][0:rows, 0:4 * DH]
                    pe.matmul(dst, lhs[0], rhs[0], start=(k == 0), stop=False)
                    pe.matmul(dst, lhs[0], rhs[1], start=False, stop=False)
                    ins = pe.matmul(dst, lhs[1], rhs[0], start=False, stop=(k == KC - 1))
                ins.then_inc(pj_done, 1)
                pj[0] = b + 1

            def projection_step(g, k):
                if k < 4:
                    project(2 + 6 * g + k)
                else:
                    for j in range(2 * (k - 4), min(2 * (k - 4) + 2, len(v_tiles(g)))):
                        project_v(g, j)

            def qk(g, k):
                n = g * UNITS + k
                c, b = k // NT, k % NT
                k0, _, w, _ = window(g, b)
                if n:
                    pe.wait_ge(s_done, 2 * n)
                for e in range(2):
                    rows = slice(DH * e, DH * e + DH)
                    ins = pe.matmul(bank[4 + e][:, 0:w], qt[g % 2][rows, c, b * P:(b + 1) * P],
                                    kt[g % 2][rows, c, k0:k0 + w], start=True, stop=True)
                ins.then_inc(qk_done, 1)

            def turn(g, k):
                n = g * UNITS + k
                pe.wait_ge(p_done, n + 1)
                if n:
                    pe.wait_ge(pt_ev, n)
                _, lo, _, tiles = window(g, k % NT)
                for e in range(2):
                    for j, (_, rows) in enumerate(tiles):
                        c0 = lo if j == 0 else P
                        ins = pe.transpose(bank[6][0:rows, (2 * e + j) * P:(2 * e + j + 1) * P],
                                           pr[:, n % 2, e, c0:c0 + rows], ident[:, :])
                ins.then_inc(pt_done, 1)

            def pv(g, k):
                n = g * UNITS + k
                c = k // NT
                pe.wait_ge(pt_ev, n + 1)
                if n:
                    pe.wait_ge(ot_ev, n)
                tiles = window(g, k % NT)[3]
                for e in range(2):
                    for j, (tile, rows) in enumerate(tiles):
                        ins = pe.matmul(bank[7][DH * e:DH * e + DH, 0:P],
                                        vt[g % 2][0:rows, tile, (2 * c + e) * DH:(2 * c + e + 1) * DH],
                                        pt[0:rows, n % 2, 2 * e + j, :], start=(j == 0), stop=(j == len(tiles) - 1))
                ins.then_inc(pv_done, 1)

            project(0)
            project(1)
            for k in range(4 + (len(v_tiles(0)) + 1) // 2):
                projection_step(0, k)
            pool_steps = (8, 18)
            for c in range(2):
                pe.wait_ge(pool_st, pool_steps[c])
                for hf in range(2):
                    if c:
                        pe.wait_ge(pool_ev, hf + 1)
                    for a in (0, DH):
                        ins = pe.matmul(bank[6 + hf][a:a + DH, :], wpool[a:a + DH, c, :],
                                        pa[a:a + DH, c, 8 + hf * HALF:8 + (hf + 1) * HALF], start=True, stop=True)
                    ins.then_inc(pool_mm, 1)
            pe.wait_ge(pool_ev, 4)
            for g in range(GROUPS):
                pe.wait_ge(pj_free, PJ_G[g])
                qk(g, 0)
                for k in range(UNITS):
                    turn(g, k)
                    if k + 1 < UNITS:
                        qk(g, k + 1)
                    if k:
                        pv(g, k - 1)
                    if g + 1 < GROUPS and k < 4 + (len(v_tiles(g + 1)) + 1) // 2:
                        projection_step(g + 1, k)
                pv(g, UNITS - 1)

            for m in range(4 * GROUPS):
                g, n = m // 4, m % 4
                if m == 0:
                    pe.wait_ge(s_done, 2 * GROUPS * UNITS)
                if m >= 2:
                    pe.wait_ge(st_ev, m - 1)
                stat = (stat_nm, stat_den)[n // 2]
                for q in range(4):
                    ins = pe.transpose(bank[4 + n % 2][0:4, q * P:(q + 1) * P], stat[:, g, 4 * (n % 2) + q, :],
                                       ident[:, :])
                ins.then_inc(st_done, 1)
            pe.wait_ge(al_st, 8)
            for n in range(4 * GROUPS):
                if n >= 4:
                    pe.wait_ge(bc_mul, n - 3)
                g, c = n // 4, n // 2 % 2
                pe.matmul(bank[n % 4][:, :], sel[0:4, c, :], lt[0:4, 0, g, n % 2 * HALF:(n % 2 + 1) * HALF],
                          start=True, stop=True).then_inc(bc_done, 1)

            for i in range(NT):
                if i == 0:
                    pe.wait_ge(bc_mul, 4 * GROUPS)
                if i >= 2:
                    pe.wait_ge(x1_done, 2 * i - 2)
                toks = slice(i * P, (i + 1) * P)
                for k in range(KC):
                    if i == 0:
                        pe.wait_ge(mx_lo, 2 * k + 2)
                        pe.wait_ge(lo_done, W_OUT0 + k + 1)
                    for lhs, rhs in ((h_hi, wo_hi), (h_hi, wo_lo), (h_lo, wo_hi)):
                        for h in range(2):
                            ins = pe.matmul(bank[(2 * i + h) % 4][:, :], lhs[:, k, toks],
                                            rhs[:, k, h * HALF:(h + 1) * HALF], start=(k == 0 and rhs is wo_hi
                                                                                      and lhs is h_hi),
                                            stop=(k == KC - 1 and lhs is h_lo))
                            if k == KC - 1 and lhs is h_lo:
                                ins.then_inc(op_done, 1)
                if i:
                    norm_turn(1, i - 1)
            norm_turn(1, NT - 1)

            def key_scores(hp):
                pe.wait_ge(pj_free, PJ_IN + 2 * hp + 2)
                for q in range(2):
                    n = 2 * hp + q
                    if n >= 4:
                        pe.wait_ge(sc_free, n - 3)
                    for t in range(4):
                        ins = pe.matmul(bank[4 + n % 4][:, t * NK:(t + 1) * NK],
                                        q2[:, hp % 2, (4 * q + t) * P:(4 * q + t + 1) * P], sk[:, hp, :],
                                        start=True, stop=True)
                    ins.then_inc(sc_done, 1)

            pe.wait_ge(hl_done, 2 * LO_BANKS)
            pe.wait_ge(x1_done, 2 * NT)
            for hp in range(Q_PIECES):
                project(W_Q0 + hp)
                if hp == 0:
                    pe.wait_ge(sk_in, 16)
                else:
                    key_scores(hp - 1)
            key_scores(Q_PIECES - 1)

            def chunk(it, s, first, between=None):
                pe.wait_ge(lo_done, it * 2 + (W_U0 + s + 1))
                if first:
                    pe.wait_ge(pj_free, PJ_ALL)
                else:
                    pe.wait_ge(act_done, it * 4 + (2 * s - 2))
                both_halves(w_hi[:, s, :], w_lo[:, s, :], [bank[2 * s], bank[2 * s + 1]], m1_done, MH, between)

            for s in range(2):
                chunk(0, s, True)
            with pe.Fori(1, B0) as it:
                for s in range(2):
                    chunk(it, s, False)
            pe.wait_ge(route_done, 1)
            for n in range(6):
                if n >= 4:
                    pe.wait_ge(rt_ev, n - 3)
                for q in range(HT[n % 2]):
                    ins = pe.transpose(bank[4 + n % 4][:, q * P:(q + 1) * P], route[:, n // 2, 4 * (n % 2) + q, :],
                                       ident[:, :])
                ins.then_inc(rt_done, 1)

            def gates(it, s2, n, first):
                pe.wait_ge(oh_done, it * 16 + (8 * s2 + n + 1))
                if not (first and n < 2):
                    pe.wait_ge(gs_done, it * 16 + (8 * s2 + n - 1))
                for k in range(4):
                    ins = pe.matmul(bank[4 + n % 2][:, k * NK:(k + 1) * NK], oneh[:, n % 2, 0, k, :],
                                    oneh[:, n % 2, 1, k, :], start=True, stop=True)
                ins.then_inc(gp_done, 1)

            def strip(it, s2, first):
                for s in range(2):
                    def between(k):
                        if k % 2 == 0:
                            gates(it, s2, 4 * s + k // 2, first)
                    chunk(it * 2 + (B0 + s2), s, False, between)

            pe.wait_ge(rt_ev, 6)
            strip(0, 0, True)
            strip(0, 1, False)
            with pe.Fori(1, STRIPS // 2) as it:
                for s2 in range(2):
                    strip(it, s2, False)
            with pe.Fori(C0, BODIES) as it:
                for s in range(2):
                    chunk(it, s, False)

            def products(hf, it, s, j):
                n = hf * NK + VJ * s + j
                pe.wait_ge(vl_done, it * (2 * VJ) + (n + 1))
                pe.wait_ge(al_done, it * (2 * VJ) + (n + 1))
                for q in range(HT[hf]):
                    toks = slice(q * P, (q + 1) * P)
                    for lhs, rhs in ((a_hi, v_hi), (a_hi, v_lo), (a_lo, v_hi)):
                        for c in range(2):
                            ins = pe.matmul(bank[2 * q + c][:, :], lhs[:, j, toks],
                                            rhs[:, j, c * HALF:(c + 1) * HALF], start=False, stop=True,
                                            skip_group_check=True)
                ins.then_inc(m2_done, 1)

            pe.wait_ge(z_set, 1)
            pe.wait_ge(act_done, 2 * NK)
            pe.wait_ge(gs_done, 8 * STRIPS)
            for hf in range(2):
                for n in range(2 * HT[hf]):
                    if hf:
                        pe.wait_ge(y_done, n + 1)
                    pe.matmul(bank[n][:, :], zero[:, 0:P], zero[:, :], start=True, stop=True)
                with pe.Fori(0, NG2) as it:
                    for s in range(2):
                        for j in range(VJ):
                            products(hf, it, s, j)


def kernel(x, g_mix, w_in, w_pool, pool_scale, w_out, g_ffn, w_peer_q, peer_subkeys, peer_u, peer_v, g_final):
    import numpy as np
    import concourse.bacc as bacc
    from concourse.bass_utils import run_bass_kernel_spmd

    def arr(a):
        return np.ascontiguousarray(a)

    w_in = np.asarray(w_in)[0]
    def cols(c0):
        return w_in[:, c0:c0 + P].reshape(KC, P, P).transpose(1, 0, 2).reshape(P, 1024)

    pool_w, attn_w = 256, 768
    pieces = [cols(0), cols(P)]
    for g in range(GROUPS):
        for part in range(2):
            for c in range(2):
                pieces.append(cols(pool_w + part * attn_w + (2 * g + c) * P))
        wv = w_in[:, pool_w + 2 * attn_w + g * 256:pool_w + 2 * attn_w + (g + 1) * 256]
        for k in range(2):
            pieces.append(wv.reshape(2, 4, P, 256)[k].transpose(1, 0, 2).reshape(P, 1024))
    ins = {
        "x": arr(x),
        "g_mix": arr(g_mix),
        "w_in": np.stack(pieces),
        "w_pool": arr(np.asarray(w_pool)[0].reshape(2, 2 * DH, DH).transpose(1, 0, 2)),
        "pool_scale": arr(np.asarray(pool_scale)[0].reshape(2, P).T),
        "w_out": arr(np.asarray(w_out)[0].reshape(KC, P, D)),
        "g_ffn": arr(g_ffn),
        "w_q": arr(np.asarray(w_peer_q)[0].reshape(KC, P, Q_PIECES, P).transpose(2, 1, 0, 3)).reshape(Q_PIECES, P, 1024),
        "subkeys": arr(np.asarray(peer_subkeys)[0].reshape(Q_PIECES, NK, P).transpose(2, 0, 1)),
        "u": arr(np.asarray(peer_u)[0].reshape(NK, NK, KC, P).transpose(1, 3, 2, 0)).reshape(NK, P, 1024),
        "u_rows": arr(np.asarray(peer_u)[0].reshape(NK, NK, D).transpose(1, 0, 2)).reshape(NK * NK, D),
        "v": arr(np.asarray(peer_v)[0].reshape(NK, NK, D).transpose(1, 0, 2)),
        "g_final": arr(np.asarray(g_final).reshape(1, D)),
    }
    slopes = (2.0 ** (-8.0 * np.arange(1, 13) / 12)).astype(np.float32)
    q = np.arange(P)[:, None]
    rel = np.abs(np.arange(2 * P)[None, :] - SPAN - q)
    bias01 = np.stack([np.where(rel <= SPAN, slopes[h] * (DIL[h // 4] * rel).astype(np.float32), np.float32(1e30))
                       for h in range(8)], axis=1).astype(np.float32)
    k = np.arange(P)[None, :]
    bias2 = np.stack([np.where(q // 64 == k // 64, slopes[8 + h] * (DIL[2] * np.abs(q - k)).astype(np.float32),
                               np.float32(1e30)) for h in range(4)], axis=1).astype(np.float32)
    sel = np.zeros((4, 2, P), np.float32)
    for h in range(4):
        sel[h, h // 2, DH * (h % 2):DH * (h % 2) + DH] = 1.0
    edge = np.zeros((P, 2, 16), np.float32)
    inv = np.zeros((P, 2), np.float32)
    t = np.concatenate([np.arange(8), np.arange(S - 8, S)])
    for g, w in enumerate((2, 4, 8, 16)):
        rows = slice(DH * (g % 2), DH * (g % 2) + DH)
        n = np.clip(t + w // 2, 0, S) - np.clip(t - w // 2, 0, S)
        edge[rows, g // 2, :] = (1.0 / n).astype(np.float32)
        inv[rows, g // 2] = 1.0 / w
    ins |= {"ident_c": np.eye(P, dtype=np.float32),
            "iota_c": np.ascontiguousarray(np.broadcast_to(np.arange(P, dtype=np.float32), (P, P))),
            "bias01_c": arr(bias01), "bias2_c": arr(bias2), "sel_c": sel, "edge_c": edge, "inv_c": inv}

    nc = bacc.Bacc("TRN2", target_bir_lowering=False, num_devices=1)
    aps = {n: nc.dram_tensor(f"in_{n}", a.shape, mybir.dt.from_np(a.dtype), kind="ExternalInput").ap()
           for n, a in ins.items()}
    out = nc.dram_tensor("out", (1, S, D), F32, kind="ExternalOutput").ap()
    build(nc, out=out, **aps)
    r = run_bass_kernel_spmd(nc, [{f"in_{n}": a for n, a in ins.items()}], core_ids=[0])
    return r.results[0]["out"]
```

```python
import concourse.bass as bass
from concourse import mybir
from contextlib import ExitStack

F32 = mybir.dt.float32
F32R = mybir.dt.float32r
U32 = mybir.dt.uint32
ALU = mybir.AluOpType
ACT = mybir.ActivationFunctionType
AX = mybir.AxisListType

P = 128
D = 1024
S = 1024
KC = D // P
NT = S // P
HALF = 512
DH = 64
GROUPS = 3
DIL = (1, 4, 16)
NRES = DIL
SPAN = 64
EPS = 1e-6
PH = 8
TOP = 16
NK = 128
FAR = 3.0e38

IN_PIECES = 2 + 6 * GROUPS
OUT_PIECES = KC
Q_PIECES = 2 * PH
W_OUT0 = IN_PIECES
W_Q0 = W_OUT0 + OUT_PIECES
W_U0 = W_Q0 + Q_PIECES

DT = NT - 1
DS = DT * P
MH = DS // 2
HT = (4, DT - 4)
TW = 32
STRIPS = DS // TW
BODIES = NK // 2
GR = 4
U_STEPS = P // GR
A_BODIES = 16
EXP_BODY = 14
A2_BODIES = 4
B0 = A_BODIES + A2_BODIES
C0 = B0 + STRIPS
UC_FIRST = A2_BODIES + STRIPS // 2
UC_STEPS = U_STEPS - UC_FIRST
assert UC_STEPS < BODIES - C0
NG2 = NK // 8
assert U_STEPS == 2 * NG2
VJ = 4
QT = S // 4
WO_EARLY = 3
UNITS = 16


def v_tiles(g):
    if g == 2:
        return [(r * SPAN, SPAN) for r in range(NRES[2])]
    length = S // NRES[g]
    out = []
    for r in range(NRES[g]):
        for x in range(length // P + 1):
            lo, hi = max(x * P - SPAN, 0), min(x * P + SPAN, length)
            out.append((r * length + lo, hi - lo))
    return out


def window(g, b):
    if g == 2:
        return b * P, 0, P, [(b, P)]
    per = S // NRES[g] // P
    r, x = b // per, b % per
    lo = SPAN if x == 0 else 0
    hi = 2 * P - SPAN if x == per - 1 else 2 * P
    return b * P - SPAN + lo, lo, hi - lo, [(r * (per + 1) + x, P - lo), (r * (per + 1) + x + 1, hi - P)]


def by_residue(ap, g, r0, nr, l0, nl):
    n = NRES[g]
    return ap.rearrange("p (l r) -> p r l", r=n)[:, r0:r0 + nr, l0:l0 + nl]


def build(nc, x, g_mix, w_in, w_pool, pool_scale, w_out, g_ffn, w_q, subkeys, u, u_rows, v, g_final,
          ident_c, iota_c, bias01_c, bias2_c, sel_c, edge_c, inv_c, out):
    ctx = ExitStack()
    with ctx:
        base = (nc.sbuf_base + 63) // 64 * 64

        def at(name, kb, shape, dt=F32):
            return nc.alloc_sbuf_tensor_at(name, shape, dt, offset=base + int(kb * 1024))

        def sem(name):
            return ctx.enter_context(nc.semaphore(name))

        h_hi = at("h_hi", 0, [P, KC, S], F32R)
        h_lo = at("h_lo", 32, [P, KC, S], F32R)
        xs = at("xs", 64, [P, NT, D])
        ot = at("ot", 64, [P, 2 * GROUPS, S])
        pmix = at("pmix", 88, [P, 2, S])
        w_raw = at("w_raw", 96, [P, 2, 1024])
        w_hi = at("w_hi", 104, [P, 2, 1024], F32R)
        w_lo = at("w_lo", 112, [P, 2, 1024], F32R)
        gain = at("gain", 120, [P, D])
        ident = at("ident", 124, [P, P])
        iota = at("iota", 124.5, [P, P])
        stats = at("stats", 125, [P, 2, GROUPS, NT * 4 + 28])
        stat_nm, stat_den = [stats[:, k, :, 0:NT * 4].rearrange("p g (b h) -> p g b h", b=NT) for k in range(2)]
        ss = at("ss", 126.5, [P, 3, NT])
        std = at("std", 126.625, [P, 3, NT])
        rstd = at("rstd", 126.75, [P, 3, NT])
        wpool = at("wpool", 127.125, [P, 2, DH])
        pscale = at("pscale", 127.625, [P, 2])
        edge = at("edge", 127.6875, [P, 2, 16])
        inv = at("inv", 127.8125, [P, 2])
        xn = at("xn", 128, [P, 2, D])
        bias01 = at("bias01", 128, [P, 8, 2 * P])
        bias2 = at("bias2", 136, [P, 4, P])
        qt = [at(f"qt{s}", 138 + 28 * s, [P, 2, S]) for s in range(2)]
        kt = [at(f"kt{s}", 146 + 28 * s, [P, 2, S]) for s in range(2)]
        vt = [at(f"vt{s}", 154 + 28 * s, [P, 12, 4 * DH]) for s in range(2)]
        sc = at("sc", 194, [P, 2, 2, 2 * P])
        pr = at("pr", 198, [P, 2, 2, 2 * P])
        pt = at("pt", 202, [P, 2, 4, P])
        PADW = S + 16
        pp = at("pp", 166, [P, 2, PADW])
        pa = at("pa", 174.125, [P, 2, PADW])
        pb_ = at("pb_", 182.25, [P, PADW])
        lt = at("lt", 104, [P, 2, GROUPS, QT])
        mn = at("mn", 110, [P, 2, QT])
        sel = at("sel", 128, [P, 4, 2, P])
        wo = [at(f"wo{k}", base, [P, 2, D], F32R) for k, base in enumerate((166, 174, 182, 142, 150, 158, 190, 198))]
        squares = at("squares", 138, [P, D])
        sk = at("sk", 138, [P, 2 * PH, NK])
        q2 = at("q2", 146, [P, 2, S])
        top1 = at("top1", 154, [P, NT, PH, 2, TOP])
        ix1 = at("ix1", 162, [P, NT, PH, 2, TOP], U32)
        ix1f = at("ix1f", 170, [P, NT, PH, 2, TOP])
        cand = at("cand", 178, [P, PH, TOP * TOP])
        eq = at("eq", 186, [P, PH, TOP, TOP])
        rep = at("rep", 194, [P, 8, 2 * P])
        pos = at("pos", 202, [P, 2, PH, TOP], U32)
        posf = at("posf", 203, [P, 2, PH, TOP])
        top2 = at("top2", 204, [P, PH, TOP])
        gsum = at("gsum", 204.5, [P, 2, NT, PH])
        act_st = at("act_st", 64, [P, 2, DS])
        route = at("route", 72, [P, 3, NT, P])
        is_i = at("is_i", 84, [P, 2, 4, P], F32R)
        gate_j = at("gate_j", 88, [P, 2, 4, 2, P], F32R)
        g_st = at("g_st", 138, [P, 2, NK, TW])
        route_t = at("route_t", 170, [P, 4, DS])
        rows = at("rows", 184, [P, GR, D])
        ya = at("ya", 200, [P, D])
        is_j = at("is_j", 200, [P, 2, 4, P])
        ids = at("ids", 205, [P, P], U32)
        uh = at("uh", 205.5, [P, P])
        ids4 = at("ids4", 206, [P, GR], U32)
        uh4 = at("uh4", 206.125, [P, GR])
        gate4 = at("gate4", 206.25, [P, GR])
        strip_r = at("strip_r", 206.5, [P, 2, 4, TW])
        v_raw = [at(f"v_raw{s}", base, [P, VJ, D]) for s, base in enumerate((138, 0))]
        a_raw = [at(f"a_raw{s}", base, [P, VJ, HALF]) for s, base in enumerate((154, 16))]
        g_raw = [at(f"g_raw{s}", base, [P, HALF // TW, VJ * TW]) for s, base in enumerate((162, 24))]
        v_hi = at("v_hi", 32, [P, VJ, D], F32R)
        v_lo = at("v_lo", 48, [P, VJ, D], F32R)
        a_hi = at("a_hi", 96, [P, VJ, HALF], F32R)
        a_lo = at("a_lo", 104, [P, VJ, HALF], F32R)
        prod = at("prod", 112, [P, 2, HALF])
        zero = at("zero", 94, [P, HALF], F32R)
        y = at("y", 64, [P, DT, D])
        yo = at("yo", 184, [P, 4, D])

        bank = [ctx.enter_context(nc.psum_tensor(f"bank{k}", [P, HALF], F32)) for k in range(8)]

        act_d = nc.dram_tensor("act_d", [NK, P, DS], F32).ap()
        g_d = nc.dram_tensor("g_d", [STRIPS, P, NK, TW], F32).ap()
        x1_d = nc.dram_tensor("x1_d", [NT, P, D], F32).ap()

        cst_in = sem("cst_in")
        bias_in = sem("bias_in")
        sel_in = sem("sel_in")
        stat_pad = sem("stat_pad")
        gain_in = sem("gain_in")
        x_in = [sem(f"x_in{i}") for i in range(NT)]
        sk_in = sem("sk_in")
        raw_in = [sem("raw_in0"), sem("raw_in1")]
        hi_done = sem("hi_done")
        lo_done = sem("lo_done")
        ss_done = sem("ss_done")
        std_done = sem("std_done")
        rs_done = sem("rs_done")
        xn_done = sem("xn_done")
        xt_done = sem("xt_done")
        hh_done = sem("hh_done")
        hl_done = sem("hl_done")
        pj_done = sem("pj_done")
        pj_free = sem("pj_free")
        pool_pad = sem("pool_pad")
        pool_st = sem("pool_st")
        pool_mm = sem("pool_mm")
        pool_ev = sem("pool_ev")
        qk_done = sem("qk_done")
        s_done = sem("s_done")
        p_done = sem("p_done")
        pt_done = sem("pt_done")
        pt_ev = sem("pt_ev")
        pv_done = sem("pv_done")
        ot_ev = sem("ot_ev")
        st_done = sem("st_done")
        st_ev = sem("st_ev")
        al_st = sem("al_st")
        al_e = sem("al_e")
        bc_done = sem("bc_done")
        bc_mul = sem("bc_mul")
        mx_hi = sem("mx_hi")
        mx_lo = sem("mx_lo")
        op_done = sem("op_done")
        x1_done = sem("x1_done")
        x1_out = sem("x1_out")
        sc_done = sem("sc_done")
        sc_free = sem("sc_free")
        r_st = sem("r_st")
        g_e = sem("g_e")
        g_ask = sem("g_ask")
        route_done = sem("route_done")
        m1_done = sem("m1_done")
        act_done = sem("act_done")
        act_out = [sem("act_out0"), sem("act_out1")]
        rt_done = sem("rt_done")
        rt_ev = sem("rt_ev")
        rt_hi = sem("rt_hi")
        oh_cp = sem("oh_cp")
        isj_done = sem("isj_done")
        oh_done = sem("oh_done")
        ohh_done = sem("ohh_done")
        ohl_done = sem("ohl_done")
        gp_done = sem("gp_done")
        gsh_done = sem("gsh_done")
        gs_done = sem("gs_done")
        g_out = [sem("g_out0"), sem("g_out1")]
        ids_done = sem("ids_done")
        ids_cp = sem("ids_cp")
        row_in = [sem(f"row_in{r}") for r in range(GR)]
        row_used = sem("row_used")
        uh_cp = sem("uh_cp")
        uh_act = sem("uh_act")
        uh_gate = sem("uh_gate")
        gate4_cp = sem("gate4_cp")
        ya_in = sem("ya_in")
        v_in = [sem("v_in0"), sem("v_in1")]
        a_in = [sem("a_in0"), sem("a_in1")]
        g_in = [sem("g_in0"), sem("g_in1")]
        y_in = sem("y_in")
        z_set = sem("z_set")
        vh_done = sem("vh_done")
        vl_done = sem("vl_done")
        pd_done = sem("pd_done")
        ah_done = sem("ah_done")
        al_done = sem("al_done")
        m2_done = sem("m2_done")
        tile_done = sem("tile_done")
        y_done = sem("y_done")
        yo_done = sem("yo_done")
        y_out = [sem(f"y_out{k}") for k in range(4)]

        block = ctx.enter_context(nc.Block())
        win_d, wout_d, wq_d, u_d = w_in, w_out, w_q, u
        v_rows = v.rearrange("j i d -> (j i) d")
        out_t = out.rearrange("a (t p) d -> (a t) p d", p=P)
        x_t = x.rearrange("a (t p) d -> (a t) p d", p=P)

        def bcast_row(row):
            return bass.AP(tensor=row.tensor, offset=row.offset, ap=[[0, P]] + [list(a) for a in row.ap[-1:]])

        PIECE_BANKS = [2, 4]
        for g in range(GROUPS):
            for _ in range(4):
                PIECE_BANKS.append(PIECE_BANKS[-1] + 2)
            PIECE_BANKS += [PIECE_BANKS[-1] + len(v_tiles(g))] * 2
        PJ_G = [PIECE_BANKS[2 + 6 * g + 5] for g in range(GROUPS)]
        PJ_IN = PIECE_BANKS[-1]
        for _ in range(Q_PIECES):
            PIECE_BANKS.append(PIECE_BANKS[-1] + 2)
        PJ_ALL = PIECE_BANKS[-1]

        def four(row, s2, n):
            return strip_r[:, s2, row, 4 * n:4 * n + 4].unsqueeze(2).broadcast_to([P, 4, P])

        def gate_banks(n, pair):
            return bank[4 + 2 * (n % 2) + pair][:, :].rearrange("p (t part j) -> p part j t", t=2, part=2)

        def parts_by(g, k):
            n = 8 + len(v_tiles(g))
            m = n * (k + 2) // UNITS
            return 8 if m > 8 > n * (k + 1) // UNITS else min(m, n)

        LOWER_AT = (1, 3)
        FINAL = [*range(HT[0]), DT, *range(HT[0], DT)]
        AL_LESS, AL_ALL = 4, 12

        def score_bank(n):
            return 0 if n >= (GROUPS - 1) * UNITS and n % 2 else 4

        def stat_place(kind, g):
            return (2 + kind, g * QT) if g < GROUPS - 1 else (4 + kind, 0)

        LO_BANKS = 2 * NT

        @block.sync
        def _(sp):
            for i in range(NT):
                sp.dma_start(xs[:, i, :], x_t[i]).then_inc(x_in[i], 16)
                if i == 0:
                    sp.dma_start(gain[:, :], bcast_row(g_mix)).then_inc(gain_in, 16)
                if i == 1:
                    consts = ((ident[:, :], ident_c), (iota[:, :], iota_c),
                              (wpool[:, :, :], w_pool), (pscale[:, :], pool_scale), (edge[:, :, :], edge_c),
                              (inv[:, :], inv_c))
                    for dst, src in consts:
                        sp.dma_start(dst, src).then_inc(cst_in, 16)

            def load_piece(n, src):
                if n >= 2:
                    sp.wait_ge(lo_done, n - 1)
                sp.dma_start(w_raw[:, n % 2, :], src).then_inc(raw_in[n % 2], 16)

            for n in range(IN_PIECES):
                load_piece(n, win_d[n])
                if n == 2:
                    sp.wait_ge(xt_done, LO_BANKS)
                    sp.dma_start(bias01[:, :, :], bias01_c).then_inc(bias_in, 16)
                    sp.dma_start(bias2[:, :, :], bias2_c).then_inc(bias_in, 16)
                    sp.dma_start(gain[:, :], bcast_row(g_ffn)).then_inc(gain_in, 16)
            for n in range(OUT_PIECES):
                load_piece(W_OUT0 + n, wout_d[n])
                if n == 1:
                    sp.wait_ge(s_done, 2 * 2 * UNITS)
                    sp.dma_start(sel[:, :, :, :], sel_c).then_inc(sel_in, 16)
            sp.wait_ge(mx_lo, 2 * GROUPS * 2 + 4)
            for i in range(NT):
                sp.dma_start(xs[:, i, :], x_t[i]).then_inc(x_in[i], 16)
                if i < 2:
                    load_piece(W_Q0 + i, wq_d[i])
            for i in range(NT):
                sp.wait_ge(x1_done, 2 * i + 2)
                sp.dma_start(x1_d[i], xs[:, i, :]).then_inc(x1_out, 16)
            sp.wait_ge(op_done, 2 * NT)
            sp.wait_ge(ss_done, 2 * NT)
            sp.dma_start(sk[:, :, :], subkeys).then_inc(sk_in, 16)
            sp.wait_ge(xn_done, 2 * NT)
            sp.dma_start(gain[:, :], bcast_row(g_final)).then_inc(gain_in, 16)
            for n in range(2, Q_PIECES):
                load_piece(W_Q0 + n, wq_d[n])
            load_piece(W_U0, u_d[0])
            load_piece(W_U0 + 1, u_d[1])

            def first_half(it, last=False):
                for s in range(2):
                    if not last:
                        sp.wait_ge(lo_done, it * 2 + (W_U0 + s + 1))
                        sp.dma_start(w_raw[:, s, :], u_d[it * 2 + (2 + s)]).then_inc(raw_in[s], 16)
                    sp.wait_ge(act_done, it * 4 + (2 * s + 2))
                    sp.dma_start(act_d[it * 2 + s], act_st[:, s, :]).then_inc(act_out[s], 16)

            with sp.Fori(0, B0) as it:
                first_half(it)
            with sp.Fori(0, STRIPS // 2) as it:
                for s2 in range(2):
                    first_half(it * 2 + (B0 + s2))
                    sp.wait_ge(gs_done, it * 16 + (8 * s2 + 8))
                    sp.dma_start(g_d[it * 2 + s2], g_st[:, s2, :, :]).then_inc(g_out[s2], 16)

            def load_v(it, s):
                sp.dma_start(v_raw[s][:, :, :], v[bass.ds(it * (2 * VJ) + VJ * s, VJ), :, :]
                             .rearrange("j p d -> p j d")).then_inc(v_in[s], 16)

            def load_a(hf, it, s):
                t0, n = hf * HALF, HT[hf] * P
                sp.dma_start(a_raw[s][:, :, 0:n],
                             act_d[bass.ds(it * (2 * VJ) + VJ * s, VJ), :, t0:t0 + n]
                             .rearrange("j p t -> p j t")).then_inc(a_in[s], 16)

            def load_g(hf, it, s):
                t0, n = hf * HALF, HT[hf] * P
                sp.dma_start(g_raw[s][:, 0:n // TW, :],
                             g_d[t0 // TW:(t0 + n) // TW, :, bass.ds(it * (2 * VJ) + VJ * s, VJ), :]
                             .rearrange("b p j t -> p b (j t)")).then_inc(g_in[s], 16)

            def loads(hf, it, s):
                load_v(it, s)
                load_a(hf, it, s)
                load_g(hf, it, s)

            sp.wait_ge(x1_out, 16 * NT)
            for s in range(2):
                sp.wait_ge(g_out[s], 16 * STRIPS // 2)
                sp.wait_ge(act_out[s], 16 * VJ // 2)
            for k in range(3):
                first_half(C0 + k)
                if k == 0:
                    load_v(0, 0)
                elif k == 1:
                    load_a(0, 0, 0)
                else:
                    load_g(0, 0, 0)
            sp.dma_start(ya[:, :], x1_d[DT]).then_inc(ya_in, 16)
            with sp.Fori(C0 + 3, BODIES - 1) as it:
                first_half(it)
            first_half(BODIES - 1, last=True)

            for s in range(2):
                sp.wait_ge(act_out[s], 16 * NK // 2)
            sp.wait_ge(m1_done, 2 * NK)

            def free_raw(hf, it, s):
                sp.wait_ge(vl_done, it * (2 * VJ) + (hf * NK + VJ * s - VJ))
                sp.wait_ge(pd_done, it * (2 * VJ) + (hf * NK + VJ * s - VJ))

            for hf in range(2):
                for s in range(2):
                    if hf:
                        free_raw(hf, 0, s)
                    if hf or s:
                        loads(hf, 0, s)
                if hf == 0:
                    sp.wait_ge(uh_gate, 1)
                    sp.dma_start(y[:, 0:DT, :], x1_d[0:DT].rearrange("t p d -> p t d")).then_inc(y_in, 16)
                with sp.Fori(1, NG2) as it:
                    for s in range(2):
                        free_raw(hf, it, s)
                        loads(hf, it, s)
            for n, i in enumerate(FINAL):
                sp.wait_ge(yo_done, n + 1)
                sp.dma_start(out_t[i], yo[:, n % 4, :]).then_inc(y_out[n % 4], 16)
            for k in range(4):
                sp.wait_ge(y_out[k], 16 * NT // 4)

        @block.gpsimd
        def _(pool):
            def lower(n, dst, hi):
                pool.wait_ge(hi_done, n + 1)
                nc.gpsimd.tensor_tensor(dst, w_raw[:, n % 2, :], hi, ALU.subtract).then_inc(lo_done, 1)

            for n in range(IN_PIECES):
                lower(n, w_lo[:, n % 2, :], w_hi[:, n % 2, :])
            for n in range(OUT_PIECES):
                lower(W_OUT0 + n, wo[n][:, 1, :], wo[n][:, 0, :])
            for n in range(Q_PIECES):
                lower(W_Q0 + n, w_lo[:, n % 2, :], w_hi[:, n % 2, :])

            def lower_u(it, s):
                pool.wait_ge(hi_done, it * 2 + (W_U0 + s + 1))
                nc.gpsimd.tensor_tensor(w_lo[:, s, :], w_raw[:, s, :], w_hi[:, s, :],
                                        ALU.subtract).then_inc(lo_done, 1)

            def lower_half(it, s, half):
                if half == 0:
                    pool.wait_ge(hi_done, it * 2 + (W_U0 + s + 1))
                cols = slice(half * HALF, (half + 1) * HALF)
                ins = nc.gpsimd.tensor_tensor(w_lo[:, s, cols], w_raw[:, s, cols], w_hi[:, s, cols], ALU.subtract)
                if half:
                    ins.then_inc(lo_done, 1)

            def next_ids(it, step0, first=False):
                if first:
                    pool.wait_ge(ids_done, 1)
                else:
                    pool.wait_ge(row_used, it * GR + GR * step0)
                nc.gpsimd.tensor_copy(ids4[:, :], ids[:, bass.ds(it * GR, GR)]).then_inc(ids_cp, 1)
                pool.wait_ge(ids_cp, it + (step0 + 1))

            def gather_row(table, r):
                nc.gpsimd.indirect_dma_start(rows[:, r, :], None, table,
                                             bass.IndirectOffsetOnAxis(ids4[:, r:r + 1], 0)).then_inc(row_in[r], 16)

            def gather(table):
                for r in range(GR):
                    gather_row(table, r)

            with pool.Fori(0, A_BODIES) as it:
                for s in range(2):
                    lower_u(it, s)
            next_ids(0, 0, first=True)
            lower_u(A_BODIES, 0)
            gather(u_rows)
            lower_u(A_BODIES, 1)

            def gathering_body(it, step):
                next_ids(step, 0)
                lower_u(it, 0)
                gather(u_rows)
                lower_u(it, 1)

            with pool.Fori(1, A2_BODIES) as it:
                gathering_body(it + A_BODIES, it)

            def gates_lower(it, m, first):
                s2, n = m // 8, m % 8
                pool.wait_ge(isj_done, it * 16 + (m + 1))
                if not (first and m < 2):
                    pool.wait_ge(gp_done, it * 16 + (m - 1))
                nc.gpsimd.tensor_tensor(gate_j[:, n % 2, :, 1, :], is_j[:, n % 2, :, :], four(3, s2, n),
                                        ALU.mult).then_inc(ohl_done, 1)

            def strip_pair(it, first):
                for m in range(16):
                    if m == 2:
                        next_ids(it + A2_BODIES, 0)
                    gates_lower(it, m, first)
                    if m in (2, 4, 6, 8):
                        gather_row(u_rows, m // 2 - 1)
                    if m % 4 in LOWER_AT:
                        c = m // 4 + 1
                        lower_half(it * 2 + (B0 + c // 2), c % 2, LOWER_AT.index(m % 4))

            lower_u(B0, 0)
            strip_pair(0, True)
            with pool.Fori(1, STRIPS // 2) as it:
                strip_pair(it, False)
            next_ids(UC_FIRST, 0)
            lower_u(C0, 1)
            gather(u_rows)
            with pool.Fori(1, UC_STEPS) as it:
                gathering_body(it + C0, it + UC_FIRST)
            with pool.Fori(C0 + UC_STEPS, BODIES) as it:
                for s in range(2):
                    lower_u(it, s)

            for hf in range(2):
                with pool.Fori(0, NG2) as it:
                    for s in range(2):
                        for j in range(VJ):
                            fetch = s == 0 and j == 1
                            if fetch:
                                next_ids(it + hf * NG2, U_STEPS)
                            pool.wait_ge(vh_done, it * (2 * VJ) + (hf * NK + VJ * s + j + 1))
                            nc.gpsimd.tensor_tensor(v_lo[:, j, :], v_raw[s][:, j, :], v_hi[:, j, :],
                                                    ALU.subtract).then_inc(vl_done, 1)
                            if fetch:
                                gather(v_rows)

        @block.scalar
        def _(act):
            def upper(n, dst):
                act.wait_ge(raw_in[n % 2], 16 * (n // 2 + 1))
                nc.scalar.activation(dst, w_raw[:, n % 2, :], ACT.Copy).then_inc(hi_done, 1)

            def upper_slot(n, m):
                if m >= 2:
                    act.wait_ge(pj_done, PIECE_BANKS[m - 2])
                upper(n, w_hi[:, n % 2, :])

            def norm_stats(k, i):
                norm_squares(k, i)
                norm_root(k, i)

            def norm_squares(k, i):
                if k * NT + i:
                    act.wait_ge(ss_done, k * NT + i)
                nc.scalar.activation(squares[:, :], xs[:, i, :], ACT.Square,
                                     accum_out=ss[:, k, i:i + 1]).then_inc(ss_done, 1)

            def norm_root(k, i):
                act.wait_ge(rs_done, 2 * (k * NT + i) + 1)
                nc.scalar.activation(std[:, k, i:i + 1], rstd[:, k, i:i + 1], ACT.Sqrt).then_inc(std_done, 1)

            def norm_upper(k, i):
                for c in range(2):
                    n = k * LO_BANKS + 2 * i + c
                    act.wait_ge(xt_done, n + 1)
                    nc.scalar.activation(h_hi[:, 4 * c:4 * c + 4, i * P:(i + 1) * P],
                                         bank[(4 if k else 0) + (2 * i + c) % 4][:, :]
                                         .rearrange("p (k t) -> p k t", k=4), ACT.Copy).then_inc(hh_done, 1)

            for i in range(NT):
                if i == 0:
                    act.wait_ge(x_in[0], 16)
                    norm_squares(0, 0)
                if i + 1 < NT:
                    act.wait_ge(x_in[i + 1], 16)
                    norm_squares(0, i + 1)
                norm_root(0, i)
                if i:
                    norm_upper(0, i - 1)
            upper_slot(0, 0)
            norm_upper(0, NT - 1)
            upper_slot(1, 1)

            pj = [0]

            def take(dst, src_of, scale=1.0):
                n = pj[0]
                act.wait_ge(pj_done, n + 1)
                nc.scalar.activation(dst, src_of(bank[n % 4]), ACT.Copy, scale=scale).then_inc(pj_free, 1)
                pj[0] = n + 1

            act.wait_ge(pool_pad, 1)
            for c in range(2):
                for hf in range(2):
                    take(pp[:, c, 8 + hf * HALF:8 + (hf + 1) * HALF], lambda b: b[:, :])
                upper_slot(2 + c, 2 + c)

            def exps(g, k):
                n = g * UNITS + k
                c, b = k // NT, k % NT
                _, lo, w, _ = window(g, b)
                for e in range(2):
                    if e == 0:
                        act.wait_ge(s_done, 2 * n + 2)
                        if n >= 2:
                            act.wait_ge(pt_done, n - 1)
                    ins = nc.scalar.activation(pr[:, n % 2, e, lo:lo + w], sc[:, n % 2, e, lo:lo + w], ACT.Exp,
                                               bias=stat_nm[:, g, b, 2 * c + e:2 * c + e + 1], scale=-1.0,
                                               accum_out=stat_den[:, g, b, 2 * c + e:2 * c + e + 1])
                ins.then_inc(p_done, 1)

            def projections(g):
                length, n_res = S // NRES[g], NRES[g]
                if g == 1:
                    act.wait_ge(pool_mm, 4)
                if g == 2:
                    act.wait_ge(pv_done, UNITS)
                for q in range(4):
                    n = 2 + 6 * g + q
                    dst = (qt if q < 2 else kt)[g % 2][:, q % 2, :].rearrange("p (r l) -> p r l", r=n_res)
                    for hf in range(2):
                        take(dst[:, :, hf * length // 2:(hf + 1) * length // 2],
                             lambda b: b[:, :].rearrange("p (l r) -> p r l", r=n_res),
                             -DH ** -0.5 if q < 2 else 1.0)
                        yield
                    upper_slot(n + 2, n + 2)
                for j, (_, rows) in enumerate(v_tiles(g)):
                    dst = vt[0][SPAN * (j % 2):SPAN * (j % 2) + rows, j // 2, :] if g == 2 else vt[g][0:rows, j, :]
                    take(dst, lambda b: b[0:rows, 0:4 * DH])
                    yield
                for n in (8 + 6 * g, 9 + 6 * g):
                    if n < IN_PIECES:
                        upper_slot(n, n)
                yield

            for _ in projections(0):
                pass
            for g in range(1, GROUPS):
                work = projections(g)
                for k in range(UNITS):
                    exps(g - 1, k)
                    if k or g == 1:
                        for _ in range(parts_by(g, k - 1) - (parts_by(g, k - 2) if k > (g != 1) else 0)):
                            next(work, None)
                for _ in work:
                    pass
            act.wait_ge(pj_done, PJ_IN)
            for k in range(UNITS):
                exps(GROUPS - 1, k)
                if k in (2, 3, 5, 6):
                    n = (2, 3, 5, 6).index(k)
                    act.wait_ge(pool_ev, 4)
                    cols = slice(n % 2 * HALF, (n % 2 + 1) * HALF)
                    nc.scalar.activation(h_hi[:, n // 2, cols], pmix[:, n // 2, cols], ACT.Copy).then_inc(mx_hi, 1)
                if k in (4, 8, 12):
                    if k == 4:
                        act.wait_ge(pv_done, (GROUPS - 1) * UNITS)
                    upper(W_OUT0 + k // 4 - 1, wo[k // 4 - 1][:, 0, :])
            act.wait_ge(pv_done, GROUPS * UNITS)
            upper(W_OUT0 + WO_EARLY, wo[WO_EARLY][:, 0, :])
            upper(W_OUT0 + WO_EARLY + 1, wo[WO_EARLY + 1][:, 0, :])
            act.wait_ge(al_st, AL_LESS)
            nc.scalar.activation(lt[:, 0, :, :], lt[:, 0, :, :], ACT.Exp).then_inc(al_e, 1)
            for n in range(WO_EARLY + 2, OUT_PIECES):
                upper(W_OUT0 + n, wo[n][:, 0, :])
            for n in range(4 * GROUPS):
                act.wait_ge(bc_mul, n + 1)
                cols = slice(n % 2 * HALF, (n % 2 + 1) * HALF)
                nc.scalar.activation(h_hi[:, 2 + n // 2, cols], ot[:, n // 2, cols], ACT.Copy).then_inc(mx_hi, 1)
            act.wait_ge(bc_done, 4 * GROUPS)
            upper_slot(W_Q0, IN_PIECES)
            upper_slot(W_Q0 + 1, IN_PIECES + 1)
            for i in range(NT):
                act.wait_ge(x1_done, 2 * i + 2)
                norm_stats(1, i)
                if i:
                    norm_upper(1, i - 1)
            norm_upper(1, NT - 1)

            def take_query(hp):
                if hp >= 2:
                    act.wait_ge(sc_done, 2 * (hp - 1))
                if hp == 0:
                    act.wait_ge(op_done, 2 * NT)
                for hf in range(2):
                    take(q2[:, hp % 2, hf * HALF:(hf + 1) * HALF], lambda b: b[:, :])

            for hp in range(Q_PIECES):
                take_query(hp)
                m = IN_PIECES + hp + 2
                upper_slot(W_Q0 + hp + 2, m)

            def gelus(it, s, first):
                if not first:
                    act.wait_ge(act_out[s], it * 16)
                for hf in range(2):
                    act.wait_ge(m1_done, it * 4 + (2 * s + hf + 1))
                    nc.scalar.activation(act_st[:, s, hf * MH:(hf + 1) * MH], bank[2 * s + hf][:, 0:MH],
                                         ACT.Gelu).then_inc(act_done, 1)

            def upper_ahead(it, s):
                act.wait_ge(raw_in[s], it * 16 + 16 * (W_U0 // 2 + 2))
                nc.scalar.activation(w_hi[:, s, :], w_raw[:, s, :], ACT.Copy).then_inc(hi_done, 1)

            def chunk(it, s, first, ahead):
                gelus(it, s, first)
                if ahead:
                    upper_ahead(it, s)

            for s in range(2):
                chunk(0, s, True, True)
            with act.Fori(1, EXP_BODY) as it:
                for s in range(2):
                    chunk(it, s, False, True)
            act.wait_ge(g_ask, NT)
            nc.scalar.activation(route[:, 2, :, :], route[:, 2, :, :], ACT.Exp).then_inc(g_e, 1)
            with act.Fori(EXP_BODY, B0) as it:
                for s in range(2):
                    chunk(it, s, False, True)

            def gates_upper(it, m, free):
                s2, n = m // 8, m % 8
                act.wait_ge(isj_done, it * 16 + (m + 1))
                if free:
                    act.wait_ge(gp_done, it * 16 + (m - 1))
                for k in range(4):
                    ins = nc.scalar.activation(gate_j[:, n % 2, k, 0, :], is_j[:, n % 2, k, :], ACT.Copy,
                                               scale=strip_r[:, s2, 2, 4 * n + k:4 * n + k + 1])
                ins.then_inc(ohh_done, 1)

            def upper_to_strip(it, m, first):
                s2, n = m // 8, m % 8
                act.wait_ge(gp_done, it * 16 + (m + 1))
                if n == 0 and not first:
                    act.wait_ge(g_out[s2], it * 16)
                for pair in range(2):
                    ins = nc.scalar.activation(g_st[:, s2, :, 4 * n + 2 * pair:4 * n + 2 * pair + 2],
                                               gate_banks(n, pair)[:, 0], ACT.Copy)
                ins.then_inc(gsh_done, 1)

            def strip_pair(it, first=False, last=False):
                for m in range(16):
                    if m:
                        upper_to_strip(it, m - 1, first)
                    elif not first:
                        upper_to_strip(it - 1, 15, False)
                    if m < 15:
                        gates_upper(it, m + 1, not (first and m < 1))
                    elif not last:
                        gates_upper(it + 1, 0, True)
                    if m % 4 == 3:
                        gelus(it * 2 + (B0 + m // 8), m // 4 % 2, False)
                    if m % 4 == 0 and not (first and m == 0):
                        upper_ahead(it * 2 + (B0 + (m - 4) // 8), (m - 4) // 4 % 2)

            gates_upper(0, 0, False)
            strip_pair(0, first=True)
            with act.Fori(1, STRIPS // 2 - 1) as it:
                strip_pair(it)
            strip_pair(STRIPS // 2 - 1, last=True)
            upper_to_strip(STRIPS // 2 - 1, 15, False)
            upper_ahead(C0 - 1, 1)
            with act.Fori(C0, BODIES - 1) as it:
                for s in range(2):
                    chunk(it, s, False, True)
            act.wait_ge(uh_cp, U_STEPS)
            nc.scalar.activation(uh[:, :], uh[:, :], ACT.Gelu).then_inc(uh_act, 1)
            for s in range(2):
                chunk(BODIES - 1, s, False, False)

            def upper_v(hf, it, s, j, first):
                n = hf * NK + VJ * s + j
                if j == 0:
                    act.wait_ge(v_in[s], it * 16 + (hf * 8 * (NK // VJ) + 16))
                if not first:
                    act.wait_ge(m2_done, it * (2 * VJ) + (n - VJ + 1))
                nc.scalar.activation(v_hi[:, j, :], v_raw[s][:, j, :], ACT.Copy).then_inc(vh_done, 1)
                act.wait_ge(pd_done, it * (2 * VJ) + (n + 1))
                n = HT[hf] * P
                nc.scalar.activation(a_hi[:, j, 0:n], prod[:, j % 2, 0:n], ACT.Copy).then_inc(ah_done, 1)

            for hf in range(2):
                for s in range(2):
                    for j in range(VJ):
                        upper_v(hf, 0, s, j, hf == 0 and s == 0)
                with act.Fori(1, NG2) as it:
                    for s in range(2):
                        for j in range(VJ):
                            upper_v(hf, it, s, j, False)
            act.wait_ge(row_used, 2 * P)

            def final_squares(n):
                i = FINAL[n]
                if i < DT:
                    act.wait_ge(y_done, 2 * (i + 1))
                if n >= 4:
                    act.wait_ge(y_out[n % 4], 16 * (n // 4))
                nc.scalar.activation(yo[:, n % 4, :], y[:, i, :] if i < DT else ya[:, :], ACT.Square,
                                     accum_out=ss[:, 2, n:n + 1]).then_inc(ss_done, 1)

            early = HT[0] + 1
            for n in range(NT):
                if n == 0 or n >= early:
                    final_squares(n)
                if n + 1 < early:
                    final_squares(n + 1)
                act.wait_ge(rs_done, 2 * (2 * NT + n) + 1)
                nc.scalar.activation(std[:, 2, n:n + 1], rstd[:, 2, n:n + 1], ACT.Sqrt).then_inc(std_done, 1)

        @block.vector
        def _(dve):
            V = nc.vector

            def norm_scale(k, i, src, dst, done):
                norm_mean(k, i)
                norm_apply(k, i, src, dst, done)

            def norm_mean(k, i):
                dve.wait_ge(ss_done, k * NT + i + 1)
                V.tensor_scalar(rstd[:, k, i:i + 1], ss[:, k, i:i + 1], 1.0 / D, EPS, ALU.mult,
                                ALU.add).then_inc(rs_done, 1)

            def norm_apply(k, i, src, dst, done):
                n = k * NT + i
                dve.wait_ge(std_done, n + 1)
                V.reciprocal(rstd[:, k, i:i + 1], std[:, k, i:i + 1]).then_inc(rs_done, 1)
                dve.wait_ge(rs_done, 2 * n + 2)
                if k < 2 and n >= 2:
                    dve.wait_ge(xt_done, 2 * (n - 1))
                V.scalar_tensor_tensor(out=dst, in0=src, scalar=rstd[:, k, i:i + 1], in1=gain[:, :],
                                       op0=ALU.mult, op1=ALU.mult).then_inc(done, 1)

            def norm_lower(k, i):
                for c in range(2):
                    n = k * LO_BANKS + 2 * i + c
                    dve.wait_ge(hh_done, n + 1)
                    cols = slice(i * P, (i + 1) * P)
                    V.tensor_tensor(h_lo[:, 4 * c:4 * c + 4, cols],
                                    bank[(4 if k else 0) + (2 * i + c) % 4][:, :].rearrange("p (k t) -> p k t", k=4),
                                    h_hi[:, 4 * c:4 * c + 4, cols], ALU.subtract).then_inc(hl_done, 1)

            dve.wait_ge(gain_in, 16)
            norm_mean(0, 0)
            for i in range(NT):
                norm_apply(0, i, xs[:, i, :], xn[:, i % 2, :], xn_done)
                if i + 1 < NT:
                    norm_mean(0, i + 1)
                if i:
                    norm_lower(0, i - 1)
            norm_lower(0, NT - 1)

            V.memset(pp[:, :, :], 0.0).then_inc(pool_pad, 1)
            V.memset(stats[:, :, :, NT * 4:], 1.0).then_inc(stat_pad, 1)
            st = [0]

            def step(ins, sem_=pool_st, count=st):
                ins.then_inc(sem_, 1)
                count[0] += 1
                dve.wait_ge(sem_, count[0])

            dve.wait_ge(cst_in, 16 * 6)
            for c in range(2):
                dve.wait_ge(pj_free, 2 * c + 2)
                n1, n2, n4, n8 = PADW - 1, PADW - 3, PADW - 7, PADW - 15
                step(V.tensor_tensor(pb_[:, 0:n1], pp[:, c, 0:n1], pp[:, c, 1:n1 + 1], ALU.add))
                if c == 0:
                    step(V.tensor_tensor(pa[64:128, 0, 0:n2], pb_[64:128, 0:n2], pb_[64:128, 2:n2 + 2], ALU.add))
                    parts = ((0, 64, pb_[0:64, 7:7 + S]), (64, 128, pa[64:128, 0, 6:6 + S]))
                else:
                    step(V.tensor_tensor(pa[:, 1, 0:n2], pb_[:, 0:n2], pb_[:, 2:n2 + 2], ALU.add))
                    step(V.tensor_tensor(pb_[:, 0:n4], pa[:, 1, 0:n4], pa[:, 1, 4:n4 + 4], ALU.add))
                    step(V.tensor_tensor(pa[64:128, 1, 0:n8], pb_[64:128, 0:n8], pb_[64:128, 8:n8 + 8], ALU.add))
                    parts = ((0, 64, pb_[0:64, 4:4 + S]), (64, 128, pa[64:128, 1, 0:S]))
                for a, b, sums in parts:
                    dst = pmix[a:b, c, :]
                    step(V.tensor_scalar(dst, sums, inv[a:b, c:c + 1], None, ALU.mult))
                    V.tensor_tensor(dst[:, 0:8], sums[:, 0:8], edge[a:b, c, 0:8], ALU.mult)
                    step(V.tensor_tensor(dst[:, S - 8:S], sums[:, S - 8:S], edge[a:b, c, 8:16], ALU.mult))
                    step(V.tensor_tensor(pa[a:b, c, 8:8 + S], dst, pp[a:b, c, 8:8 + S], ALU.subtract))
            for c in range(2):
                for hf in range(2):
                    n = 2 * c + hf
                    dve.wait_ge(pool_mm, n + 1)
                    V.tensor_scalar(pmix[:, c, hf * HALF:(hf + 1) * HALF], bank[6 + n % 2][:, :],
                                    pscale[:, c:c + 1], None, ALU.mult).then_inc(pool_ev, 1)

            def scores(g, k):
                n = g * UNITS + k
                c, b = k // NT, k % NT
                _, lo, w, _ = window(g, b)
                dve.wait_ge(qk_done, n + 1)
                if n >= 2:
                    dve.wait_ge(p_done, n - 1)
                for e in range(2):
                    table = bias2[:, 2 * c + e, :] if g == 2 else bias01[:, 4 * g + 2 * c + e, lo:lo + w]
                    V.tensor_tensor_reduce(sc[:, n % 2, e, lo:lo + w], bank[score_bank(n) + e][:, 0:w],
                                           table, 1.0, FAR, ALU.add, ALU.min,
                                           stat_nm[:, g, b, 2 * c + e:2 * c + e + 1]).then_inc(s_done, 1)

            def probs_out(g, k):
                n = g * UNITS + k
                dve.wait_ge(pt_done, n + 1)
                if n >= 2:
                    dve.wait_ge(pv_done, n - 1)
                tiles = window(g, k % NT)[3]
                for j, (_, rows) in enumerate(tiles):
                    src = bank[6][0:rows, :].rearrange("p (e j q) -> p e j q", e=2, j=2)[:, :, j, :]
                    dst = pt[0:rows, n % 2, :, :].rearrange("p (e j) q -> p e j q", e=2)[:, :, j, :]
                    ins = V.tensor_copy(dst, src)
                ins.then_inc(pt_ev, 1)

            def attn_out(g, k):
                n = g * UNITS + k
                c, b = k // NT, k % NT
                dve.wait_ge(pv_done, n + 1)
                per = S // NRES[g]
                if per >= P:
                    dst = by_residue(ot[:, 2 * g + c, :], g, b * P // per, 1, b * P % per, P)
                else:
                    dst = by_residue(ot[:, 2 * g + c, :], g, b * P // per, P // per, 0, per)
                V.tensor_copy(dst, bank[7][:, 0:P].rearrange("p (r l) -> p r l", l=min(per, P))).then_inc(ot_ev, 1)

            def quarter(kind, g):
                b, c0 = stat_place(kind, g)
                return bank[b][:, c0:c0 + QT].rearrange("p (r s) -> p s r", r=NRES[g])

            def natural(ap, g):
                return ap.rearrange("p (s r) -> p s r", r=NRES[g])

            dve.wait_ge(bias_in, 32)
            for n in range(GROUPS * UNITS + 2):
                if n < GROUPS * UNITS:
                    scores(n // UNITS, n % UNITS)
                if 1 <= n <= GROUPS * UNITS:
                    probs_out((n - 1) // UNITS, (n - 1) % UNITS)
                if n >= 2:
                    attn_out((n - 2) // UNITS, (n - 2) % UNITS)
                m = n - (GROUPS - 1) * UNITS - 6
                if 0 <= m < 8 and m % 2 == 0:
                    m //= 2
                    if m == 0:
                        dve.wait_ge(pj_done, PJ_IN)
                    dve.wait_ge(st_done, m // 2 * 2 + 2)
                    V.tensor_copy(natural(lt[:, m // 2, m % 2, :], m % 2), quarter(m // 2, m % 2)).then_inc(st_ev, 1)
                if 0 <= m - 8 < 4:
                    m -= 8
                    cols = slice(m % 2 * HALF, (m % 2 + 1) * HALF)
                    dve.wait_ge(mx_hi, m + 1)
                    V.tensor_tensor(h_lo[:, m // 2, cols], pmix[:, m // 2, cols], h_hi[:, m // 2, cols],
                                    ALU.subtract).then_inc(mx_lo, 1)

            al = [0]
            dve.wait_ge(st_ev, 4)
            step(V.tensor_tensor(mn[:, 0, :], lt[:, 0, 0, :], lt[:, 0, 1, :], ALU.min), al_st, al)
            dve.wait_ge(st_done, 5)
            last = GROUPS - 1
            step(V.tensor_tensor(natural(mn[:, 0, :], last), natural(mn[:, 0, :], last), quarter(0, last), ALU.min),
                 al_st, al)
            low2 = mn[:, 0, :].unsqueeze(1).broadcast_to([P, 2, QT])
            step(V.tensor_tensor(lt[:, 0, 0:2, :], low2, lt[:, 0, 0:2, :], ALU.subtract), al_st, al)
            step(V.tensor_tensor(natural(lt[:, 0, last, :], last), natural(mn[:, 0, :], last), quarter(0, last),
                                 ALU.subtract), al_st, al)
            assert al[0] == AL_LESS
            dve.wait_ge(st_done, 6)
            dve.wait_ge(al_e, 1)
            step(V.tensor_tensor(lt[:, 1, 0:2, :], lt[:, 1, 0:2, :], lt[:, 0, 0:2, :], ALU.mult), al_st, al)
            step(V.tensor_tensor(natural(lt[:, 1, last, :], last), natural(lt[:, 0, last, :], last),
                                 quarter(1, last), ALU.mult), al_st, al)
            step(V.tensor_tensor(mn[:, 1, :], lt[:, 1, 0, :], lt[:, 1, 1, :], ALU.add), al_st, al)
            step(V.tensor_tensor(mn[:, 1, :], mn[:, 1, :], lt[:, 1, 2, :], ALU.add), al_st, al)
            step(V.reciprocal(mn[:, 0, :], mn[:, 1, :]), al_st, al)
            for g in range(GROUPS):
                step(V.tensor_tensor(lt[:, 0, g, :], lt[:, 0, g, :], mn[:, 0, :], ALU.mult), al_st, al)
            assert al[0] == AL_ALL
            dve.wait_ge(ot_ev, GROUPS * UNITS)
            for n in range(4 * GROUPS):
                cols = slice(n % 2 * HALF, (n % 2 + 1) * HALF)
                dve.wait_ge(bc_done, n + 1)
                V.tensor_tensor(ot[:, n // 2, cols], ot[:, n // 2, cols], bank[n % 4][:, :],
                                ALU.mult).then_inc(bc_mul, 1)
            for n in range(4 * GROUPS):
                cols = slice(n % 2 * HALF, (n % 2 + 1) * HALF)
                dve.wait_ge(mx_hi, 4 + n + 1)
                V.tensor_tensor(h_lo[:, 2 + n // 2, cols], ot[:, n // 2, cols], h_hi[:, 2 + n // 2, cols],
                                ALU.subtract).then_inc(mx_lo, 1)

            dve.wait_ge(gain_in, 32)
            for i in range(NT):
                dve.wait_ge(x_in[i], 32)
                for hf in range(2):
                    n = 2 * i + hf
                    dve.wait_ge(op_done, n + 1)
                    cols = slice(hf * HALF, (hf + 1) * HALF)
                    V.tensor_tensor(xs[:, i, cols], bank[n % 4][:, :], xs[:, i, cols], ALU.add).then_inc(x1_done, 1)
                norm_scale(1, i, xs[:, i, :], xn[:, i % 2, :], xn_done)
                if i:
                    norm_lower(1, i - 1)
            norm_lower(1, NT - 1)

            rs = [0]

            def group(instructions):
                for ins in instructions:
                    ins.then_inc(r_st, 1)
                    rs[0] += 1
                dve.wait_ge(r_st, rs[0])

            for hp in range(Q_PIECES):
                h, half = hp // 2, hp % 2
                for q in range(2):
                    n = 2 * hp + q
                    dve.wait_ge(sc_done, n + 1)
                    src = [bank[4 + n % 4][:, t * NK:(t + 1) * NK] for t in range(4)]
                    val = [top1[:, 4 * q + t, h, half, :] for t in range(4)]
                    idx = [ix1[:, 4 * q + t, h, half, :] for t in range(4)]
                    rest = [rep[:, t, 0:NK] for t in range(4)]
                    group([V.max(val[t][:, 0:8], src[t]) for t in range(4)])
                    group([V.match_replace(rest[t], val[t][:, 0:8], src[t], -FAR) for t in range(4)])
                    group([V.max(val[t][:, 8:16], rest[t]) for t in range(4)])
                    for t in range(4):
                        ins = V.max_index(idx[t][:, 0:8], val[t][:, 0:8], src[t])
                    ins.then_inc(sc_free, 1)
                    for t in range(4):
                        last = V.max_index(idx[t][:, 8:16], val[t][:, 8:16], rest[t])
                    group([last])

            for t in range(NT):
                one, two = top1[:, t, :, 0, :], top1[:, t, :, 1, :]
                shape = [P, PH, TOP, TOP]
                sums = cand[:, :, :].rearrange("p h (a b) -> p h a b", a=TOP)
                group([V.tensor_tensor(sums, one.unsqueeze(3).broadcast_to(shape),
                                       two.unsqueeze(2).broadcast_to(shape), ALU.add),
                       V.tensor_copy(ix1f[:, t, :, :, :], ix1[:, t, :, :, :])])
                group([V.max(top2[:, h, 0:8], cand[:, h, :]) for h in range(PH)])
                group([V.match_replace(rep[:, h, :], top2[:, h, 0:8], cand[:, h, :], -FAR) for h in range(PH)])
                group([V.max(top2[:, h, 8:16], rep[:, h, :]) for h in range(PH)])
                V.tensor_tensor(route[:, 2, t, :].rearrange("p (h k) -> p h k", h=PH), top2[:, :, :],
                                top2[:, :, 0:1].broadcast_to([P, PH, TOP]), ALU.subtract).then_inc(g_ask, 1)
                group([V.max_index(pos[:, 0, h, 0:8], top2[:, h, 0:8], cand[:, h, :]) for h in range(PH)]
                      + [V.max_index(pos[:, 0, h, 8:16], top2[:, h, 8:16], rep[:, h, :]) for h in range(PH)])
                group([V.tensor_scalar(pos[:, 1, :, :], pos[:, 0, :, :], TOP - 1, None, ALU.bitwise_and)])
                group([V.tensor_scalar(pos[:, 0, :, :], pos[:, 0, :, :], 4, None, ALU.logical_shift_right)])
                group([V.tensor_copy(posf[:, :, :, :], pos[:, :, :, :])])
                for half in range(2):
                    ranks = iota[:, 0:TOP].unsqueeze(1).unsqueeze(1).broadcast_to(shape)
                    group([V.tensor_tensor(eq[:, :, :, :], posf[:, half, :, :].unsqueeze(3).broadcast_to(shape),
                                           ranks, ALU.is_equal)])
                    group([V.tensor_tensor(eq[:, :, :, :], eq[:, :, :, :],
                                           ix1f[:, t, :, half, :].unsqueeze(2).broadcast_to(shape), ALU.mult)])
                    group([V.tensor_reduce(route[:, half, t, :].rearrange("p (h k) -> p h k", h=PH),
                                           eq[:, :, :, :], AX.X, ALU.add)])
            group([V.scalar_tensor_tensor(out=uh[:, :], in0=route[:, 1, DT, :], scalar=float(NK),
                                          in1=route[:, 0, DT, :], op0=ALU.mult, op1=ALU.add)])
            V.tensor_copy(ids[:, :], uh[:, :]).then_inc(ids_done, 1)
            dve.wait_ge(g_e, 1)
            gate = route[:, 2, :, :].rearrange("p t (h k) -> p t h k", h=PH)
            group([V.tensor_reduce(gsum[:, 0, :, :], gate, AX.X, ALU.add)])
            group([V.reciprocal(gsum[:, 1, :, :], gsum[:, 0, :, :])])
            V.tensor_tensor(gate, gate, gsum[:, 1, :, :].unsqueeze(3).broadcast_to([P, NT, PH, TOP]),
                            ALU.mult).then_inc(route_done, 1)

            def dots_row(it, r):
                dve.wait_ge(row_in[r], it * 16 + 16)
                V.tensor_tensor_reduce(rows[:, r, :], rows[:, r, :], xn[:, DT % 2, :], 1.0, 0.0, ALU.mult,
                                       ALU.add, uh4[:, r:r + 1]).then_inc(row_used, 1)

            def dots_out(it):
                dve.wait_ge(row_used, it * GR + GR)
                V.tensor_copy(uh[:, bass.ds(it * GR, GR)], uh4[:, :]).then_inc(uh_cp, 1)
                dve.wait_ge(uh_cp, it + 1)

            def dots(it):
                for r in range(GR):
                    dots_row(it, r)
                dots_out(it)

            def add_rows(it):
                V.tensor_copy(gate4[:, :], uh[:, bass.ds(it * GR, GR)]).then_inc(gate4_cp, 1)
                dve.wait_ge(gate4_cp, it + 1)
                for r in range(GR):
                    dve.wait_ge(row_in[r], it * 16 + 16 * (U_STEPS + 1))
                    V.scalar_tensor_tensor(out=ya[:, :], in0=rows[:, r, :], scalar=gate4[:, r:r + 1], in1=ya[:, :],
                                           op0=ALU.mult, op1=ALU.add).then_inc(row_used, 1)
                    dve.wait_ge(row_used, it * GR + (GR * U_STEPS + r + 1))

            with dve.Fori(0, A2_BODIES) as it:
                dots(it)
            for n in range(6):
                w = HT[n % 2] * P
                dve.wait_ge(rt_done, n + 1)
                cols = slice(n % 2 * HALF, n % 2 * HALF + w)
                if n < 4:
                    V.tensor_copy(route_t[:, n // 2, cols], bank[4 + n % 4][:, 0:w]).then_inc(rt_ev, 1)
                else:
                    V.tensor_copy(route_t[:, 2, cols].bitcast(F32R), bank[4 + n % 4][:, 0:w]).then_inc(rt_hi, 1)
                    dve.wait_ge(rt_hi, n - 3)
                    V.tensor_tensor(route_t[:, 3, cols], bank[4 + n % 4][:, 0:w], route_t[:, 2, cols],
                                    ALU.subtract).then_inc(rt_ev, 1)
            dve.wait_ge(rt_ev, 6)

            def one_hots(it, s2, n, first):
                m = 8 * s2 + n
                if not (first and m < 2):
                    dve.wait_ge(ohh_done, it * 16 + (m - 1))
                    dve.wait_ge(ohl_done, it * 16 + (m - 1))
                    dve.wait_ge(gp_done, it * 16 + (m - 1))
                for dst, row, done in ((is_j, 1, isj_done), (is_i, 0, oh_done)):
                    V.tensor_tensor(dst[:, n % 2, :, :], iota[:, :].unsqueeze(1).broadcast_to([P, 4, P]),
                                    four(row, s2, n), ALU.is_equal).then_inc(done, 1)

            def to_strip(it, m):
                s2, n = m // 8, m % 8
                dve.wait_ge(gsh_done, it * 16 + (m + 1))
                for pair in range(2):
                    lower = gate_banks(n, pair)[:, 1]
                    part = g_st[:, s2, :, 4 * n + 2 * pair:4 * n + 2 * pair + 2]
                    ins = V.tensor_tensor(part, lower, part, ALU.add)
                ins.then_inc(gs_done, 1)

            def strip_pair(it, first):
                for s2 in range(2):
                    if not first:
                        for done in (isj_done, oh_done, ohh_done, ohl_done):
                            dve.wait_ge(done, it * 16 + (8 * s2 - 8))
                    V.tensor_copy(strip_r[:, s2, :, :],
                                  route_t[:, :, bass.ds(it * (2 * TW) + s2 * TW, TW)]).then_inc(oh_cp, 1)
                    dve.wait_ge(oh_cp, it * 2 + (s2 + 1))
                    for n in range(8):
                        one_hots(it, s2, n, first)
                        m = 8 * s2 + n - 2
                        if m >= 0:
                            to_strip(it, m)
                        elif not first:
                            to_strip(it - 1, 16 + m)
                        if s2 == 1 and n % 2 == 1:
                            dots_row(it + A2_BODIES, n // 2)
                dots_out(it + A2_BODIES)

            strip_pair(0, True)
            with dve.Fori(1, STRIPS // 2) as it:
                strip_pair(it, False)
            for m in (14, 15):
                to_strip(STRIPS // 2 - 1, m)
            with dve.Fori(0, UC_STEPS) as it:
                dots(it + UC_FIRST)
            dve.wait_ge(gp_done, 8 * STRIPS)
            V.memset(zero[:, :].bitcast(F32), 0.0).then_inc(z_set, 1)
            dve.wait_ge(uh_act, 1)
            V.tensor_tensor(uh[:, :], uh[:, :], route[:, 2, DT, :], ALU.mult).then_inc(uh_gate, 1)
            dve.wait_ge(uh_gate, 1)
            dve.wait_ge(ya_in, 16)
            dve.wait_ge(m1_done, 2 * NK)

            def gated(hf, it, s, j, first):
                n = hf * NK + VJ * s + j
                if j == 0:
                    dve.wait_ge(a_in[s], it * 16 + (hf * 8 * (NK // VJ) + 16))
                    dve.wait_ge(g_in[s], it * 16 + (hf * 8 * (NK // VJ) + 16))
                if not (first and j < 2):
                    dve.wait_ge(ah_done, it * (2 * VJ) + (n - 1))
                w = HT[hf] * P
                V.tensor_tensor(prod[:, j % 2, 0:w].rearrange("p (b t) -> p b t", t=TW),
                                a_raw[s][:, j, 0:w].rearrange("p (b t) -> p b t", t=TW),
                                g_raw[s][:, 0:w // TW, j * TW:(j + 1) * TW], ALU.mult).then_inc(pd_done, 1)

            def lower_a(hf, it, n, j):
                w = HT[hf] * P
                dve.wait_ge(ah_done, it * (2 * VJ) + (n + 1))
                V.tensor_tensor(a_lo[:, j, 0:w], prod[:, j % 2, 0:w], a_hi[:, j, 0:w],
                                ALU.subtract).then_inc(al_done, 1)

            def gated_group(hf, it, first):
                for s in range(2):
                    for j in range(VJ):
                        gated(hf, it, s, j, first and s == 0)
                        lower_a(hf, it, hf * NK + VJ * s + j, j)
                add_rows(it + hf * NG2)

            def add_residual(i):
                dve.wait_ge(tile_done, i + 1)
                for c in range(2):
                    cols = slice(c * HALF, (c + 1) * HALF)
                    V.tensor_tensor(y[:, i, cols], y[:, i, cols], bank[2 * (i % 4) + c][:, :],
                                    ALU.add).then_inc(y_done, 1)

            gated_group(0, 0, True)
            with dve.Fori(1, NG2) as it:
                gated_group(0, it, False)
            dve.wait_ge(y_in, 16)
            for i in range(HT[0]):
                add_residual(i)
            with dve.Fori(0, NG2) as it:
                gated_group(1, it, False)
            dve.wait_ge(gain_in, 48)
            for n, i in enumerate(FINAL):
                if HT[0] <= i < DT - 1:
                    add_residual(i)
                if i == DT - 2:
                    add_residual(i + 1)
                norm_scale(2, n, y[:, i, :] if i < DT else ya[:, :], yo[:, n % 4, :], yo_done)

        @block.tensor
        def _(pe):
            def both_halves(lhs_hi, lhs_lo, banks, done, n=HALF, between=None):
                for k in range(KC):
                    part = slice(k * P, (k + 1) * P)
                    for lhs, rhs in ((lhs_hi, h_hi), (lhs_hi, h_lo), (lhs_lo, h_hi)):
                        for h in range(2):
                            ins = pe.matmul(banks[h][:, 0:n], lhs[:, part], rhs[:, k, h * n:(h + 1) * n],
                                            start=(k == 0 and lhs is lhs_hi and rhs is h_hi),
                                            stop=(k == KC - 1 and lhs is lhs_lo))
                            if k == KC - 1 and lhs is lhs_lo:
                                ins.then_inc(done, 1)
                    if between is not None:
                        between(k)

            def norm_turn(k, i):
                n0 = k * NT + i
                pe.wait_ge(xn_done, n0 + 1)
                for c in range(2):
                    n = k * LO_BANKS + 2 * i + c
                    if 2 * i + c >= 4:
                        pe.wait_ge(hl_done, n - 3)
                    for q in range(4):
                        kc = 4 * c + q
                        ins = pe.transpose(bank[(4 if k else 0) + (2 * i + c) % 4][:, q * P:(q + 1) * P],
                                           xn[:, i % 2, kc * P:(kc + 1) * P], ident[:, :])
                    ins.then_inc(xt_done, 1)

            pe.wait_ge(cst_in, 16 * 6)
            for i in range(NT):
                norm_turn(0, i)
            pe.wait_ge(hl_done, LO_BANKS)

            pj = [0]

            def project(n):
                pe.wait_ge(lo_done, n + 1)
                b = pj[0]
                if b >= 4:
                    pe.wait_ge(pj_free, b - 2)
                both_halves(w_hi[:, n % 2, :], w_lo[:, n % 2, :], [bank[b % 4], bank[(b + 1) % 4]], pj_done)
                pj[0] = b + 2

            def project_half(n, h):
                pe.wait_ge(lo_done, n + 1)
                b = pj[0]
                pe.wait_ge(pj_free, b - 3)
                for k in range(KC):
                    part = slice(k * P, (k + 1) * P)
                    for lhs, rhs in ((w_hi, h_hi), (w_hi, h_lo), (w_lo, h_hi)):
                        ins = pe.matmul(bank[b % 4][:, :], lhs[:, n % 2, part], rhs[:, k, h * HALF:(h + 1) * HALF],
                                        start=(k == 0 and lhs is w_hi and rhs is h_hi),
                                        stop=(k == KC - 1 and lhs is w_lo))
                ins.then_inc(pj_done, 1)
                pj[0] = b + 1

            def project_v(g, j):
                n = 6 + 6 * g
                first, rows = v_tiles(g)[j]
                per = S // NRES[g]
                b = pj[0]
                pe.wait_ge(pj_free, b - 3)
                for k in range(KC):
                    if k % 4 == 0:
                        pe.wait_ge(lo_done, n + 1 + k // 4)
                    rhs = [w[:, k // 4, :].rearrange("p (k n) -> p k n", k=4)[:, k % 4, :] for w in (w_hi, w_lo)]
                    lhs = []
                    for h in (h_hi, h_lo):
                        lhs.append(by_residue(h[:, k, :], g, first // per, 1, first % per, rows)[:, 0, :])
                    dst = bank[b % 4][0:rows, 0:4 * DH]
                    pe.matmul(dst, lhs[0], rhs[0], start=(k == 0), stop=False)
                    pe.matmul(dst, lhs[0], rhs[1], start=False, stop=False)
                    ins = pe.matmul(dst, lhs[1], rhs[0], start=False, stop=(k == KC - 1))
                ins.then_inc(pj_done, 1)
                pj[0] = b + 1

            def projection_parts(g, m0, m1):
                for m in range(m0, m1):
                    if m < 8:
                        project_half(2 + 6 * g + m // 2, m % 2)
                    else:
                        project_v(g, m - 8)

            def qk(g, k):
                n = g * UNITS + k
                c, b = k // NT, k % NT
                k0, _, w, _ = window(g, b)
                if n and score_bank(n) == score_bank(n - 1):
                    pe.wait_ge(s_done, 2 * n)
                elif n:
                    pe.wait_ge(s_done, 2 * n - 2)
                for e in range(2):
                    rows = slice(DH * e, DH * e + DH)
                    ins = pe.matmul(bank[score_bank(n) + e][:, 0:w], qt[g % 2][rows, c, b * P:(b + 1) * P],
                                    kt[g % 2][rows, c, k0:k0 + w], start=True, stop=True)
                ins.then_inc(qk_done, 1)

            def turn(g, k):
                n = g * UNITS + k
                pe.wait_ge(p_done, n + 1)
                if n:
                    pe.wait_ge(pt_ev, n)
                _, lo, _, tiles = window(g, k % NT)
                for e in range(2):
                    for j, (_, rows) in enumerate(tiles):
                        c0 = lo if j == 0 else P
                        ins = pe.transpose(bank[6][0:rows, (2 * e + j) * P:(2 * e + j + 1) * P],
                                           pr[:, n % 2, e, c0:c0 + rows], ident[:, :])
                ins.then_inc(pt_done, 1)

            def pv(g, k):
                n = g * UNITS + k
                c = k // NT
                pe.wait_ge(pt_ev, n + 1)
                if n:
                    pe.wait_ge(ot_ev, n)
                tiles = window(g, k % NT)[3]
                for e in range(2):
                    for j, (tile, rows) in enumerate(tiles):
                        ins = pe.matmul(bank[7][DH * e:DH * e + DH, 0:P],
                                        vt[g % 2][0:rows, tile, (2 * c + e) * DH:(2 * c + e + 1) * DH],
                                        pt[0:rows, n % 2, 2 * e + j, :], start=(j == 0), stop=(j == len(tiles) - 1))
                ins.then_inc(pv_done, 1)

            project(0)
            project(1)
            for k in range(4):
                project(2 + k)
            pool_steps = (8, 18)
            for c in range(2):
                pe.wait_ge(pool_st, pool_steps[c])
                for hf in range(2):
                    if c:
                        pe.wait_ge(pool_ev, hf + 1)
                    for a in (0, DH):
                        ins = pe.matmul(bank[6 + hf][a:a + DH, :], wpool[a:a + DH, c, :],
                                        pa[a:a + DH, c, 8 + hf * HALF:8 + (hf + 1) * HALF], start=True, stop=True)
                    ins.then_inc(pool_mm, 1)
            projection_parts(0, 8, 8 + len(v_tiles(0)))
            pe.wait_ge(pool_ev, 4)

            def turn_stats(kind, g):
                per, steps = S // NRES[g], S // NRES[g] // 4
                runs = min(P, steps)
                nq = max(min(P, per) // runs, 1)
                b_, c0 = stat_place(kind, g)
                pick = ident[:, :].rearrange("p (r q l) -> p q r l", q=nq, l=runs)
                for b in range(NT):
                    t0 = b * P % per
                    for q in range(nq):
                        Q = t0 // steps + q
                        c = c0 + b * P // per * steps + t0 % steps
                        ins = pe.matmul(bank[b_][32 * Q:32 * Q + 32, c:c + P // nq],
                                        stats[:, kind, g, 4 * b:4 * b + 32], pick[:, q],
                                        start=True, stop=True)
                ins.then_inc(st_done, 1)

            pe.wait_ge(pj_free, PJ_G[0])
            qk(0, 0)
            asked = 1
            projection_parts(1, 0, parts_by(1, -1))
            for n in range(GROUPS * UNITS):
                g, k = n // UNITS, n % UNITS
                turn(g, k)
                while asked < min(n + (3 if n + 1 >= (GROUPS - 1) * UNITS else 2), GROUPS * UNITS):
                    if asked % UNITS == 0:
                        pe.wait_ge(pj_free, PJ_G[asked // UNITS])
                    qk(asked // UNITS, asked % UNITS)
                    asked += 1
                if n:
                    pv((n - 1) // UNITS, (n - 1) % UNITS)
                if g + 1 < GROUPS:
                    projection_parts(g + 1, parts_by(g + 1, k - 1) if k or g == 0 else 0, parts_by(g + 1, k))
                m = n - (GROUPS - 1) * UNITS - 2
                if 0 <= m < 8 and m % 2 == 0:
                    if m == 0:
                        pe.wait_ge(stat_pad, 1)
                    turn_stats(m // 4, m // 2 % 2)
            pv(GROUPS - 1, UNITS - 1)
            for kind in range(2):
                if kind == 0:
                    pe.wait_ge(s_done, 2 * GROUPS * UNITS)
                turn_stats(kind, GROUPS - 1)
            pe.wait_ge(sel_in, 16)
            for n in range(4 * GROUPS):
                g, c = n // 4, n // 2 % 2
                pe.wait_ge(al_st, AL_ALL - GROUPS + 1 + g)
                if n >= 4:
                    pe.wait_ge(bc_mul, n - 3)
                for q in range(2):
                    ins = pe.matmul(bank[n % 4][:, q * QT:(q + 1) * QT], sel[:, 2 * (n % 2) + q, c, :],
                                    lt[:, 0, g, :], start=True, stop=True)
                ins.then_inc(bc_done, 1)

            for i in range(NT):
                if i == 0:
                    pe.wait_ge(bc_mul, 4 * GROUPS)
                if i >= 2:
                    pe.wait_ge(x1_done, 2 * i - 2)
                toks = slice(i * P, (i + 1) * P)
                for k in range(KC):
                    if i == 0:
                        pe.wait_ge(mx_lo, 2 * k + 2)
                        pe.wait_ge(lo_done, W_OUT0 + k + 1)
                    for lhs, rhs in ((h_hi, 0), (h_hi, 1), (h_lo, 0)):
                        for h in range(2):
                            ins = pe.matmul(bank[(2 * i + h) % 4][:, :], lhs[:, k, toks],
                                            wo[k][:, rhs, h * HALF:(h + 1) * HALF],
                                            start=(k == 0 and rhs == 0 and lhs is h_hi),
                                            stop=(k == KC - 1 and lhs is h_lo))
                            if k == KC - 1 and lhs is h_lo:
                                ins.then_inc(op_done, 1)
                if i:
                    norm_turn(1, i - 1)
            norm_turn(1, NT - 1)

            def key_scores(hp):
                pe.wait_ge(pj_free, PJ_IN + 2 * hp + 2)
                for q in range(2):
                    n = 2 * hp + q
                    if n >= 4:
                        pe.wait_ge(sc_free, n - 3)
                    for t in range(4):
                        ins = pe.matmul(bank[4 + n % 4][:, t * NK:(t + 1) * NK],
                                        q2[:, hp % 2, (4 * q + t) * P:(4 * q + t + 1) * P], sk[:, hp, :],
                                        start=True, stop=True)
                    ins.then_inc(sc_done, 1)

            pe.wait_ge(hl_done, 2 * LO_BANKS)
            pe.wait_ge(x1_done, 2 * NT)
            for hp in range(Q_PIECES):
                project(W_Q0 + hp)
                if hp == 0:
                    pe.wait_ge(sk_in, 16)
                else:
                    key_scores(hp - 1)
            key_scores(Q_PIECES - 1)

            def chunk(it, s, first, between=None):
                pe.wait_ge(lo_done, it * 2 + (W_U0 + s + 1))
                if first:
                    pe.wait_ge(pj_free, PJ_ALL)
                else:
                    pe.wait_ge(act_done, it * 4 + (2 * s - 2))
                both_halves(w_hi[:, s, :], w_lo[:, s, :], [bank[2 * s], bank[2 * s + 1]], m1_done, MH, between)

            for s in range(2):
                chunk(0, s, True)
            with pe.Fori(1, B0) as it:
                for s in range(2):
                    chunk(it, s, False)
            pe.wait_ge(route_done, 1)
            for n in range(6):
                if n >= 4:
                    pe.wait_ge(rt_ev, n - 3)
                for q in range(HT[n % 2]):
                    ins = pe.transpose(bank[4 + n % 4][:, q * P:(q + 1) * P], route[:, n // 2, 4 * (n % 2) + q, :],
                                       ident[:, :])
                ins.then_inc(rt_done, 1)

            def gates(it, s2, n, first):
                pe.wait_ge(oh_done, it * 16 + (8 * s2 + n + 1))
                pe.wait_ge(ohh_done, it * 16 + (8 * s2 + n + 1))
                pe.wait_ge(ohl_done, it * 16 + (8 * s2 + n + 1))
                if not (first and n < 2):
                    pe.wait_ge(gs_done, it * 16 + (8 * s2 + n - 1))
                for k in range(4):
                    ins = pe.matmul(bank[4 + 2 * (n % 2) + k // 2][:, (k % 2) * 2 * NK:(k % 2 + 1) * 2 * NK],
                                    is_i[:, n % 2, k, :], gate_j[:, n % 2, k, :, :].rearrange("p a j -> p (a j)"),
                                    start=True, stop=True)
                ins.then_inc(gp_done, 1)

            def strip(it, s2, first):
                for s in range(2):
                    def between(k):
                        if k % 2 == 0:
                            gates(it, s2, 4 * s + k // 2, first)
                    chunk(it * 2 + (B0 + s2), s, False, between)

            pe.wait_ge(rt_ev, 6)
            strip(0, 0, True)
            strip(0, 1, False)
            with pe.Fori(1, STRIPS // 2) as it:
                for s2 in range(2):
                    strip(it, s2, False)
            with pe.Fori(C0, BODIES) as it:
                for s in range(2):
                    chunk(it, s, False)

            def products(hf, it, s, j):
                n = hf * NK + VJ * s + j
                pe.wait_ge(vl_done, it * (2 * VJ) + (n + 1))
                pe.wait_ge(al_done, it * (2 * VJ) + (n + 1))
                for q in range(HT[hf]):
                    toks = slice(q * P, (q + 1) * P)
                    for lhs, rhs in ((a_hi, v_hi), (a_hi, v_lo), (a_lo, v_hi)):
                        for c in range(2):
                            ins = pe.matmul(bank[2 * q + c][:, :], lhs[:, j, toks],
                                            rhs[:, j, c * HALF:(c + 1) * HALF], start=False, stop=True,
                                            skip_group_check=True)
                ins.then_inc(m2_done, 1)

            def last_products(hf, s, j):
                n = (hf + 1) * NK - 2
                pe.wait_ge(vl_done, n + 2)
                pe.wait_ge(al_done, n + 2)
                for q in range(HT[hf]):
                    toks = slice(q * P, (q + 1) * P)
                    for jj in (j, j + 1):
                        for lhs, rhs in ((a_hi, v_hi), (a_hi, v_lo), (a_lo, v_hi)):
                            for c in range(2):
                                ins = pe.matmul(bank[2 * q + c][:, :], lhs[:, jj, toks],
                                                rhs[:, jj, c * HALF:(c + 1) * HALF], start=False, stop=True,
                                                skip_group_check=True)
                    ins.then_inc(tile_done, 1)
                pe.wait_ge(tile_done, sum(HT[:hf + 1]))
                pe.nop().then_inc(m2_done, 2)

            pe.wait_ge(z_set, 1)
            pe.wait_ge(act_done, 2 * NK)
            pe.wait_ge(gs_done, 8 * STRIPS)
            for hf in range(2):
                for n in range(2 * HT[hf]):
                    if hf:
                        pe.wait_ge(y_done, n + 1)
                    pe.matmul(bank[n][:, :], zero[:, 0:P], zero[:, :], start=True, stop=True)
                with pe.Fori(0, NG2 - 1) as it:
                    for s in range(2):
                        for j in range(VJ):
                            products(hf, it, s, j)
                for s in range(2):
                    for j in range(VJ if s == 0 else VJ - 2):
                        products(hf, NG2 - 1, s, j)
                last_products(hf, 1, VJ - 2)


def kernel(x, g_mix, w_in, w_pool, pool_scale, w_out, g_ffn, w_peer_q, peer_subkeys, peer_u, peer_v, g_final):
    import numpy as np
    import concourse.bacc as bacc
    from concourse.bass_utils import run_bass_kernel_spmd

    def arr(a):
        return np.ascontiguousarray(a)

    w_in = np.asarray(w_in)[0]
    def cols(c0):
        return w_in[:, c0:c0 + P].reshape(KC, P, P).transpose(1, 0, 2).reshape(P, 1024)

    pool_w, attn_w = 256, 768
    pieces = [cols(0), cols(P)]
    for g in range(GROUPS):
        for part in range(2):
            for c in range(2):
                pieces.append(cols(pool_w + part * attn_w + (2 * g + c) * P))
        wv = w_in[:, pool_w + 2 * attn_w + g * 256:pool_w + 2 * attn_w + (g + 1) * 256]
        for k in range(2):
            pieces.append(wv.reshape(2, 4, P, 256)[k].transpose(1, 0, 2).reshape(P, 1024))
    ins = {
        "x": arr(x),
        "g_mix": arr(g_mix),
        "w_in": np.stack(pieces),
        "w_pool": arr(np.asarray(w_pool)[0].reshape(2, 2 * DH, DH).transpose(1, 0, 2)),
        "pool_scale": arr(np.asarray(pool_scale)[0].reshape(2, P).T),
        "w_out": arr(np.asarray(w_out)[0].reshape(KC, P, D)),
        "g_ffn": arr(g_ffn),
        "w_q": arr(np.asarray(w_peer_q)[0].reshape(KC, P, Q_PIECES, P).transpose(2, 1, 0, 3))
        .reshape(Q_PIECES, P, 1024),
        "subkeys": arr(np.asarray(peer_subkeys)[0].reshape(Q_PIECES, NK, P).transpose(2, 0, 1)),
        "u": arr(np.asarray(peer_u)[0].reshape(NK, NK, KC, P).transpose(1, 3, 2, 0)).reshape(NK, P, 1024),
        "u_rows": arr(np.asarray(peer_u)[0].reshape(NK, NK, D).transpose(1, 0, 2)).reshape(NK * NK, D),
        "v": arr(np.asarray(peer_v)[0].reshape(NK, NK, D).transpose(1, 0, 2)),
        "g_final": arr(np.asarray(g_final).reshape(1, D)),
    }
    slopes = (2.0 ** (-8.0 * np.arange(1, 13) / 12)).astype(np.float32)
    q = np.arange(P)[:, None]
    rel = np.abs(np.arange(2 * P)[None, :] - SPAN - q)
    bias01 = np.stack([np.where(rel <= SPAN, slopes[h] * (DIL[h // 4] * rel).astype(np.float32), np.float32(1e30))
                       for h in range(8)], axis=1).astype(np.float32)
    k = np.arange(P)[None, :]
    bias2 = np.stack([np.where(q // 64 == k // 64, slopes[8 + h] * (DIL[2] * np.abs(q - k)).astype(np.float32),
                               np.float32(1e30)) for h in range(4)], axis=1).astype(np.float32)
    sel = np.zeros((P, 4, 2, P), np.float32)
    for h in range(4):
        for quarter in range(4):
            sel[32 * quarter + h, quarter, h // 2, DH * (h % 2):DH * (h % 2) + DH] = 1.0
    edge = np.zeros((P, 2, 16), np.float32)
    inv = np.zeros((P, 2), np.float32)
    t = np.concatenate([np.arange(8), np.arange(S - 8, S)])
    for g, w in enumerate((2, 4, 8, 16)):
        rows = slice(DH * (g % 2), DH * (g % 2) + DH)
        n = np.clip(t + w // 2, 0, S) - np.clip(t - w // 2, 0, S)
        edge[rows, g // 2, :] = (1.0 / n).astype(np.float32)
        inv[rows, g // 2] = 1.0 / w
    ins |= {"ident_c": np.eye(P, dtype=np.float32),
            "iota_c": np.ascontiguousarray(np.broadcast_to(np.arange(P, dtype=np.float32), (P, P))),
            "bias01_c": arr(bias01), "bias2_c": arr(bias2), "sel_c": sel, "edge_c": edge, "inv_c": inv}

    nc = bacc.Bacc("TRN2", target_bir_lowering=False, num_devices=1)
    aps = {n: nc.dram_tensor(f"in_{n}", a.shape, mybir.dt.from_np(a.dtype), kind="ExternalInput").ap()
           for n, a in ins.items()}
    out = nc.dram_tensor("out", (1, S, D), F32, kind="ExternalOutput").ap()
    build(nc, out=out, **aps)
    r = run_bass_kernel_spmd(nc, [{f"in_{n}": a for n, a in ins.items()}], core_ids=[0])
    return r.results[0]["out"]
```
